# Optimizing a Trainium2 kernel written in Bass

```python
import jax, jax.numpy as jnp
from jax import lax
import numpy as np
import math

D_MODEL = 2048
BATCH = 1
SEQ = 512
DEPTH = 1

PLE_DIM = 256
ATT_HEADS = 16
ATT_HD = 64
ATT_W = ATT_HEADS * ATT_HD
ROT_DIM = ATT_HD // 4
ROPE_THETA = 500000.0
DILATION_CFG = ((128, 1), (512, 4), (2048, 16))
HG_HEADS = 8
HG_DK = 128
HG_DV = 128
HG_W = HG_HEADS * HG_DV
HG_F = HG_HEADS * HG_DK
HG_CHUNK = 64
MIX_W = ATT_W + HG_W
SPLITS = (ATT_W, ATT_W, ATT_W, ATT_W,
          HG_F, HG_F, HG_F, HG_W, HG_W)
IN_W = sum(SPLITS)
SPLIT_IDX = [int(i) for i in np.cumsum(SPLITS)[:-1]]
EPS = 1e-6
NEG = -1e30


def rmsnorm(x, g):
    xf = x.astype(jnp.float32)
    y = xf * lax.rsqrt(jnp.mean(xf * xf, axis=-1, keepdims=True) + EPS)
    return (y * g.astype(jnp.float32)).astype(x.dtype)

def rope_partial(x, pos):
    inv = jnp.power(ROPE_THETA, -jnp.arange(0, ROT_DIM, 2, dtype=jnp.float32) / ROT_DIM)
    ang = pos.astype(jnp.float32)[..., None] * inv
    c = jnp.cos(ang)[:, :, None, :]
    s = jnp.sin(ang)[:, :, None, :]
    x1 = x[..., :ROT_DIM // 2]
    x2 = x[..., ROT_DIM // 2:ROT_DIM]
    return jnp.concatenate([x1 * c - x2 * s, x2 * c + x1 * s, x[..., ROT_DIM:]], axis=-1)

def dilated_band_attention(q, k, v, window, dilation):
    B, S, H, E = q.shape
    half = (window // 2) // dilation
    blk = half
    L = S // dilation
    nb = -(-L // blk)
    Lp = nb * blk

    def strided(t):
        t = t.reshape(B, L, dilation, H, E).transpose(0, 2, 3, 1, 4)
        return jnp.pad(t, ((0, 0), (0, 0), (0, 0), (0, Lp - L), (0, 0)))

    def neighbours(t):
        tp = jnp.pad(t, ((0, 0), (0, 0), (0, 0), (blk, blk), (0, 0)))
        parts = [tp[:, :, :, j * blk:j * blk + Lp].reshape(B, dilation, H, nb, blk, E) for j in range(3)]
        return jnp.concatenate(parts, axis=4)

    qb = strided(q).reshape(B, dilation, H, nb, blk, E)
    kb = neighbours(strided(k))
    vb = neighbours(strided(v))
    qa = jnp.arange(nb)[:, None] * blk + jnp.arange(blk)[None, :]
    ka = jnp.arange(nb)[:, None] * blk - blk + jnp.arange(3 * blk)[None, :]
    rel = ka[:, None, :] - qa[:, :, None]
    valid = (jnp.abs(rel) <= half) & (ka[:, None, :] >= 0) & (ka[:, None, :] < L)
    s = jnp.einsum('bdhnqe,bdhnke->bdhnqk', qb, kb)
    s = jnp.where(valid, s, NEG)
    m = jnp.max(s, axis=-1, keepdims=True)
    pe = jnp.exp(s - m)
    den = jnp.sum(pe, axis=-1)
    o = jnp.einsum('bdhnqk,bdhnke->bdhnqe', pe, vb) / den[..., None]
    lse = m[..., 0] + jnp.log(den)
    o = o.reshape(B, dilation, H, Lp, E)[:, :, :, :L].transpose(0, 3, 1, 2, 4).reshape(B, S, H, E)
    lse = lse.reshape(B, dilation, H, Lp)[:, :, :, :L].transpose(0, 3, 1, 2).reshape(B, S, H)
    return o, lse

def hgrn2_chunk_scan(q, k, v, g):
    B, S, H, K = q.shape
    V = v.shape[-1]
    C = HG_CHUNK
    N = S // C

    def chunks(t):
        return t.reshape(B, N, C, H, t.shape[-1]).transpose(1, 0, 3, 2, 4)

    tri = jnp.tril(jnp.ones((C, C), dtype=bool))

    def step(state, inp):
        qc, kc, vc, gc = inp
        b = jnp.cumsum(gc, axis=2)
        diff = b[:, :, :, None, :] - b[:, :, None, :, :]
        decay = jnp.exp(jnp.where(tri[:, :, None], diff, -jnp.inf))
        att = jnp.einsum('bhtk,bhsk,bhtsk->bhts', qc, kc, decay)
        o = (jnp.einsum('bhts,bhsv->bhtv', att, vc)
             + jnp.einsum('bhtk,bhkv->bhtv', qc * jnp.exp(b), state))
        b_last = b[:, :, -1:, :]
        state = (jnp.exp(b_last[:, :, 0, :])[..., None] * state
                 + jnp.einsum('bhsk,bhsv->bhkv', kc * jnp.exp(b_last - b), vc))
        return state, o

    s0 = jnp.zeros((B, H, K, V), dtype=q.dtype)
    _, o = lax.scan(step, s0, (chunks(q), chunks(k), chunks(v), chunks(g)))
    return o.transpose(1, 0, 3, 2, 4).reshape(B, S, H, V)

def hgrn2_direction(qh, vh, f_logit, lb):
    f = lb + (1.0 - lb) * jax.nn.sigmoid(f_logit)
    return hgrn2_chunk_scan(qh, 1.0 - f, vh, jnp.log(f))

def hybrid_layer(h, p_l, pos, w_in, w_out, g_pre, g_post, g_hg, lb_f, lb_b, w_pg, w_pp, g_ple):
    B, S, _ = h.shape
    f32 = jnp.float32
    u = rmsnorm(h, g_pre)
    z = u @ w_in
    aq, ak, av, ag, hq, hf_f, hf_b, hv, hg = jnp.split(z, SPLIT_IDX, axis=-1)

    def heads(t, n):
        return t.reshape(B, S, n, -1).astype(f32)

    q = rope_partial(heads(aq, ATT_HEADS), pos) * (ATT_HD ** -0.5)
    k = rope_partial(heads(ak, ATT_HEADS), pos)
    v = heads(av, ATT_HEADS)
    res = [dilated_band_attention(q, k, v, w, d) for (w, d) in DILATION_CFG]
    outs = jnp.stack([r[0] for r in res])
    lses = jnp.stack([r[1] for r in res])
    alpha = jax.nn.softmax(lses, axis=0)
    o_att = jnp.einsum('gbsh,gbshe->bshe', alpha, outs).reshape(B, S, ATT_W)
    y_att = o_att * jax.nn.silu(ag.astype(f32))

    qh = jax.nn.silu(heads(hq, HG_HEADS))
    vh = heads(hv, HG_HEADS)
    o_fw = hgrn2_direction(qh, vh, heads(hf_f, HG_HEADS), lb_f)
    o_bw = jnp.flip(hgrn2_direction(jnp.flip(qh, 1), jnp.flip(vh, 1),
                                    jnp.flip(heads(hf_b, HG_HEADS), 1), lb_b), 1)
    o_hg = rmsnorm(o_fw + o_bw, g_hg).reshape(B, S, HG_W)
    y_hg = o_hg * jax.nn.silu(hg.astype(f32))

    y = jnp.concatenate([y_att, y_hg], axis=-1).astype(h.dtype) @ w_out
    h = h + rmsnorm(y, g_post)

    gate = jax.nn.sigmoid((h @ w_pg).astype(f32))
    e = (p_l @ w_pp).astype(f32)
    h = h + rmsnorm((gate * e).astype(h.dtype), g_ple)
    return h

def first_inputs(seed: int = 0) -> dict:
    key = jax.random.key(seed)
    ks = jax.random.split(key, 16)
    nrm = jax.random.normal
    x = nrm(ks[0], (BATCH, SEQ, D_MODEL), jnp.float32)
    p = nrm(ks[1], (DEPTH, BATCH, SEQ, PLE_DIM), jnp.float32)
    positions = (jnp.arange(SEQ, dtype=jnp.int32)[None, :]
                 + jax.random.randint(ks[2], (BATCH, 1), 0, 1024, dtype=jnp.int32))
    w_in = nrm(ks[3], (DEPTH, D_MODEL, IN_W), jnp.float32) * D_MODEL ** -0.5
    w_out = nrm(ks[4], (DEPTH, MIX_W, D_MODEL), jnp.float32) * MIX_W ** -0.5
    g_pre = 1.0 + 0.05 * nrm(ks[5], (DEPTH, D_MODEL), jnp.float32)
    g_post = 1.0 + 0.05 * nrm(ks[6], (DEPTH, D_MODEL), jnp.float32)
    g_hg = 1.0 + 0.05 * nrm(ks[7], (DEPTH, HG_DV), jnp.float32)
    lb_fwd = 0.1 * nrm(ks[8], (DEPTH + 1, HG_F), jnp.float32)
    lb_bwd = 0.1 * nrm(ks[9], (DEPTH + 1, HG_F), jnp.float32)
    w_pg = nrm(ks[10], (DEPTH, D_MODEL, D_MODEL), jnp.float32) * D_MODEL ** -0.5
    w_pp = nrm(ks[11], (DEPTH, PLE_DIM, D_MODEL), jnp.float32) * PLE_DIM ** -0.5
    g_ple = 1.0 + 0.05 * nrm(ks[12], (DEPTH, D_MODEL), jnp.float32)
    return {'x': x, 'p': p, 'positions': positions, 'w_in': w_in, 'w_out': w_out,
            'g_pre': g_pre, 'g_post': g_post, 'g_hg': g_hg, 'lb_fwd': lb_fwd, 'lb_bwd': lb_bwd,
            'w_pg': w_pg, 'w_pp': w_pp, 'g_ple': g_ple}

def first_block(x, p, positions, w_in, w_out, g_pre, g_post, g_hg, lb_fwd, lb_bwd, w_pg, w_pp, g_ple):
    lb_f_all = jnp.cumsum(jax.nn.softmax(lb_fwd.astype(jnp.float32), axis=0), axis=0)
    lb_b_all = jnp.cumsum(jax.nn.softmax(lb_bwd.astype(jnp.float32), axis=0), axis=0)
    h = x
    for i in range(DEPTH):
        h = hybrid_layer(h, p[i], positions, w_in[i], w_out[i], g_pre[i], g_post[i], g_hg[i],
                         lb_f_all[i].reshape(HG_HEADS, HG_DK), lb_b_all[i].reshape(HG_HEADS, HG_DK),
                         w_pg[i], w_pp[i], g_ple[i])
    return h


DEPTH_2 = 2

HEAD_DIM = 128
RET_HEADS = 6
RET_W = RET_HEADS * HEAD_DIM
RET_CHUNK = 128
DIFF_HEADS = 4
DIFF_QK = HEAD_DIM // 2
DIFF_W = DIFF_HEADS * HEAD_DIM
Q_BLOCK = 128
LRU_W = 768
LRU_BLOCKS = 8
LRU_BW = LRU_W // LRU_BLOCKS
CONV_W = 4
LRU_C = 8.0
D_MIX = RET_W + DIFF_W + LRU_W
SPLIT_SIZES = (RET_W, RET_W, RET_W, RET_W,
               DIFF_W, DIFF_W, DIFF_W, DIFF_W,
               LRU_W, LRU_W)
D_IN = sum(SPLIT_SIZES)
ROPE_THETA_2 = 10000.0


def rms_norm(x, g=None):
    x32 = x.astype(jnp.float32)
    y = x32 * lax.rsqrt(jnp.mean(x32 * x32, axis=-1, keepdims=True) + EPS)
    if g is not None:
        y = y * g.astype(jnp.float32)
    return y.astype(x.dtype)

def rope(x, positions, inv_freq):
    ang = positions.astype(jnp.float32)[..., None] * inv_freq
    cos = jnp.cos(ang)[:, :, None, :].astype(x.dtype)
    sin = jnp.sin(ang)[:, :, None, :].astype(x.dtype)
    x1, x2 = jnp.split(x, 2, axis=-1)
    return jnp.concatenate([x1 * cos - x2 * sin, x2 * cos + x1 * sin], axis=-1)

def retention(q, k, v, positions):
    B, S, H, D = q.shape
    dt = q.dtype
    inv = 1.0 / (ROPE_THETA_2 ** jnp.linspace(0.0, 1.0, D // 2, dtype=jnp.float32))
    q = rope(q, positions, inv)
    k = rope(k, positions, inv) * (D ** -0.5)
    log_g = jnp.log1p(-jnp.power(2.0, -5.0 - jnp.arange(H, dtype=jnp.float32)))
    C = RET_CHUNK
    N = S // C
    idx = jnp.arange(C, dtype=jnp.float32)
    rel = idx[:, None] - idx[None, :]
    intra_decay = jnp.where(rel[None] >= 0,
                            jnp.exp(jnp.maximum(rel, 0.0)[None] * log_g[:, None, None]),
                            0.0).astype(dt)
    qc = q.reshape(B, N, C, H, D)
    kc = k.reshape(B, N, C, H, D)
    vc = v.reshape(B, N, C, H, D)
    scores = jnp.einsum('bnihd,bnjhd->bnhij', qc, kc) * intra_decay
    o_intra = jnp.einsum('bnhij,bnjhe->bnihe', scores, vc)
    k_w = jnp.exp((C - 1.0 - idx)[:, None] * log_g[None, :]).astype(dt)
    kv = jnp.einsum('bnjhd,bnjhe->nbhde', kc * k_w[:, :, None], vc)
    chunk_decay = jnp.exp(C * log_g)[None, :, None, None].astype(kv.dtype)

    def step(state, kv_n):
        return state * chunk_decay + kv_n, state

    _, s_prev = lax.scan(step, jnp.zeros_like(kv[0]), kv)
    q_w = jnp.exp((idx + 1.0)[:, None] * log_g[None, :]).astype(dt)
    o_cross = jnp.einsum('bnihd,nbhde->bnihe', qc * q_w[:, :, None], s_prev)
    return (o_intra + o_cross).reshape(B, S, H, D)

def diff_attention(q, k, v, positions, lam):
    B, S, H, _, DQ = q.shape
    inv = 1.0 / (ROPE_THETA_2 ** (jnp.arange(0, DQ, 2, dtype=jnp.float32) / DQ))
    q = rope(q.reshape(B, S, H * 2, DQ), positions, inv).reshape(B, S, H, 2, DQ) * (DQ ** -0.5)
    k = rope(k.reshape(B, S, H * 2, DQ), positions, inv).reshape(B, S, H, 2, DQ)
    kpos = jnp.arange(S)

    def block(i):
        qb = lax.dynamic_slice_in_dim(q, i * Q_BLOCK, Q_BLOCK, axis=1)
        s = jnp.einsum('bqhcd,bkhcd->bhcqk', qb, k).astype(jnp.float32)
        qpos = i * Q_BLOCK + jnp.arange(Q_BLOCK)
        s = jnp.where(kpos[None, :] <= qpos[:, None], s, -jnp.inf)
        p = jax.nn.softmax(s, axis=-1)
        w = p[:, :, 0] - lam * p[:, :, 1]
        return jnp.einsum('bhqk,bkhe->bqhe', w.astype(v.dtype), v)

    o = lax.map(block, jnp.arange(S // Q_BLOCK))
    return jnp.transpose(o, (1, 0, 2, 3, 4)).reshape(B, S, H, v.shape[-1])

def rg_lru(x, conv_w, conv_b, wa, ba, wx, bx, lam):
    B, S, W = x.shape
    xp = jnp.pad(x, ((0, 0), (CONV_W - 1, 0), (0, 0)))
    xc = conv_b + xp[:, 0:S] * conv_w[0]
    for j in range(1, CONV_W):
        xc = xc + xp[:, j:j + S] * conv_w[j]
    xb = xc.reshape(B, S, LRU_BLOCKS, LRU_BW)
    r = jax.nn.sigmoid(jnp.einsum('bsnk,nkj->bsnj', xb, wa).reshape(B, S, W) + ba)
    i = jax.nn.sigmoid(jnp.einsum('bsnk,nkj->bsnj', xb, wx).reshape(B, S, W) + bx)
    log_a = (LRU_C * r.astype(jnp.float32)) * jax.nn.log_sigmoid(lam.astype(jnp.float32))
    a = jnp.exp(log_a)
    mult = jnp.sqrt(-jnp.expm1(2.0 * log_a))
    b = mult * (i * xc).astype(jnp.float32)

    def combine(left, right):
        a1, b1 = left
        a2, b2 = right
        return a1 * a2, a2 * b1 + b2

    _, h = lax.associative_scan(combine, (a, b), axis=1)
    return h.astype(x.dtype)

def second_inputs(seed: int = 0) -> dict:
    key = jax.random.key(seed)
    ks = jax.random.split(key, 20)
    f32 = jnp.float32
    x = jax.random.normal(ks[0], (BATCH, SEQ, D_MODEL), f32)
    positions = jnp.broadcast_to(jnp.arange(SEQ, dtype=jnp.int32), (BATCH, SEQ))
    pre_norm_g = 1.0 + 0.05 * jax.random.normal(ks[1], (DEPTH_2, D_MODEL), f32)
    w_in = jax.random.normal(ks[2], (DEPTH_2, D_MODEL, D_IN), f32) * (D_MODEL ** -0.5)
    diff_lambda_q1 = 0.1 * jax.random.normal(ks[3], (DEPTH_2, DIFF_QK), f32)
    diff_lambda_k1 = 0.1 * jax.random.normal(ks[4], (DEPTH_2, DIFF_QK), f32)
    diff_lambda_q2 = 0.1 * jax.random.normal(ks[5], (DEPTH_2, DIFF_QK), f32)
    diff_lambda_k2 = 0.1 * jax.random.normal(ks[6], (DEPTH_2, DIFF_QK), f32)
    diff_subln_g = 1.0 + 0.05 * jax.random.normal(ks[7], (DEPTH_2, HEAD_DIM), f32)
    lru_conv_w = jax.random.normal(ks[8], (DEPTH_2, CONV_W, LRU_W), f32) * (CONV_W ** -0.5)
    lru_conv_b = 0.01 * jax.random.normal(ks[9], (DEPTH_2, LRU_W), f32)
    lru_wa = jax.random.normal(ks[10], (DEPTH_2, LRU_BLOCKS, LRU_BW, LRU_BW), f32) * (LRU_BW ** -0.5)
    lru_ba = 0.01 * jax.random.normal(ks[11], (DEPTH_2, LRU_W), f32)
    lru_wx = jax.random.normal(ks[12], (DEPTH_2, LRU_BLOCKS, LRU_BW, LRU_BW), f32) * (LRU_BW ** -0.5)
    lru_bx = 0.01 * jax.random.normal(ks[13], (DEPTH_2, LRU_W), f32)
    u = jax.random.uniform(ks[14], (DEPTH_2, LRU_W), f32, minval=0.9, maxval=0.999)
    s = u ** (1.0 / LRU_C)
    lru_lambda = jnp.log(s) - jnp.log1p(-s)
    w_out = jax.random.normal(ks[15], (DEPTH_2, D_MIX, D_MODEL), f32) * (D_MIX ** -0.5)
    post_norm_g = 1.0 + 0.05 * jax.random.normal(ks[16], (DEPTH_2, D_MODEL), f32)
    return {"x": x, "positions": positions, "pre_norm_g": pre_norm_g, "w_in": w_in,
            "diff_lambda_q1": diff_lambda_q1, "diff_lambda_k1": diff_lambda_k1,
            "diff_lambda_q2": diff_lambda_q2, "diff_lambda_k2": diff_lambda_k2,
            "diff_subln_g": diff_subln_g, "lru_conv_w": lru_conv_w, "lru_conv_b": lru_conv_b,
            "lru_wa": lru_wa, "lru_ba": lru_ba, "lru_wx": lru_wx, "lru_bx": lru_bx,
            "lru_lambda": lru_lambda, "w_out": w_out, "post_norm_g": post_norm_g}

def second_block(x, positions, pre_norm_g, w_in, diff_lambda_q1, diff_lambda_k1,
              diff_lambda_q2, diff_lambda_k2, diff_subln_g, lru_conv_w, lru_conv_b,
              lru_wa, lru_ba, lru_wx, lru_bx, lru_lambda, w_out, post_norm_g):
    B, S, _ = x.shape
    split_idx = [int(v) for v in np.cumsum(SPLIT_SIZES)[:-1]]
    for l in range(DEPTH_2):
        h = rms_norm(x, pre_norm_g[l])
        proj = jnp.einsum('bsd,de->bse', h, w_in[l])
        (rq, rk, rv, rg, dq, dk, dv, dg, lx, lg) = jnp.split(proj, split_idx, axis=-1)

        ro = retention(rq.reshape(B, S, RET_HEADS, HEAD_DIM),
                       rk.reshape(B, S, RET_HEADS, HEAD_DIM),
                       rv.reshape(B, S, RET_HEADS, HEAD_DIM), positions)
        ret_out = rms_norm(ro).reshape(B, S, RET_W) * jax.nn.silu(rg)

        lam_init = 0.8 - 0.6 * math.exp(-0.3 * l)
        lam = (jnp.exp(jnp.sum(diff_lambda_q1[l] * diff_lambda_k1[l]).astype(jnp.float32))
               - jnp.exp(jnp.sum(diff_lambda_q2[l] * diff_lambda_k2[l]).astype(jnp.float32))
               + lam_init)
        do = diff_attention(dq.reshape(B, S, DIFF_HEADS, 2, DIFF_QK),
                            dk.reshape(B, S, DIFF_HEADS, 2, DIFF_QK),
                            dv.reshape(B, S, DIFF_HEADS, HEAD_DIM), positions, lam)
        diff_out = (rms_norm(do, diff_subln_g[l]) * (1.0 - lam_init)).reshape(B, S, DIFF_W) * jax.nn.silu(dg)

        lru_out = rg_lru(lx, lru_conv_w[l], lru_conv_b[l], lru_wa[l], lru_ba[l],
                         lru_wx[l], lru_bx[l], lru_lambda[l]) * jax.nn.silu(lg)

        mixed = jnp.concatenate([ret_out, diff_out, lru_out], axis=-1)
        y = jnp.einsum('bse,ed->bsd', mixed, w_out[l])
        x = x + rms_norm(y, post_norm_g[l])
    return x


def setup_inputs(seed=0):
    out = dict(first_inputs(seed))
    for name, value in second_inputs(seed + 1).items():
        if name != "x":
            out[name + "_2"] = value
    return out


def reference(
    x, p, positions, w_in, w_out, g_pre, g_post, g_hg, lb_fwd, lb_bwd, w_pg, w_pp, g_ple,
    positions_2, pre_norm_g_2, w_in_2, diff_lambda_q1_2, diff_lambda_k1_2, diff_lambda_q2_2,
    diff_lambda_k2_2, diff_subln_g_2, lru_conv_w_2, lru_conv_b_2, lru_wa_2, lru_ba_2, lru_wx_2,
    lru_bx_2, lru_lambda_2, w_out_2, post_norm_g_2,
):
    x = first_block(
        x, p, positions, w_in, w_out, g_pre, g_post, g_hg, lb_fwd, lb_bwd, w_pg, w_pp, g_ple,
    )
    return second_block(
        x, positions_2, pre_norm_g_2, w_in_2, diff_lambda_q1_2, diff_lambda_k1_2,
        diff_lambda_q2_2, diff_lambda_k2_2, diff_subln_g_2, lru_conv_w_2, lru_conv_b_2,
        lru_wa_2, lru_ba_2, lru_wx_2, lru_bx_2, lru_lambda_2, w_out_2, post_norm_g_2,
    )


_drawn_inputs = setup_inputs


def setup_inputs(seed=0):
    import zlib

    import numpy as np

    out = dict(_drawn_inputs(seed))
    spreads = {}
    factors = {'lb_fwd': 8.0,
     'lb_bwd': 8.0,
     'diff_lambda_k1_2': 2.853,
     'diff_subln_g_2': 3.597,
     'lru_ba_2': 64.0,
     'lru_bx_2': 63.673,
     'lru_conv_b_2': 3.939}
    for name, (base, spread) in spreads.items():
        noise = np.random.default_rng([zlib.crc32(name.encode()), seed]).standard_normal(out[name].shape)
        drawn = base * np.exp(spread * noise) if base else spread * noise
        out[name] = __import__('jax').numpy.asarray(drawn.astype(out[name].dtype))
    for name, factor in factors.items():
        out[name] = (out[name] * factor).astype(out[name].dtype)
    return out
```

```python
from contextlib import ExitStack

import numpy as np
import concourse.bass as bass
from concourse import mybir

F32 = mybir.dt.float32
F32R = mybir.dt.float32r
U8 = mybir.dt.uint8
I32 = mybir.dt.int32
ACT = mybir.ActivationFunctionType
ALU = mybir.AluOpType
AX = mybir.AxisListType

P = 128
S = 512
D = 2048
KT = D // P
EPS = 1e-6
NEG = -1e30
ROWS = 36
PRIMED = 1
REUSE_SIGNALS = ("hav_done", "hg_done", "lv_free", "hro_ready", "att_done", "pte0", "pte1", "sm_done", "pt_done", "av_done",
                 "ra_ready", "ret_done", "dpte", "dsm_done", "dif_done", "dpt_done", "dav_done", "rav_done", "scan_done",
                 "gate_read", "par_used", "rot_used", "sq_used")

ATT_W, ATT_HD = 1024, 64
HG_HEADS = 8
PAIRS = 8
LAYERS = 2
RET_HEADS, DIF_HEADS, LRU_TILES = 6, 4, 6
LRU_BW = 96

T_PP, T_HGG, T_HG, T_ATT, T_OUT, T_PG, T_L2 = 0, 2, 10, 42, 74, 90, 106
R_RET, R_DIF, R_LX, R_LG, R_OUT, PER_LAYER = 0, 24, 40, 46, 52, 68
NT = T_L2 + LAYERS * PER_LAYER

G_PRE, G_POST, G_PLE, G_HG, LBF, LBB = 0, 16, 32, 48, 49, 65
PAR1 = 81
G2_PRE, G2_POST, G2_SUB, CONV_W, CONV_B, BA, BX, LAM = 0, 16, 32, 33, 57, 63, 69, 75
PAR2 = 81
C_INV, C_EPS, C_LAM = 0, 3, 4
CST = 8

LRU_PAIRS = [(a, b) for b in range(LRU_TILES) for a in range(LRU_TILES)
             if any(max(LRU_BW * n, P * a) < min(LRU_BW * (n + 1), P * (a + 1)) and
                    max(LRU_BW * n, P * b) < min(LRU_BW * (n + 1), P * (b + 1)) for n in range(8))]
NG = len(LRU_PAIRS)


LEVEL_AT = {1: 0, 2: 1, 3: 2, 4: 3, 6: 4, 7: 5, 8: 6, 10: 7, 11: 8, 12: 9}


class Tile:

    def __init__(self, c, *terms):
        self.c, self.terms = c, terms

    def plus(self, n):
        return Tile(self.c + n, *self.terms)

    def times(self, k, add=0):
        v = self.c * k + add
        for m, i in self.terms:
            v = i * (m * k) + v
        return v

    def pair(self):
        v = self.c // 2
        for m, i in self.terms:
            v = i * (m // 2) + v
        return v

    @property
    def odd(self):
        return self.c % 2


def build(nc, wt, xT, pT, pos1, pos2, par1, par2, dlam, gw, cst, rots, idn, masks, bias, dec, cmask, out):
    ctx = ExitStack()
    with ctx:
        sems = {}

        def sb(name, shape, dt=F32):
            return ctx.enter_context(nc.sbuf_tensor(name, shape, dt))

        def sem(name):
            if name not in sems:
                sems[name] = ctx.enter_context(nc.semaphore(name))
            return sems[name]

        tabs = nc.dram_tensor("rope_tables", [6, P, S], F32, kind="Internal").ap()
        e_dram = nc.dram_tensor("e_scratch", [KT, P, S], F32, kind="Internal").ap()

        RAW = sb("w_raw", [P, 2, KT * P])
        WH = sb("w_high", [P, KT, P], F32R)
        WL = sb("w_low", [P, KT, P], F32R)
        UH = sb("u_high", [P, KT, S], F32R)
        UL = sb("u_low", [P, KT, S], F32R)
        MIX = sb("mixed", [P, KT, S])
        W = sb("work", [P, ROWS, S])
        MSK = sb("level_masks", [P, 8, P], U8)
        ONES = sb("ones", [P, P])
        IDN = sb("identity", [P, P])
        ROT = sb("rotations", [P, 3, P])
        PR1 = sb("params_1", [P, PAR1])
        PR2 = sb("params_2", [P, PAR2])
        LB = sb("lower_bounds", [P, 4, 8])
        DL = sb("lambda_vectors", [P, 4, 64])
        CS = sb("constants", [P, CST])
        SM = sb("small", [P, 64])
        PRIME = sb("prime", [1, len(REUSE_SIGNALS)])

        Z = [ctx.enter_context(nc.psum_tensor(f"z{i}", [P, S], F32)) for i in range(2)]
        SC = [ctx.enter_context(nc.psum_tensor(f"scores{i}", [P, S], F32)) for i in range(2)]
        TP = [ctx.enter_context(nc.psum_tensor(f"turned{i}", [P, S], F32)) for i in range(2)]
        OB = ctx.enter_context(nc.psum_tensor("o_bank", [P, S], F32))
        MB = ctx.enter_context(nc.psum_tensor("rot_bank", [P, S], F32))

        def row(r, n=1):
            return W[:, r, :] if n == 1 else W[:, r:r + n, :]

        def view(r, off, dims):
            a = W[:]
            return bass.AP(a.tensor, r * S + off, [a.ap[0]] + dims)

        H = 0
        E = 16
        SQ0, SQ1, ACC, RSTD = 32, 33, 34, 35
        FB, FF, Q, VT, QB, KF, QF, KB, TT, HVN, AT = 0, 1, 2, 3, 4, 5, 6, 7, 8, 10, 11
        HSQ, HRO, HTMP, KM, KS, SG, SE = 15, 16, 17, 18, 19, 20, 21
        QT, KTR, VTA, QN, KN, RW, TM = 22, 23, 24, 25, 26, 27, 28
        CT1, ST1, BIAS = 29, 30, 31
        SMR, PRB, VN, PT = 0, 2, 4, 5
        CTR, STR, CTD, STD, CM, DEC = 29, 30, 31, 32, 33, 34
        RA, NTMP, NSQ, NRO = 0, 6, 7, 8
        XC, GW = 9, 15
        HS = 0
        LT = [22, 23, 24, 27, 28, 6, 7, 8]

        block = ctx.enter_context(nc.Block())

        @block.sync
        def _(sp):
            def load(t):
                sp.dma_start(RAW[:, t.odd, :], wt[t_index(t)]).then_inc(sem("w_raw1" if t.odd else "w_raw0"), 16)

            def t_index(t):
                return t.times(1)

            load(Tile(0))
            load(Tile(1))
            with sp.Fori(1, NT // 2) as g:
                for o in range(2):
                    t = Tile(o, (2, g))
                    sp.wait_ge(sem("l_ready"), t.times(4, -4))
                    load(t)
            sp.wait_ge(sem("l_ready"), 4 * NT - 4)
            load(Tile(NT))
            sp.wait_ge(sem("w_raw0"), 16 * (NT // 2 + 1))

        @block.gpsimd
        def _(pool):
            for n, name in enumerate(REUSE_SIGNALS):
                pool.memset(PRIME[:, n:n + 1], 0.0).then_inc(sem(name), PRIMED)
            with pool.Fori(0, NT // 2) as g:
                for o in range(2):
                    t = Tile(o, (2, g))
                    for q in range(4):
                        pool.wait_ge(sem("h_ready"), t.times(4, q + 1))
                        pool.tensor_tensor(
                            WL[:, 4 * q:4 * q + 4, :], RAW[:, o, 512 * q:512 * q + 512].rearrange("p (k c) -> p k c", k=4),
                            WH[:, 4 * q:4 * q + 4, :].bitcast(F32), ALU.subtract).then_inc(sem("l_ready"), 1)

        @block.tensor
        def _(pe):
            def quarter(t, q, gen=None):
                bank = Z[t.odd]
                if q == 0:
                    if t.c in (T_HGG, T_HGG + 1) and not t.terms:
                        pe.wait_ge(sem("e_out"), 16)
                    else:
                        pe.wait_ge(sem("z_free"), t.times(1, -T_HGG - 1))
                pe.wait_ge(sem("l_ready"), t.times(4, q + 1))
                for k in range(4 * q, 4 * q + 4):
                    if gen is not None:
                        pe.wait_ge(sem("u_ready"), gen * 16 + k + 1)
                    for n, (w, u) in enumerate(((WH, UH), (WH, UL), (WL, UH))):
                        mm = pe.matmul(bank[:], w[:, k, :], u[:, k, :], start=(k == 0 and n == 0),
                                       stop=(k == KT - 1 and n == 2))
                mm.then_inc(sem("w_free"), 1)

            def sum_rows(src, bank, wait, done):
                pe.wait_ge(*wait)
                pe.matmul(bank[:], ONES[:], src, start=True, stop=True).then_inc(sem(done), 1)

            def turn_v(src, wait, done):
                pe.wait_ge(*wait)
                for c in range(4):
                    mm = pe.transpose(TP[0][:, c * P:(c + 1) * P], src[:, c * P:(c + 1) * P], IDN[:])
                mm.then_inc(sem(done), 1)

            def rotate(t, n, which):
                pe.wait_ge(sem("z_free"), t.times(1, -T_HGG + 1))
                pe.wait_ge(sem("rot_used"), PRIMED + n)
                pe.matmul(MB[:], ROT[:, which, :], row(RW), start=True, stop=True).then_inc(sem("rot_done"), 1)

            def hg_work(j, p):
                def level(n):
                    pe.wait_ge(sem("qk_ready"), j * 9 + max(n, 1))
                    if 1 <= n <= 7:
                        pe.wait_ge(sem("km_ready"), j * 7 + n)
                    if n < 2:
                        pe.wait_ge(sem("lv_free"), PRIMED + j * 10)
                    elif n < 9:
                        pe.wait_ge(sem("lv_free"), PRIMED + j * 10 + n - 1)
                    if n <= 8:
                        bank = SC[n % 2]
                        for c in range(4):
                            if n == 0:
                                kk, qq = row(KS)[:, c * P:(c + 1) * P], row(Q)[:, c * P:(c + 1) * P]
                            elif n < 8:
                                h = 1 << (n - 1)
                                kk = row(KM)[:, c * P:(c + 1) * P]
                                qq = view(QB, c * P, [[2 * h, P // (2 * h)], [2 * S + h, 2], [1, h]])
                            else:
                                kk = row(KB if c % 2 else KF)[:, c * P:(c + 1) * P]
                                o = c ^ 1
                                qq = row(QF if o % 2 else QB)[:, o * P:(o + 1) * P]
                            mm = pe.matmul(bank[:, c * P:(c + 1) * P], kk, qq, start=True, stop=True)
                    else:
                        pe.wait_ge(sem("hvn_ready"), j + 1)
                        pe.wait_ge(sem("hro_ready"), PRIMED + j)
                        for c in range(4):
                            bank = TP[c // 2]
                            kk = row(KF if c < 2 else KB)[:, c * P:(c + 1) * P]
                            qq = row(QF)[:, 256:512] if c < 2 else row(QB)[:, 0:256]
                            mm = pe.matmul(bank[:, (c % 2) * 256:(c % 2) * 256 + 256], kk, qq, start=True, stop=True)
                    mm.then_inc(sem("lv_done"), 1)

                if p == 1:
                    turn_v(row(VT), (sem("qk_ready"), j * 9 + 1), "hv_turned")
                if p in LEVEL_AT:
                    level(LEVEL_AT[p])
                if p == 13:
                    pe.wait_ge(sem("lv_free"), PRIMED + j * 10 + 10)
                    pe.wait_ge(sem("hg_done"), PRIMED + j)
                    for c in range(4):
                        mm = pe.matmul(OB[:], row(HVN)[:, c * P:(c + 1) * P], row(AT + c), start=(c == 0), stop=(c == 3))
                    mm.then_inc(sem("hav_done"), 1)
                if p == 14:
                    sum_rows(row(HSQ), TP[1], (sem("hsq_ready"), j + 1), "hss_done")

            def att_work(j, p):
                a = p // 4
                if p == 0:
                    pe.wait_ge(sem("pte0"), PRIMED + j * 4)
                    turn_v(row(VTA), (sem("qt_ready"), j + 1), "v_turned")
                if p % 4 == 0:
                    for hd in range(2):
                        u = 2 * a + hd
                        pe.wait_ge(sem("sm_done"), PRIMED + j * 8 + max(u - 1, 0))
                        o = 64 * hd
                        pe.matmul(SC[hd][:], row(QT)[o:o + 64, a * P:(a + 1) * P], row(KTR)[o:o + 64, :],
                                  start=True, stop=True).then_inc(sem("s_done"), 1)
                if p % 4 == 2:
                    for hd in range(2):
                        pe.wait_ge(sem("p_ready"), j * 8 + 2 * a + hd + 1)
                        if hd == 0 and a == 0:
                            pe.wait_ge(sem("vn_ready"), j + 1)
                        pe.wait_ge(sem(f"pte{hd}"), PRIMED + j * 4 + a)
                        for c in range(4):
                            mm = pe.transpose(TP[hd][:, c * P:(c + 1) * P], row(PRB + hd)[:, c * P:(c + 1) * P], IDN[:])
                        mm.then_inc(sem("pt_done"), 1)
                if p % 4 == 3:
                    if a == 0:
                        pe.wait_ge(sem("att_done"), PRIMED + j)
                    for hd in range(2):
                        pe.wait_ge(sem(f"pte{hd}"), PRIMED + j * 4 + a + 1)
                        for c in range(4):
                            mm = pe.matmul(OB[64 * hd:64 * hd + 64, a * P:(a + 1) * P],
                                           row(VN)[:, c * P + 64 * hd:c * P + 64 * hd + 64],
                                           row(PT + hd)[:, c * P:(c + 1) * P], start=(c == 0), stop=(c == 3))
                    mm.then_inc(sem("av_done"), 1)

            def ret_work(j, p):
                if p == 0:
                    turn_v(row(VTA), (sem("rqt_ready"), j + 1), "rv_turned")
                if 1 <= p <= 4:
                    c = p - 1
                    pe.wait_ge(sem("ra_ready"), PRIMED + j * 4 + max(c - 1, 0))
                    pe.matmul(SC[c % 2][:, 0:S - c * P], row(KTR)[:, c * P:(c + 1) * P], row(QT)[:, c * P:S],
                              start=True, stop=True).then_inc(sem("rs_done"), 1)
                if p == 6:
                    pe.wait_ge(sem("ra_ready"), PRIMED + j * 4 + 4)
                    pe.wait_ge(sem("rvn_ready"), j + 1)
                    pe.wait_ge(sem("ret_done"), PRIMED + j)
                    for c in range(4):
                        mm = pe.matmul(OB[:, c * P:S], row(VN)[:, c * P:(c + 1) * P], row(RA + c)[:, 0:S - c * P],
                                       start=(c == 0), stop=(c == 3), skip_group_check=True)
                    mm.then_inc(sem("rav_done"), 1)
                if p == 8:
                    sum_rows(row(NSQ), TP[1], (sem("rsq_ready"), j + 1), "rss_done")

            def dif_work(j, p):
                a = p // 4
                if p == 0:
                    pe.wait_ge(sem("dpte"), PRIMED + j * 4)
                    turn_v(row(VTA), (sem("dqt_ready"), j + 1), "dv_turned")
                if p % 4 == 0:
                    for hd in range(2):
                        u = 2 * a + hd
                        pe.wait_ge(sem("dsm_done"), PRIMED + j * 8 + max(u - 1, 0))
                        o, w = 64 * hd, (a + 1) * P
                        pe.matmul(SC[hd][:, 0:w], row(QT)[o:o + 64, a * P:(a + 1) * P], row(KTR)[o:o + 64, 0:w],
                                  start=True, stop=True).then_inc(sem("ds_done"), 1)
                if p % 4 == 2:
                    pe.wait_ge(sem("dp_ready"), j * 4 + a + 1)
                    if a == 0:
                        pe.wait_ge(sem("dvn_ready"), j + 1)
                    pe.wait_ge(sem("dpte"), PRIMED + j * 4 + a)
                    for c in range(a + 1):
                        mm = pe.transpose(TP[0][:, c * P:(c + 1) * P], row(PRB)[:, c * P:(c + 1) * P], IDN[:])
                    mm.then_inc(sem("dpt_done"), 1)
                if p % 4 == 3:
                    if a == 0:
                        pe.wait_ge(sem("dif_done"), PRIMED + j)
                    pe.wait_ge(sem("dpte"), PRIMED + j * 4 + a + 1)
                    for c in range(a + 1):
                        mm = pe.matmul(OB[:, a * P:(a + 1) * P], row(VN)[:, c * P:(c + 1) * P],
                                       row(PT)[:, c * P:(c + 1) * P], start=(c == 0), stop=(c == a))
                    mm.then_inc(sem("dav_done"), 1)
                if p == 15:
                    sum_rows(row(NSQ), TP[1], (sem("dsq_ready"), j + 1), "dss_done")

            WORK = {"hg": hg_work, "att": att_work, "ret": ret_work, "dif": dif_work}

            def step(t, rot=None, work=None, j=None, gen=None, norm=None):
                for p in range(16):
                    s, q = divmod(p, 4)
                    if t is not None:
                        quarter(t.plus(s), q, gen if s == 0 else None)
                    if rot is not None and p in (4, 8):
                        rotate(t.plus(s - 1), rot[0] + int(p == 8), rot[1])
                    if norm is not None and p == 7:
                        sum_rows(row(ACC), OB, norm, "ss_done")
                    if work is not None:
                        WORK[work](j, p)

            def slots(t, n, gen=None):
                for s in range(2):
                    for q in range(4):
                        quarter(t.plus(s), q, gen if s == 0 else None)
                with pe.Fori(1, n // 2) as i:
                    for s in range(2):
                        for q in range(4):
                            quarter(Tile(t.c + s, *t.terms, (2, i)), q)

            pe.wait_ge(sem("consts"), 32)
            pe.wait_ge(sem("ones_set"), 1)
            pe.wait_ge(sem("p_split"), 2)
            for m in range(KT):
                t, n = divmod(m, 8)
                if n % 2 == 0:
                    pe.wait_ge(sem("l_ready"), 4 * t + n // 2 + 1)
                if m >= 2:
                    pe.wait_ge(sem("e_out"), m - 1)
                for k in range(2):
                    for i, (w, u) in enumerate(((WH, UH), (WH, UL), (WL, UH))):
                        mm = pe.matmul(Z[m % 2][:], w[:, 2 * n + k, :], u[:, KT - 2 + k, :], start=(k == 0 and i == 0),
                                       stop=(k == 1 and i == 2))
                mm.then_inc(sem("w_free") if n % 2 else sem("e_even"), 1)

            for s in range(2):
                for q in range(4):
                    quarter(Tile(T_HGG + s), q, 0 if s == 0 else None)
            sum_rows(row(ACC), OB, (sem("sq_used"), PRIMED + 16), "ss_done")
            with pe.Fori(1, 4) as i:
                for s in range(2):
                    for q in range(4):
                        quarter(Tile(T_HGG + s, (2, i)), q)
            step(Tile(T_HG))
            with pe.Fori(1, HG_HEADS) as i:
                step(Tile(T_HG, (4, i)), work="hg", j=i - 1)
            step(Tile(T_ATT), rot=(0, 0), work="hg", j=HG_HEADS - 1)
            pe.wait_ge(sem("hg_done"), PRIMED + HG_HEADS)
            with pe.Fori(1, PAIRS) as i:
                step(Tile(T_ATT, (4, i)), rot=(i * 2, 0), work="att", j=i - 1)
            step(None, work="att", j=PAIRS - 1)
            slots(Tile(T_OUT), 16, gen=1)
            sum_rows(row(ACC), OB, (sem("sq_used"), PRIMED + 32), "ss_done")
            slots(Tile(T_PG), 16, gen=2)
            sum_rows(row(ACC), OB, (sem("sq_used"), PRIMED + 48), "ss_done")

            R1 = 2 * PAIRS
            with pe.Fori(0, LAYERS) as l:
                base = l * PER_LAYER
                rots_l = l * (2 * (RET_HEADS + DIF_HEADS)) + R1
                step(Tile(T_L2 + R_RET, (PER_LAYER, l)), rot=(rots_l, 1), gen=l * 2 + 3,
                     norm=(sem("sq_used"), PRIMED + l * 32 + 64))
                with pe.Fori(1, RET_HEADS) as i:
                    step(Tile(T_L2 + R_RET, (PER_LAYER, l), (4, i)), rot=(rots_l + i * 2, 1), work="ret",
                         j=l * RET_HEADS + i - 1)
                step(Tile(T_L2 + R_DIF, (PER_LAYER, l)), rot=(rots_l + 2 * RET_HEADS, 2), work="ret",
                     j=l * RET_HEADS + RET_HEADS - 1)
                rets = pe.to_reg(l * RET_HEADS + (RET_HEADS + PRIMED))
                pe.wait_ge(sem("ones_set"), 1)
                pe.wait_ge(sem("ret_done"), rets)
                with pe.Fori(1, DIF_HEADS) as i:
                    step(Tile(T_L2 + R_DIF, (PER_LAYER, l), (4, i)), rot=(rots_l + 2 * RET_HEADS + i * 2, 2),
                         work="dif", j=l * DIF_HEADS + i - 1)
                step(Tile(T_L2 + R_LX, (PER_LAYER, l)), work="dif", j=l * DIF_HEADS + DIF_HEADS - 1)
                for m in range(4, 2 * LRU_TILES):
                    for q in range(4):
                        quarter(Tile(T_L2 + R_LX + m, (PER_LAYER, l)), q)
                    b = m - LRU_TILES
                    if b < 0:
                        continue
                    if b == 0:
                        pe.wait_ge(sem("dif_done"), PRIMED + l * DIF_HEADS + DIF_HEADS)
                        pe.wait_ge(sem("gw_loaded"), l * 16 + 16)
                    if b in (0, 3):
                        pe.wait_ge(sem("xc_ready"), l * 6 + b + 3)
                    for g in range(2):
                        pe.wait_ge(sem("gate_read"), PRIMED + (l * 12 + 2 * b if b else l * 12))
                        use = [n for n, (x, y) in enumerate(LRU_PAIRS) if y == b]
                        for n in use:
                            mm = pe.matmul(SC[g][:], view(GW, (g * NG + n) * P, [[1, P]]), row(XC + LRU_PAIRS[n][0]),
                                           start=(n == use[0]), stop=(n == use[-1]))
                        mm.then_inc(sem("gate_done"), 1)
                slots(Tile(T_L2 + R_OUT, (PER_LAYER, l)), 16, gen=l * 2 + 4)
                sum_rows(row(ACC), OB, (sem("sq_used"), PRIMED + l * 32 + 80), "ss_done")

        @block.scalar
        def _(act):
            def high(t, q):
                n = t.plus(1)
                act.wait_ge(sem("w_raw1" if n.odd else "w_raw0"), n.pair() * 16 + 16)
                act.wait_ge(sem("w_free"), t.times(4, q + 1))
                act.activation(WH[:, 4 * q:4 * q + 4, :],
                               RAW[:, n.odd, 512 * q:512 * q + 512].rearrange("p (k c) -> p k c", k=4),
                               ACT.Copy).then_inc(sem("h_ready"), 1)

            def copy(dst, src, done=None, **kw):
                i = act.activation(dst, src, ACT.Copy, **kw)
                if done:
                    i.then_inc(sem(done), 1)

            def inv_root(bank, dst, width, wait, done):
                act.wait_ge(*wait)
                act.activation(dst, bank[:], ACT.Ln, bias=CS[:, C_EPS:C_EPS + 1], scale=1.0 / width)
                act.drain()
                act.activation(dst, dst, ACT.Exp, scale=-0.5).then_inc(sem(done), 1)

            def gate_exp(t, src=RW, dst=TM, done="gexp"):
                act.wait_ge(sem("z_free"), t.times(1, -T_HGG + 1))
                act.activation(row(dst), row(src), ACT.Exp, scale=-1.0).then_inc(sem(done), 1)

            def hg_work(j, p):
                if p == 1:
                    act.wait_ge(sem("hav_done"), PRIMED + j)
                    act.wait_ge(sem("hv_turned"), j + 1)
                    copy(row(HVN), TP[0][:], "hvn_ready")
                    act.wait_ge(sem("lv_done"), j * 10 + 1)
                    copy(view(AT, 0, [[S + P, 4], [1, P]]), SC[0][:].rearrange("p (c t) -> p c t", c=4), "lv_free")
                n = LEVEL_AT.get(p, -1) + 1
                if 1 <= n <= 7:
                    h = 1 << (n - 1)
                    act.wait_ge(sem("qk_ready"), j * 9 + n)
                    copy(view(KM, 0, [[2 * h, S // (2 * h)], [h, 2], [1, h]]),
                         view(KF, 0, [[2 * h, S // (2 * h)], [2 * S + h, 2], [1, h]]), "km_ready")
                if n == 9:
                    act.wait_ge(sem("lv_done"), j * 10 + 9)
                    act.wait_ge(sem("lv_free"), PRIMED + j * 10 + 8)
                    copy(view(AT, P, [[2 * S + 2 * P, 2], [S - P, 2], [1, P]]),
                         SC[0][:].rearrange("p (a b t) -> p a b t", a=2, b=2), "lv_free")
                if n == 10:
                    act.wait_ge(sem("lv_done"), j * 10 + 10)
                    copy(view(AT, 256, [[S, 2], [1, 256]]), TP[0][:].rearrange("p (a t) -> p a t", a=2))
                    copy(view(AT + 2, 0, [[S, 2], [1, 256]]), TP[1][:].rearrange("p (a t) -> p a t", a=2), "lv_free")
                if p == 13:
                    act.wait_ge(sem("hav_done"), PRIMED + j + 1)
                    act.activation(row(HSQ), OB[:], ACT.Square).then_inc(sem("hsq_ready"), 1)
                if p == 14:
                    act.wait_ge(sem("hg_done"), PRIMED + j)
                    inv_root(TP[1], row(HRO), P, (sem("hss_done"), j + 1), "hro_ready")

            def att_work(j, p):
                a = p // 4
                if p == 0:
                    act.wait_ge(sem("av_done"), PRIMED + j * 4)
                    act.wait_ge(sem("v_turned"), j + 1)
                    copy(row(VN), TP[0][:], "vn_ready")
                if p % 4 == 1:
                    for hd in range(2):
                        u = 2 * a + hd
                        act.wait_ge(sem("sm_done"), PRIMED + j * 8 + u + 1)
                        act.wait_ge(sem("pt_done"), PRIMED + j * 8 + max(u - 1, 0))
                        act.activation(row(PRB + hd), row(SMR + hd), ACT.Exp, bias=SM[:, hd:hd + 1], scale=-1.0,
                                       accum_out=SM[:, 2 + hd:3 + hd]).then_inc(sem("exp_done"), 1)
                if p % 4 == 2:
                    act.wait_ge(sem("pt_done"), PRIMED + j * 8 + 2 * a + 1)
                    act.wait_ge(sem("av_done"), PRIMED + j * 4 + a)
                    copy(row(PT), TP[0][:], "pte0")

            def ret_work(j, p, load=None):
                if p == 0:
                    act.wait_ge(sem("rav_done"), PRIMED + j)
                    act.wait_ge(sem("rv_turned"), j + 1)
                    copy(row(VN), TP[0][:], "rvn_ready")
                if p == 5 and load is not None:
                    act.wait_ge(sem("ra_ready"), PRIMED + j * 4 + 4)
                    act.dma_start(row(DEC), dec[load]).then_inc(sem("dec_loaded"), 16)
                if p == 6:
                    act.wait_ge(sem("rav_done"), PRIMED + j + 1)
                    act.activation(row(NSQ), OB[:], ACT.Square).then_inc(sem("rsq_ready"), 1)
                if p == 8:
                    act.wait_ge(sem("ret_done"), PRIMED + j)
                    inv_root(TP[1], row(NRO), P, (sem("rss_done"), j + 1), "rro_ready")

            def dif_work(j, p):
                a = p // 4
                w = (a + 1) * P
                if p == 0:
                    act.wait_ge(sem("dav_done"), PRIMED + j * 4)
                    act.wait_ge(sem("dv_turned"), j + 1)
                    copy(row(VN), TP[0][:], "dvn_ready")
                if p % 4 == 1:
                    for hd in range(2):
                        u = 2 * a + hd
                        act.wait_ge(sem("dsm_done"), PRIMED + j * 8 + u + 1)
                        act.wait_ge(sem("dpt_done"), PRIMED + j * 4 + a)
                        act.activation(row(PRB + hd)[:, 0:w], row(SMR + hd)[:, 0:w], ACT.Exp, bias=SM[:, hd:hd + 1],
                                       scale=-1.0, accum_out=SM[:, 2 + hd:3 + hd]).then_inc(sem("dexp_done"), 1)
                if p % 4 == 2:
                    act.wait_ge(sem("dpt_done"), PRIMED + j * 4 + a + 1)
                    act.wait_ge(sem("dav_done"), PRIMED + j * 4 + a)
                    copy(row(PT)[:, 0:w], TP[0][:, 0:w], "dpte")
                if p == 15:
                    act.wait_ge(sem("dif_done"), PRIMED + j)
                    act.wait_ge(sem("dav_done"), PRIMED + j * 4 + 4)
                    act.activation(row(NSQ), OB[:], ACT.Square).then_inc(sem("dsq_ready"), 1)
                    inv_root(TP[1], row(NRO), P, (sem("dss_done"), j + 1), "dro_ready")

            WORK = {"hg": hg_work, "att": att_work, "ret": ret_work, "dif": dif_work}

            def step(t, gate=False, hg=False, work=None, j=None, norm=None, **kw):
                for p in range(16):
                    s, q = divmod(p, 4)
                    if t is not None:
                        high(t.plus(s), q)
                    if norm is not None and p == 7:
                        inv_root(OB, row(RSTD), D, norm, "rstd_ready")
                    if hg and p in (3, 7, 11):
                        gate_exp(t.plus(s), SG, SE, "sg_exp")
                    if work is not None:
                        WORK[work](j, p, **kw)
                    if gate and p == 15:
                        gate_exp(t.plus(3))

            def split(n, src, scale, wait_free):
                act.wait_ge(*wait_free)
                with act.Fori(0, KT) as m:
                    if scale is None:
                        act.activation(UH[:, m, :], src[:, m, :], ACT.Copy).then_inc(sem("uh_ready"), 1)
                    else:
                        if n is not None:
                            act.wait_ge(sem("h_new"), n + m + 1)
                        act.activation(UH[:, m, :], src[:, m, :], ACT.Copy,
                                       scale=scale[:, bass.ds(m, 1)]).then_inc(sem("uh_ready"), 1)

            def squares(n):
                for s in range(2):
                    act.wait_ge(sem("sq_used"), PRIMED + n)
                    act.activation(row(SQ0 + s), row(H + s), ACT.Square).then_inc(sem("sq_ready"), 1)
                with act.Fori(1, KT // 2) as i:
                    for s in range(2):
                        act.wait_ge(sem("sq_used"), PRIMED + i * 2 + n + s - 1)
                        act.activation(row(SQ0 + s), W[:, i * 2 + (H + s), :], ACT.Square).then_inc(sem("sq_ready"), 1)

            def out_slots(t, n, ss, root):
                def one(tt, m, s, used):
                    for q in range(4):
                        high(tt, q)
                    act.wait_ge(sem("w_free"), tt.times(4, 4))
                    act.wait_ge(sem("sq_used"), PRIMED + used)
                    act.activation(row(SQ0 + s), Z[s][:], ACT.Square).then_inc(sem("sq_ready"), 1)
                    copy(MIX[:, m, :], Z[s][:], "z_free")

                for s in range(2):
                    one(t.plus(s), s, s, n)
                with act.Fori(1, KT // 2) as i:
                    for s in range(2):
                        one(Tile(t.c + s, *t.terms, (2, i)), i * 2 + s, s, i * 2 + n + s - 1)
                inv_root(OB, row(ACC), D, (sem("ss_done"), ss), root)

            def load_h(src, done):
                for g in range(4):
                    act.dma_start(W[:, H + 4 * g:H + 4 * g + 4, :], src[4 * g:4 * g + 4].rearrange("m p t -> p m t")
                                  ).then_inc(sem(done), 16)

            def store_h(wait):
                for g in range(4):
                    act.wait_ge(sem("h_new"), wait + 4 * g + 4)
                    act.dma_start(out[4 * g:4 * g + 4].rearrange("m p t -> p m t"), W[:, H + 4 * g:H + 4 * g + 4, :]
                                  ).then_inc(sem("h_stored"), 16)

            act.dma_start(MIX[:, 14:16, :], pT.rearrange("k p t -> p k t")).then_inc(sem("p_loaded"), 16)
            act.dma_start(MIX[:, 0, :].bitcast(I32), pos1.to_broadcast([P, S])).then_inc(sem("pos_loaded"), 16)
            act.dma_start(MIX[:, 1, :].bitcast(I32), pos2.to_broadcast([P, S])).then_inc(sem("pos_loaded"), 16)
            act.dma_start(CS[:], cst).then_inc(sem("cs_loaded"), 16)
            act.dma_start(PR1[:], par1).then_inc(sem("cs_loaded"), 16)
            act.dma_start(IDN[:], idn).then_inc(sem("consts"), 16)
            act.dma_start(ROT[:], rots.rearrange("n k m -> k n m")).then_inc(sem("consts"), 16)
            act.dma_start(W[:, SQ1:SQ1 + 2, :].rearrange("p a b -> p (a b)"), masks.rearrange("p n t -> p (n t)")
                          ).then_inc(sem("masks_loaded"), 16)
            load_h(xT, "h_loaded")
            for q in range(4):
                act.wait_ge(sem("w_raw0"), 16)
                act.activation(WH[:, 4 * q:4 * q + 4, :], RAW[:, 0, 512 * q:512 * q + 512].rearrange("p (k c) -> p k c", k=4),
                               ACT.Copy).then_inc(sem("h_ready"), 1)
            act.wait_ge(sem("p_loaded"), 16)
            for k in range(2):
                copy(UH[:, 14 + k, :], MIX[:, 14 + k, :], "ph_ready")
            for n in range(6):
                act.wait_ge(sem("angle_ready"), n + 1)
                act.activation(MIX[:, 8 + n, :], MIX[:, 8 + n, :], ACT.Sin).then_inc(sem("table_ready"), 1)
            act.wait_ge(sem("table_ready"), 6)
            act.dma_start(tabs.rearrange("n p t -> p n t"), MIX[:, 8:14, :]).then_inc(sem("tables_out"), 16)
            act.preload_act_table_set("natural_log_exp_and_others")
            act.wait_ge(sem("lb_diff"), 1)
            act.activation(SM[:, 16:32], SM[:, 0:16], ACT.Exp).then_inc(sem("lb_exp"), 1)
            for m in range(KT):
                if m % 2 == 0:
                    act.wait_ge(sem("e_even"), m // 2 + 1)
                else:
                    act.wait_ge(sem("w_free"), m // 2 + 1)
                copy(row(E + m), Z[m % 2][:], "e_out")
                if m % 2:
                    high(Tile(m // 8), (m // 2) % 4)
            act.wait_ge(sem("e_out"), 16)
            act.dma_start(e_dram.rearrange("m p t -> p m t"), W[:, E:E + 16, :]).then_inc(sem("e_stored"), 16)

            act.wait_ge(sem("h_loaded"), 64)
            split(None, W[:, H:H + 16, :], PR1[:, G_PRE:G_PRE + 16], (sem("w_free"), 8))
            squares(0)
            act.wait_ge(sem("tables_out"), 16)
            act.wait_ge(sem("e_stored"), 16)
            for s in range(2):
                for q in range(4):
                    high(Tile(T_HGG + s), q)
            inv_root(OB, row(RSTD), D, (sem("ss_done"), 1), "rstd_ready")
            act.wait_ge(sem("rstd_ready"), 1)
            act.dma_start(row(CT1), tabs[0]).then_inc(sem("tab1_loaded"), 16)
            act.dma_start(row(ST1), tabs[1]).then_inc(sem("tab1_loaded"), 16)
            act.dma_start(W[:, BIAS:BIAS + 4, :], bias).then_inc(sem("tab1_loaded"), 16)
            for s in range(2):
                gate_exp(Tile(T_HGG + s))
            with act.Fori(1, 4) as i:
                for s in range(2):
                    for q in range(4):
                        high(Tile(T_HGG + s, (2, i)), q)
                    gate_exp(Tile(T_HGG + s, (2, i)))
            step(Tile(T_HG), hg=True)
            with act.Fori(1, HG_HEADS) as i:
                step(Tile(T_HG, (4, i)), hg=True, work="hg", j=i - 1)
            step(Tile(T_ATT), gate=True, work="hg", j=HG_HEADS - 1)
            act.wait_ge(sem("hg_done"), PRIMED + HG_HEADS)
            with act.Fori(1, PAIRS) as i:
                step(Tile(T_ATT, (4, i)), gate=True, work="att", j=i - 1)
            step(None, work="att", j=PAIRS - 1)
            act.wait_ge(sem("att_done"), PRIMED + PAIRS)
            load_h(xT, "h_loaded")
            act.dma_start(W[:, E:E + 16, :], e_dram.rearrange("m p t -> p m t")).then_inc(sem("e_loaded"), 16)
            split(None, MIX[:], None, (sem("w_free"), 4 * T_OUT))
            out_slots(Tile(T_OUT), 16, 2, "root_ready")
            act.wait_ge(sem("root_ready"), 1)
            act.wait_ge(sem("w_free"), 4 * T_PG)
            with act.Fori(0, KT) as m:
                act.wait_ge(sem("h_new"), m + 1)
                act.activation(UH[:, m, :], W[:, m, :], ACT.Copy).then_inc(sem("uh_ready"), 1)
            def pg_slot(t, m, s, cnt):
                for q in range(4):
                    high(t, q)
                act.wait_ge(sem("sq_used"), PRIMED + cnt)
                act.wait_ge(sem("w_free"), t.times(4, 4))
                act.activation(row(SQ0 + s), Z[s][:], ACT.Exp, scale=-1.0).then_inc(sem("z_free"), 1)

            def pg_square(m, s, cnt):
                act.wait_ge(sem("pg_prod"), cnt)
                act.activation(row(SQ0 + s), MIX[:, m, :], ACT.Square).then_inc(sem("sq_ready"), 1)

            for s in range(2):
                pg_slot(Tile(T_PG + s), s, s, 32)
                pg_square(s, s, s + 1)
            with act.Fori(1, KT // 2) as i:
                for s in range(2):
                    pg_slot(Tile(T_PG + s, (2, i)), i * 2 + s, s, i * 2 + 32 + s - 1)
                    pg_square(i * 2 + s, s, i * 2 + s + 1)
            inv_root(OB, row(ACC), D, (sem("ss_done"), 3), "root_ready")

            with act.Fori(0, LAYERS) as l:
                act.wait_ge(sem("par_used"), PRIMED + l)
                act.dma_start(PR2[:], par2[l]).then_inc(sem("par_loaded"), 16)
                act.dma_start(DL[:].rearrange("p a b -> p (a b)"), dlam[l].to_broadcast([P, 256])).then_inc(sem("par_loaded"), 16)
                act.wait_ge(sem("par_loaded"), l * 32 + 32)
                split(l * 16 + 16, W[:, H:H + 16, :], PR2[:, G2_PRE:G2_PRE + 16],
                      (sem("w_free"), Tile(T_L2, (PER_LAYER, l)).times(4)))
                act.wait_ge(sem("h_new"), l * 16 + 32)
                for g in range(4):
                    act.dma_start(out[4 * g:4 * g + 4].rearrange("m p t -> p m t"), W[:, H + 4 * g:H + 4 * g + 4, :]
                                  ).then_inc(sem("h_stored"), 16)
                squares(l * 32 + 48)
                act.dma_start(row(CTR), tabs[2]).then_inc(sem("tab2_loaded"), 16)
                act.dma_start(row(STR), tabs[3]).then_inc(sem("tab2_loaded"), 16)
                act.dma_start(row(CTD), tabs[4]).then_inc(sem("tab2_loaded"), 16)
                for n in range(2):
                    act.wait_ge(sem("lam_dot"), l + 1)
                    act.activation(SM[:, 10 + n:11 + n], SM[:, 8 + n:9 + n], ACT.Exp).then_inc(sem("lam_exp"), 1)
                act.wait_ge(sem("lam_abs"), l + 1)
                act.activation(SM[:, 18:24], SM[:, 12:18], ACT.Exp, scale=-1.0).then_inc(sem("lam_e"), 1)

                step(Tile(T_L2 + R_RET, (PER_LAYER, l)), gate=True, norm=(sem("ss_done"), l * 2 + 4))
                act.wait_ge(sem("h_stored"), l * 64 + 64)
                act.dma_start(row(STD), tabs[5]).then_inc(sem("tab3_loaded"), 16)
                act.dma_start(row(CM), cmask).then_inc(sem("tab3_loaded"), 16)
                act.dma_start(row(DEC), dec[0]).then_inc(sem("dec_loaded"), 16)
                act.dma_start(W[:, GW:GW + 7, :], gw[l].rearrange("p (r t) -> p r t", r=7)).then_inc(sem("gw_loaded"), 16)
                with act.Fori(1, RET_HEADS) as i:
                    step(Tile(T_L2 + R_RET, (PER_LAYER, l), (4, i)), gate=True, work="ret",
                         j=l * RET_HEADS + i - 1, load=i)
                step(Tile(T_L2 + R_DIF, (PER_LAYER, l)), gate=True, work="ret", j=l * RET_HEADS + RET_HEADS - 1)
                act.wait_ge(sem("ret_done"), PRIMED + l * RET_HEADS + RET_HEADS)
                with act.Fori(1, DIF_HEADS) as i:
                    step(Tile(T_L2 + R_DIF, (PER_LAYER, l), (4, i)), gate=True, work="dif",
                         j=l * DIF_HEADS + i - 1)
                step(Tile(T_L2 + R_LX, (PER_LAYER, l)), work="dif", j=l * DIF_HEADS + DIF_HEADS - 1)
                for m in range(4, 2 * LRU_TILES):
                    for q in range(4):
                        high(Tile(T_L2 + R_LX + m, (PER_LAYER, l)), q)
                    b = m - LRU_TILES
                    if b < 0:
                        continue
                    if b == 0:
                        act.wait_ge(sem("dif_done"), PRIMED + l * DIF_HEADS + DIF_HEADS)
                        act.wait_ge(sem("cl_ready"), l + 1)
                    act.wait_ge(sem("z_free"), Tile(T_L2 + R_LG + b, (PER_LAYER, l)).times(1, -T_HGG + 1))
                    act.activation(row(KN), row(QN), ACT.Exp, scale=-1.0).then_inc(sem("lg_exp"), 1)
                    for g in range(2):
                        act.wait_ge(sem("gate_done"), l * 12 + 2 * b + g + 1)
                        act.wait_ge(sem("scan_done"), PRIMED + l * 6 + b)
                        act.activation(row(LT[g]), SC[g][:], ACT.Exp, bias=SM[:, 32 + 6 * g + b:33 + 6 * g + b],
                                       scale=-1.0).then_inc(sem("gate_read"), 1)
                    act.wait_ge(sem("r_ready"), l * 6 + b + 1)
                    act.activation(row(LT[2]), row(LT[0]), ACT.Exp, scale=SM[:, 44 + b:45 + b]).then_inc(sem("a_ready"), 1)
                    act.activation(row(LT[3]), row(LT[0]), ACT.Exp, scale=SM[:, 50 + b:51 + b]).then_inc(sem("a_ready"), 1)
                    act.wait_ge(sem("m2_ready"), l * 6 + b + 1)
                    act.activation(row(LT[4]), row(LT[5]), ACT.Ln)
                    act.drain()
                    act.activation(row(LT[4]), row(LT[4]), ACT.Exp, scale=0.5).then_inc(sem("mult_ready"), 1)
                act.wait_ge(sem("lru_done"), l * 6 + 6)
                act.wait_ge(sem("h_stored"), l * 64 + 64)
                load_h(out, "h_loaded")
                split(None, MIX[:], None, (sem("w_free"), Tile(T_L2 + R_OUT, (PER_LAYER, l)).times(4)))
                out_slots(Tile(T_L2 + R_OUT, (PER_LAYER, l)), l * 32 + 64, l * 2 + 5, "root_ready")
            store_h(LAYERS * 16 + 16)
            act.wait_ge(sem("h_stored"), LAYERS * 64 + 64)

        @block.vector
        def _(v):
            def wait_apart(name, value):
                value = value if isinstance(value, int) else v.to_reg(value)
                v.wait_ge(sem("ones_set"), 1)
                v.wait_ge(sem(name), value)

            def rstd_mul(t, dst, done="z_free"):
                v.drain()
                v.wait_ge(sem("w_free"), t.times(4, 4))
                v.tensor_tensor(dst, Z[t.odd][:], row(RSTD), ALU.mult).then_inc(sem("z_free"), 1)

            def sigmoid_of(r):
                v.tensor_scalar(row(r), row(r), 1.0, None, ALU.add)
                v.drain()
                v.reciprocal(row(r), row(r))
                v.drain()

            def gate_tile(t, n, dst):
                rstd_mul(t, row(RW))
                v.wait_ge(sem("gexp"), n + 1)
                sigmoid_of(TM)
                v.tensor_tensor(dst, row(RW), row(TM), ALU.mult)
                v.drain()

            def raw_tile(t):
                v.drain()
                v.wait_ge(sem("w_free"), t.times(4, 4))
                v.tensor_copy(row(RW), Z[t.odd][:]).then_inc(sem("z_free"), 1)
                v.drain()

            def rotated(n, dst, cos, sin, scale):
                v.scalar_tensor_tensor(out=row(dst), in0=row(RW), scalar=scale, in1=row(cos), op0=ALU.mult, op1=ALU.mult)
                v.wait_ge(sem("rot_done"), n + 1)
                v.scalar_tensor_tensor(out=row(TM), in0=MB[:], scalar=scale, in1=row(sin), op0=ALU.mult,
                                       op1=ALU.mult).then_inc(sem("rot_used"), 1)
                v.drain()
                v.tensor_tensor(row(dst), row(dst), row(TM), ALU.add)

            def take_heads(done):
                v.drain()
                v.tensor_copy(row(QT), row(QN))
                v.tensor_copy(row(KTR), row(KN)).then_inc(sem(done), 1)

            def hg_work(j, p):
                if p == 0:
                    v.tensor_scalar(row(KF), row(FF), -1.0, 1.0, ALU.mult, ALU.add)
                    v.tensor_scalar(row(KB), row(FB), -1.0, 1.0, ALU.mult, ALU.add)
                    v.tensor_tensor(view(QB, 0, [[2 * S, 2], [1, S]]), view(FB, 0, [[S, 2], [1, S]]),
                                    view(Q, 0, [[0, 2], [1, S]]), ALU.mult)
                    v.tensor_tensor(view(TT, 0, [[S, 2], [1, 256]]), view(FB, 0, [[S, 2], [2, 256]]),
                                    view(FB, 1, [[S, 2], [2, 256]]), ALU.mult)
                    v.drain()
                    v.tensor_tensor(row(KS), row(KF), row(KB), ALU.add).then_inc(sem("qk_ready"), 1)
                n = LEVEL_AT.get(p, 0)
                if 1 <= n <= 8:
                    h = 1 << (n - 1)
                    nb = S // (2 * h)
                    v.wait_ge(sem("lv_done"), j * 10 + n + 1)
                    tr, to = (FB, 0) if n == 1 else (TT, [0, 256, 384, 448, 480, 496, 504, 508][n - 2])
                    x = view(QF, h, [[-(S + h), 2], [2 * h, nb], [1, h]])
                    y = view(tr + 1, to, [[1, 2], [2, nb], [0, h]])
                    v.tensor_tensor(x, x, y, ALU.mult)
                    x = view(QB, 0, [[3 * S + h, 2], [2 * h, nb], [1, h]])
                    y = view(tr, to + 1, [[-1, 2], [2, nb], [0, h]])
                    v.tensor_tensor(x, x, y, ALU.mult).then_inc(sem("qk_ready"), 1)
                    if 2 <= n <= 7:
                        to2 = [0, 256, 384, 448, 480, 496, 504, 508][n - 1]
                        v.tensor_tensor(view(TT, to2, [[S, 2], [1, nb]]), view(TT, to, [[S, 2], [2, nb]]),
                                        view(TT, to + 1, [[S, 2], [2, nb]]), ALU.mult)
                    if n <= 7:
                        if n == 1:
                            wait_apart("lv_free", PRIMED + j * 10 + 1)
                        m = MSK[:, n, :]
                        mk = bass.AP(m.tensor, m.offset, [m.ap[0], [0, 4], [1, P]])
                        v.copy_predicated(view(AT, 0, [[S + P, 4], [1, P]]), mk,
                                          SC[n % 2][:].rearrange("p (c t) -> p c t", c=4)).then_inc(sem("lv_free"), 1)
                        v.drain()
                    else:
                        v.drain()
                if p == 15:
                    v.wait_ge(sem("hro_ready"), PRIMED + j + 1)
                    v.tensor_tensor(row(HTMP), OB[:], row(HRO), ALU.mult)
                    v.drain()
                    dst = MIX[:, j + 8, :]
                    v.scalar_tensor_tensor(out=dst, in0=row(HTMP), scalar=PR1[:, G_HG:G_HG + 1], in1=dst,
                                           op0=ALU.mult, op1=ALU.mult).then_inc(sem("hg_done"), 1)

            def att_work(j, p):
                a = p // 4
                if p % 4 == 0:
                    for hd in range(2):
                        u = 2 * a + hd
                        wait_apart("s_done", j * 8 + u + 1)
                        v.tensor_tensor_reduce(row(SMR + hd), SC[hd][:], row(BIAS + a), -1.0, 3.0e38, ALU.add, ALU.min,
                                               SM[:, hd:hd + 1]).then_inc(sem("sm_done"), 1)
                if p % 4 == 1:
                    v.wait_ge(sem("exp_done"), j * 8 + 2 * a + 2)
                    v.reciprocal(SM[:, 4:6], SM[:, 2:4])
                    v.drain()
                    for hd in range(2):
                        v.tensor_scalar(row(PRB + hd), row(PRB + hd), SM[:, 4 + hd:5 + hd], None,
                                        ALU.mult).then_inc(sem("p_ready"), 1)
                if p % 4 == 2:
                    v.wait_ge(sem("pt_done"), PRIMED + j * 8 + 2 * a + 2)
                    v.wait_ge(sem("av_done"), PRIMED + j * 4 + a)
                    v.tensor_copy(row(PT + 1), TP[1][:]).then_inc(sem("pte1"), 1)
                if p == 15:
                    v.wait_ge(sem("av_done"), PRIMED + j * 4 + 4)
                    v.tensor_tensor(MIX[:, j, :], OB[:], MIX[:, j, :], ALU.mult).then_inc(sem("att_done"), 1)

            def ret_work(j, p, m=None):
                if 1 <= p <= 4:
                    c = p - 1
                    if c == 0:
                        v.wait_ge(sem("dec_loaded"), j * 16 + 16)
                    v.wait_ge(sem("rs_done"), j * 4 + c + 1)
                    v.tensor_tensor(row(RA + c)[:, 0:S - c * P], SC[c % 2][:, 0:S - c * P], row(DEC)[:, 0:S - c * P],
                                    ALU.mult).then_inc(sem("ra_ready"), 1)
                if p == 8:
                    v.wait_ge(sem("rro_ready"), j + 1)
                    v.tensor_tensor(row(NTMP), OB[:], row(NRO), ALU.mult)
                    v.drain()
                    v.tensor_tensor(MIX[:, m, :], row(NTMP), MIX[:, m, :], ALU.mult).then_inc(sem("ret_done"), 1)

            def dif_work(j, p, m=None):
                a = p // 4
                w = (a + 1) * P
                if p % 4 == 0:
                    for hd in range(2):
                        wait_apart("ds_done", j * 8 + 2 * a + hd + 1)
                        v.tensor_tensor_reduce(row(SMR + hd)[:, 0:w], SC[hd][:, 0:w], row(CM)[:, S - w:S], -1.0, 3.0e38,
                                               ALU.add, ALU.min, SM[:, hd:hd + 1]).then_inc(sem("dsm_done"), 1)
                if p % 4 == 1:
                    v.wait_ge(sem("dexp_done"), j * 8 + 2 * a + 2)
                    v.reciprocal(SM[:, 4:6], SM[:, 2:4])
                    v.drain()
                    v.tensor_tensor(SM[:, 6:7], SM[:, 5:6], SM[:, 60:61], ALU.mult)
                    v.tensor_scalar(row(PRB)[:, 0:w], row(PRB)[:, 0:w], SM[:, 4:5], None, ALU.mult)
                    v.drain()
                    v.scalar_tensor_tensor(out=row(PRB)[:, 0:w], in0=row(PRB + 1)[:, 0:w], scalar=SM[:, 6:7],
                                           in1=row(PRB)[:, 0:w], op0=ALU.mult, op1=ALU.add).then_inc(sem("dp_ready"), 1)
                if p == 15:
                    v.wait_ge(sem("dro_ready"), j + 1)
                    v.tensor_tensor(row(NTMP), OB[:], row(NRO), ALU.mult)
                    v.drain()
                    v.scalar_tensor_tensor(out=MIX[:, m, :], in0=row(NTMP), scalar=SM[:, 61:62], in1=MIX[:, m, :],
                                           op0=ALU.mult, op1=ALU.mult).then_inc(sem("dif_done"), 1)

            WORK = {"hg": hg_work, "att": att_work, "ret": ret_work, "dif": dif_work}

            def step(t, rot=None, tabs_=None, scales=None, gate=None, hg=None, work=None, j=None, lru=None, before=None, take=None, **kw):
                for p in range(16):
                    s, q = divmod(p, 4)
                    if rot is not None:
                        if p in (4, 8):
                            if before is not None and p == 4:
                                before()
                            v.drain()
                        if p in (3, 7):
                            raw_tile(t.plus(s))
                        if p in (4, 8):
                            rotated(rot + int(p == 8), QN if p == 4 else KN, *tabs_, scales[int(p == 8)])
                        if p == 11:
                            rstd_mul(t.plus(2), row(VTA))
                    if hg is not None:
                        if p in (3, 7, 11):
                            rstd_mul(t.plus(s), row(SG))
                        if p == 15:
                            rstd_mul(t.plus(3), row(VT))
                    if lru is not None and q == 3:
                        lru_conv(t.plus(s), s)
                    if work is not None:
                        v.drain()
                        WORK[work](j, p, **kw)
                    if hg is not None and p in (4, 8, 12):
                        v.wait_ge(sem("sg_exp"), hg * 3 + p // 4)
                        sigmoid_of(SE)
                        if p == 12:
                            v.tensor_tensor(row(Q), row(SG), row(SE), ALU.mult)
                        else:
                            d = 0 if p == 4 else 2
                            v.tensor_scalar(row(FF if p == 4 else FB), row(SE), LB[:, d + 1, :][:, hg_col(hg)],
                                            LB[:, d, :][:, hg_col(hg)], ALU.mult, ALU.add)
                    if take is not None and p == 13:
                        take_heads(take)
                    if gate is not None and p == 15:
                        gate_tile(t.plus(3), gate[0], MIX[:, gate[1], :])

            def hg_col(i):
                return bass.ds(i, 1)

            def lru_conv(t, m):
                rstd_mul(t, row(QN))
                v.drain()
                cw = lambda n: PR2[:, CONV_W + 4 * m + n:CONV_W + 4 * m + n + 1]
                v.tensor_scalar(row(XC + m), row(QN), cw(3), PR2[:, CONV_B + m:CONV_B + m + 1], ALU.mult, ALU.add)
                for n in range(1, 4):
                    v.drain()
                    i = v.scalar_tensor_tensor(out=row(XC + m)[:, n:S], in0=row(QN)[:, 0:S - n], scalar=cw(3 - n),
                                               in1=row(XC + m)[:, n:S], op0=ALU.mult, op1=ALU.add)
                i.then_inc(sem("xc_ready"), 1)

            def low(n, src, scale):
                with v.Fori(0, KT) as m:
                    v.wait_ge(sem("uh_ready"), m + 1 + n)
                    hi = UH[:, m, :].bitcast(F32)
                    if scale is None:
                        v.tensor_tensor(UL[:, m, :], src[:, m, :], hi, ALU.subtract).then_inc(sem("u_ready"), 1)
                    else:
                        v.scalar_tensor_tensor(out=UL[:, m, :], in0=src[:, m, :], scalar=scale[:, bass.ds(m, 1)], in1=hi,
                                               op0=ALU.mult, op1=ALU.subtract).then_inc(sem("u_ready"), 1)

            def sum_squares(n):
                def one(s, cnt, first=False):
                    v.wait_ge(sem("sq_ready"), cnt)
                    if first:
                        i = v.tensor_copy(row(ACC), row(SQ0))
                    else:
                        i = v.tensor_tensor(row(ACC), row(ACC), row(SQ0 + s), ALU.add)
                    i.then_inc(sem("sq_used"), 1)
                    v.drain()
                one(0, n + 1, True)
                one(1, n + 2)
                with v.Fori(1, KT // 2) as i:
                    for s in range(2):
                        one(s, i * 2 + n + s + 1)

            def new_residual(root, loaded, gcol):
                wait_apart("root_ready", root)
                wait_apart("h_loaded", loaded)
                with v.Fori(0, KT // 2) as i:
                    for s in range(2):
                        v.scalar_tensor_tensor(out=row(SQ0 + s), in0=MIX[:, i * 2 + s, :], scalar=gcol[:, bass.ds(i * 2 + s, 1)],
                                               in1=row(ACC), op0=ALU.mult, op1=ALU.mult)
                    v.drain()
                    for s in range(2):
                        v.tensor_tensor(W[:, i * 2 + s, :], W[:, i * 2 + s, :], row(SQ0 + s), ALU.add).then_inc(sem("h_new"), 1)
                    v.drain()

            def angles(posf, inv, dst_c, dst_s):
                TWO_PI = 6.283185307179586
                c1 = 6.28125
                c2 = 0.0019350051879882812
                c3 = TWO_PI - c1 - c2
                MAGIC = 12582912.0
                ang, nn, rr, mm = (MIX[:, r, :] for r in (4, 5, 6, 7))
                PI = 3.1415925
                v.tensor_scalar(ang, posf, CS[:, C_INV + inv:C_INV + inv + 1], None, ALU.mult)
                v.drain()
                v.tensor_scalar(nn, ang, 1.0 / TWO_PI, MAGIC, ALU.mult, ALU.add)
                v.drain()
                v.tensor_scalar(nn, nn, -MAGIC, None, ALU.add)
                v.drain()
                v.scalar_tensor_tensor(out=rr, in0=nn, scalar=-c1, in1=ang, op0=ALU.mult, op1=ALU.add)
                v.drain()
                v.scalar_tensor_tensor(out=rr, in0=nn, scalar=-c2, in1=rr, op0=ALU.mult, op1=ALU.add)
                v.drain()
                v.scalar_tensor_tensor(out=rr, in0=nn, scalar=-c3, in1=rr, op0=ALU.mult, op1=ALU.add)
                v.drain()
                v.tensor_scalar(mm, rr, TWO_PI / 4, -TWO_PI, ALU.is_gt, ALU.mult)
                v.drain()
                v.scalar_tensor_tensor(out=mm, in0=rr, scalar=TWO_PI / 4, in1=mm, op0=ALU.add, op1=ALU.add)
                v.drain()
                v.tensor_scalar(dst_c, mm, PI, -PI, ALU.min, ALU.max).then_inc(sem("angle_ready"), 1)
                v.tensor_scalar(dst_s, rr, PI, -PI, ALU.min, ALU.max).then_inc(sem("angle_ready"), 1)
                v.drain()

            v.memset(ONES[:], 1.0).then_inc(sem("ones_set"), 1)
            for k in range(2):
                v.wait_ge(sem("ph_ready"), k + 1)
                v.tensor_tensor(UL[:, 14 + k, :], MIX[:, 14 + k, :], UH[:, 14 + k, :].bitcast(F32),
                                ALU.subtract).then_inc(sem("p_split"), 1)
            v.wait_ge(sem("pos_loaded"), 32)
            v.wait_ge(sem("cs_loaded"), 32)
            for n in range(2):
                v.tensor_copy(MIX[:, 2 + n, :], MIX[:, n, :].bitcast(I32))
            v.wait_ge(sem("masks_loaded"), 16)
            v.tensor_copy(MSK[:].rearrange("p n t -> p (n t)"), W[:, SQ1:SQ1 + 2, :].rearrange("p a b -> p (a b)"))
            v.tensor_tensor(SM[:, 0:8], PR1[:, LBF + 8:LBF + 16], PR1[:, LBF:LBF + 8], ALU.subtract)
            v.tensor_tensor(SM[:, 8:16], PR1[:, LBB + 8:LBB + 16], PR1[:, LBB:LBB + 8], ALU.subtract).then_inc(sem("lb_diff"), 1)
            v.drain()
            for n in range(3):
                angles(MIX[:, 2 + (n > 0), :], n, MIX[:, 8 + 2 * n, :], MIX[:, 9 + 2 * n, :])
            v.wait_ge(sem("lb_exp"), 1)
            v.tensor_scalar(SM[:, 16:32], SM[:, 16:32], 1.0, None, ALU.add)
            v.drain()
            v.reciprocal(LB[:, 0, :], SM[:, 16:24])
            v.reciprocal(LB[:, 2, :], SM[:, 24:32])
            v.drain()
            v.tensor_scalar(LB[:, 1, :], LB[:, 0, :], -1.0, 1.0, ALU.mult, ALU.add)
            v.tensor_scalar(LB[:, 3, :], LB[:, 2, :], -1.0, 1.0, ALU.mult, ALU.add)

            low(0, W[:, H:H + 16, :], PR1[:, G_PRE:G_PRE + 16])
            sum_squares(0)
            v.wait_ge(sem("tables_out"), 16)
            v.wait_ge(sem("e_stored"), 16)
            v.wait_ge(sem("rstd_ready"), 1)
            for s in range(2):
                gate_tile(Tile(T_HGG + s), s, MIX[:, 8 + s, :])
            with v.Fori(1, 4) as i:
                for s in range(2):
                    gate_tile(Tile(T_HGG + s, (2, i)), i * 2 + s, MIX[:, i * 2 + (8 + s), :])
            step(Tile(T_HG), hg=0)
            v.drain()
            with v.Fori(1, HG_HEADS) as i:
                step(Tile(T_HG, (4, i)), hg=i, work="hg", j=i - 1)
                v.drain()
            v.wait_ge(sem("tab1_loaded"), 48)
            for r in (CT1, ST1):
                v.tensor_tensor(row(r), row(r), row(RSTD), ALU.mult)
            v.drain()
            tb = (CT1, ST1)
            sc1 = (ATT_HD ** -0.5, 1.0)
            step(Tile(T_ATT), rot=0, tabs_=tb, scales=sc1, take="qt_ready", gate=(8, 0), work="hg", j=HG_HEADS - 1)
            with v.Fori(1, PAIRS) as i:
                step(Tile(T_ATT, (4, i)), rot=i * 2, tabs_=tb, scales=sc1, take="qt_ready", gate=(i + 8, i), work="att", j=i - 1)
            step(None, work="att", j=PAIRS - 1)
            low(16, MIX[:], None)
            sum_squares(16)
            new_residual(1, 128, PR1[:, G_POST:G_POST + 16])
            low(32, W[:, H:H + 16, :], None)
            v.wait_ge(sem("e_loaded"), 16)

            def pg_tile(m, s, cnt):
                v.wait_ge(sem("z_free"), cnt)
                sigmoid_of(SQ0 + s)
                v.drain()
                v.tensor_tensor(MIX[:, m, :], row(SQ0 + s), W[:, m + E, :] if not isinstance(m, int) else row(E + m),
                                ALU.mult).then_inc(sem("pg_prod"), 1)

            def pg_sum(s, cnt, first=False):
                v.wait_ge(sem("sq_ready"), cnt)
                if first:
                    i = v.tensor_copy(row(ACC), row(SQ0))
                else:
                    i = v.tensor_tensor(row(ACC), row(ACC), row(SQ0 + s), ALU.add)
                i.then_inc(sem("sq_used"), 1)
                v.drain()

            for s in range(2):
                pg_tile(s, s, T_PG + s - 1)
                pg_sum(s, 32 + s + 1, s == 0)
            with v.Fori(1, KT // 2) as i:
                for s in range(2):
                    pg_tile(i * 2 + s, s, i * 2 + (T_PG + s - 1))
                    pg_sum(s, i * 2 + 32 + s + 1)
            new_residual(2, 128, PR1[:, G_PLE:G_PLE + 16])

            with v.Fori(0, LAYERS) as l:
                wait_apart("par_loaded", l * 32 + 32)
                low(l * 32 + 48, W[:, H:H + 16, :], PR2[:, G2_PRE:G2_PRE + 16])
                for n in range(2):
                    v.tensor_tensor(DL[:, 2 * n, :], DL[:, 2 * n, :], DL[:, 2 * n + 1, :], ALU.mult)
                v.drain()
                for n in range(2):
                    i = v.tensor_reduce(SM[:, 8 + n:9 + n], DL[:, 2 * n, :], AX.X, ALU.add)
                i.then_inc(sem("lam_dot"), 1)
                lam = PR2[:, LAM:LAM + 6]
                v.tensor_scalar(SM[:, 12:18], lam, -1.0, None, ALU.mult)
                v.tensor_scalar(SM[:, 24:30], lam, 0.0, None, ALU.min)
                v.tensor_scalar(SM[:, 32:44], PR2[:, BA:BA + 12], -1.0, None, ALU.mult)
                v.drain()
                v.tensor_tensor(SM[:, 12:18], SM[:, 12:18], lam, ALU.max).then_inc(sem("lam_abs"), 1)
                sum_squares(l * 32 + 48)
                v.wait_ge(sem("lam_exp"), l * 2 + 2)
                v.tensor_tensor(SM[:, 60:61], SM[:, 11:12], SM[:, 10:11], ALU.subtract)
                v.drain()
                v.tensor_tensor(SM[:, 60:61], SM[:, 60:61], CS[:, bass.ds(l * 2 + C_LAM, 1)], ALU.subtract)
                v.tensor_tensor(SM[:, 61:62], PR2[:, G2_SUB:G2_SUB + 1], CS[:, bass.ds(l * 2 + (C_LAM + 1), 1)], ALU.mult)
                v.wait_ge(sem("lam_e"), l + 1)
                e, w, w2, pl = SM[:, 18:24], SM[:, 44:50], SM[:, 50:56], SM[:, 12:18]
                v.tensor_scalar(w, e, 2.0, None, ALU.add)
                v.drain()
                v.reciprocal(w, w)
                v.drain()
                v.tensor_tensor(w, w, e, ALU.mult)
                v.drain()
                v.tensor_tensor(w2, w, w, ALU.mult)
                v.drain()
                v.tensor_scalar(pl, w2, 1.0 / 15, None, ALU.mult)
                for n in (13, 11, 9, 7, 5, 3):
                    v.drain()
                    v.scalar_tensor_tensor(out=pl, in0=pl, scalar=1.0 / n, in1=w2, op0=ALU.add, op1=ALU.mult)
                v.drain()
                v.scalar_tensor_tensor(out=pl, in0=pl, scalar=1.0, in1=w, op0=ALU.add, op1=ALU.mult)
                v.drain()
                v.scalar_tensor_tensor(out=pl, in0=pl, scalar=-2.0, in1=SM[:, 24:30], op0=ALU.mult, op1=ALU.add)
                v.drain()
                v.tensor_scalar(SM[:, 44:50], pl, 8.0, None, ALU.mult)
                v.tensor_scalar(SM[:, 50:56], pl, 16.0, None, ALU.mult).then_inc(sem("cl_ready"), 1)

                def tables(l=l):
                    v.wait_ge(sem("rstd_ready"), l + 2)
                    v.wait_ge(sem("tab2_loaded"), l * 48 + 48)
                    for r in (CTR, STR, CTD):
                        v.tensor_tensor(row(r), row(r), row(RSTD), ALU.mult)

                scr = (1.0, 128 ** -0.5)
                scd = (64 ** -0.5, 1.0)
                rl = l * 20 + 16
                step(Tile(T_L2 + R_RET, (PER_LAYER, l)), rot=rl, tabs_=(CTR, STR), scales=scr, take="rqt_ready", gate=(l * 10 + 16, 0),
                     before=tables)
                v.wait_ge(sem("h_stored"), l * 64 + 64)
                v.wait_ge(sem("tab3_loaded"), l * 32 + 32)
                v.tensor_tensor(row(STD), row(STD), row(RSTD), ALU.mult)
                v.drain()
                with v.Fori(1, RET_HEADS) as i:
                    step(Tile(T_L2 + R_RET, (PER_LAYER, l), (4, i)), rot=rl + i * 2, tabs_=(CTR, STR), scales=scr, take="rqt_ready",
                         gate=(l * 10 + i + 16, i), work="ret", j=l * RET_HEADS + i - 1, m=i - 1)
                step(Tile(T_L2 + R_DIF, (PER_LAYER, l)), rot=rl + 12, tabs_=(CTD, STD), scales=scd, take="dqt_ready",
                     gate=(l * 10 + 22, 6), work="ret", j=l * RET_HEADS + RET_HEADS - 1, m=5)
                with v.Fori(1, DIF_HEADS) as i:
                    step(Tile(T_L2 + R_DIF, (PER_LAYER, l), (4, i)), rot=rl + i * 2 + 12, tabs_=(CTD, STD), scales=scd, take="dqt_ready",
                         gate=(l * 10 + i + 22, i + 6), work="dif", j=l * DIF_HEADS + i - 1, m=i + 5)
                step(Tile(T_L2 + R_LX, (PER_LAYER, l)), work="dif", j=l * DIF_HEADS + DIF_HEADS - 1, m=9, lru=True)
                for m in range(4, LRU_TILES):
                    lru_conv(Tile(T_L2 + R_LX + m, (PER_LAYER, l)), m)
                R_, I_, A_, E2, MU, M2, PO, TB = LT
                for b in range(LRU_TILES):
                    t = Tile(T_L2 + R_LG + b, (PER_LAYER, l))
                    v.drain()
                    rstd_mul(t, row(QN))
                    v.wait_ge(sem("lg_exp"), l * 6 + b + 1)
                    sigmoid_of(KN)
                    v.tensor_tensor(MIX[:, 10 + b, :], row(QN), row(KN), ALU.mult)
                    v.wait_ge(sem("gate_read"), PRIMED + l * 12 + 2 * b + 2)
                    v.tensor_scalar(view(LT[0], 0, [[1, 2 * S]]), view(LT[0], 0, [[1, 2 * S]]), 1.0, None, ALU.add)
                    v.drain()
                    v.reciprocal(row(R_), row(R_)).then_inc(sem("r_ready"), 1)
                    v.reciprocal(row(I_), row(I_))
                    v.drain()
                    v.tensor_tensor(row(I_), row(I_), row(XC + b), ALU.mult)
                    v.tensor_scalar(row(TB), row(R_), SM[:, 50 + b:51 + b], None, ALU.mult)
                    v.drain()
                    v.tensor_scalar(row(PO), row(TB), -1.0 / 5040, None, ALU.mult)
                    for f in (720, 120, 24, 6, 2, 1):
                        v.drain()
                        v.scalar_tensor_tensor(out=row(PO), in0=row(PO), scalar=-1.0 / f, in1=row(TB), op0=ALU.add, op1=ALU.mult)
                    v.wait_ge(sem("a_ready"), l * 12 + 2 * b + 2)
                    v.tensor_scalar(row(M2), row(E2), -1.0, 1.0, ALU.mult, ALU.add)
                    v.drain()
                    v.tensor_scalar(row(E2).bitcast(I32), row(TB), -0.25, None, ALU.is_gt)
                    v.drain()
                    v.copy_predicated(row(M2), row(E2).bitcast(I32), row(PO))
                    v.drain()
                    v.tensor_scalar(row(M2), row(M2), 1e-19, None, ALU.max).then_inc(sem("m2_ready"), 1)
                    v.wait_ge(sem("mult_ready"), l * 6 + b + 1)
                    v.tensor_tensor(row(I_), row(I_), row(MU), ALU.mult)
                    v.drain()
                    v.tensor_tensor_scan(row(HS + b), row(A_), row(I_), 0.0, ALU.mult, ALU.add).then_inc(sem("scan_done"), 1)
                    v.drain()
                    i = v.tensor_tensor(MIX[:, 10 + b, :], MIX[:, 10 + b, :], row(HS + b), ALU.mult).then_inc(sem("lru_done"), 1)
                v.drain()
                low(l * 32 + 64, MIX[:], None)
                sum_squares(l * 32 + 64)
                new_residual(l + 3, l * 64 + 192, PR2[:, G2_POST:G2_POST + 16])
                v.drain()
                v.tensor_scalar(SM[:, 62:63], SM[:, 61:62], 1.0, None, ALU.mult).then_inc(sem("par_used"), 1)


def tiles(w):
    r, c = w.shape
    return w.reshape(r // P, P, c // P, P).transpose(2, 1, 0, 3)


def cols(v):
    return v.reshape(-1, P).T


def rotation(width, half):
    m = np.zeros((P, P), np.float32)
    for h in range(0, P, width):
        for i in range(half):
            m[h + half + i, h + i] = -1.0
            m[h + i, h + half + i] = 1.0
    return m


def constants():
    rots = np.stack([rotation(64, 8), rotation(128, 64), rotation(64, 32)])
    inv1 = np.power(np.float32(500000.0), -np.arange(0, 16, 2, dtype=np.float32) / np.float32(16))
    invr = (1.0 / (np.float32(10000.0) ** np.linspace(0, 1, 64, dtype=np.float32))).astype(np.float32)
    invd = (1.0 / (np.float32(10000.0) ** (np.arange(0, 64, 2, dtype=np.float32) / np.float32(64)))).astype(np.float32)
    cst = np.zeros((P, CST), np.float32)
    for p in range(P):
        if p % 64 < 16:
            cst[p, 0] = inv1[p % 8]
        cst[p, 1] = invr[p % 64]
        cst[p, 2] = invd[p % 32]
    cst[:, C_EPS] = EPS
    for l in range(LAYERS):
        li = 0.8 - 0.6 * np.exp(-0.3 * l)
        cst[:, C_LAM + 2 * l], cst[:, C_LAM + 2 * l + 1] = li, 1.0 - li
    a = np.arange(P)
    x = a[:, None] ^ a[None, :]
    masks = np.zeros((P, 8, P), np.float32)
    for n in range(1, 8):
        masks[:, n, :] = (x >= 1 << (n - 1)) & (x < 1 << n)
    t = np.arange(S)
    d = t[:, None] - t[None, :]
    count = np.zeros((S, S))
    for w, dil in ((128, 1), (512, 4), (2048, 16)):
        half = (w // 2) // dil
        count += (d % dil == 0) & (np.abs(d) // dil <= half)
    bias = np.where(count > 0, np.log(np.maximum(count, 1)), NEG).astype(np.float32)
    bias = np.ascontiguousarray(bias.reshape(4, P, S).transpose(1, 0, 2))
    dec = np.zeros((RET_HEADS, P, S), np.float32)
    dd = np.arange(S)[None, :] - np.arange(P)[:, None]
    for h in range(RET_HEADS):
        dec[h] = np.where(dd >= 0, np.exp(np.maximum(dd, 0) * np.log1p(-2.0 ** (-5.0 - h))), 0.0)
    cm = np.zeros((P, S), np.float32)
    cm[:, S - P:] = np.where(a[None, :] <= a[:, None], 0.0, NEG)
    return dict(cst=cst, rots=rots, idn=np.eye(P, dtype=np.float32), masks=masks, bias=bias, dec=dec, cmask=cm)


def layout(i):
    w1 = tiles(i["w_in"][0])
    A = ATT_W // P
    aq, ak, av, ag, hq, ff, fb, hv, hg = (range(8 * n, 8 * n + 8) for n in range(9))
    order1 = list(hg) + [x for j in range(8) for x in (ff[j], fb[j], hq[j], hv[j])] + \
        [x for j in range(8) for x in (aq[j], ak[j], av[j], ag[j])]
    pp = i["w_pp"][0].reshape(2, P, 2, 8, P).transpose(2, 1, 3, 0, 4).reshape(2, P, KT * P)
    parts = [pp, w1[order1], tiles(i["w_out"][0]), tiles(i["w_pg"][0])]
    for l in range(LAYERS):
        w2 = tiles(i["w_in_2"][l])
        o2 = [6 * n + j for j in range(6) for n in range(4)] + [24 + 4 * n + j for j in range(4) for n in range(4)] + \
            list(range(40, 52))
        parts += [w2[o2], tiles(i["w_out_2"][l])]
    parts.append(parts[0][0:1])
    wt = np.concatenate([x.reshape(-1, P, KT * P) for x in parts])
    par1 = np.concatenate([cols(i["g_pre"][0]), cols(i["g_post"][0]), cols(i["g_ple"][0]), cols(i["g_hg"][0])] +
                          [cols(i[n][r]) for n in ("lb_fwd", "lb_bwd") for r in range(2)], 1)
    par2, gws = [], []
    for l in range(LAYERS):
        cw = i["lru_conv_w_2"][l].reshape(4, LRU_TILES, P).transpose(2, 1, 0).reshape(P, 24)
        par2.append(np.concatenate([cols(i["pre_norm_g_2"][l]), cols(i["post_norm_g_2"][l]), cols(i["diff_subln_g_2"][l]), cw] +
                                   [cols(i[n][l]) for n in ("lru_conv_b_2", "lru_ba_2", "lru_bx_2", "lru_lambda_2")], 1))
        both = []
        for n in ("lru_wa_2", "lru_wx_2"):
            full = np.zeros((8 * LRU_BW, 8 * LRU_BW), np.float32)
            for b in range(8):
                full[b * LRU_BW:(b + 1) * LRU_BW, b * LRU_BW:(b + 1) * LRU_BW] = i[n][l, b]
            both += [full[P * x:P * x + P, P * y:P * y + P] for x, y in LRU_PAIRS]
        gws.append(np.stack(both, 1).reshape(P, 2 * NG * P))
    dl = np.stack([np.concatenate([i[f"diff_lambda_{n}_2"][l] for n in ("q1", "k1", "q2", "k2")]) for l in range(LAYERS)])
    return dict(wt=wt, xT=i["x"][0].T.reshape(KT, P, S), pT=i["p"][0, 0].T.reshape(2, P, S),
                pos1=i["positions"], pos2=i["positions_2"], par1=par1, par2=np.stack(par2), dlam=dl[:, None, :],
                gw=np.stack(gws))


ORDER = ["wt", "xT", "pT", "pos1", "pos2", "par1", "par2", "dlam", "gw", "cst", "rots", "idn", "masks", "bias", "dec", "cmask"]


def kernel(**inputs):
    import concourse.bacc as _bacc
    from concourse.bass_utils import run_bass_kernel_spmd as _run

    arrays = layout({n: np.asarray(a) for n, a in inputs.items()})
    arrays.update(constants())
    nc = _bacc.Bacc("TRN2", target_bir_lowering=False, num_devices=1)
    feed, args = {}, []
    for name in ORDER:
        a = np.ascontiguousarray(arrays[name])
        feed[f"in_{name}"] = a
        args.append(nc.dram_tensor(f"in_{name}", a.shape, mybir.dt.from_np(a.dtype), kind="ExternalInput").ap())
    args.append(nc.dram_tensor("out_hT", (KT, P, S), F32, kind="ExternalOutput").ap())
    build(nc, *args)
    r = _run(nc, [feed], core_ids=[0])
    return np.ascontiguousarray(r.results[0]["out_hT"].reshape(D, S).T)[None]
```

```python
from contextlib import ExitStack

import numpy as np
import concourse.bass as bass
from concourse import mybir

F32 = mybir.dt.float32
F32R = mybir.dt.float32r
U8 = mybir.dt.uint8
I32 = mybir.dt.int32
ACT = mybir.ActivationFunctionType
ALU = mybir.AluOpType
AX = mybir.AxisListType

P = 128
S = 512
D = 2048
KT = D // P
EPS = 1e-6
NEG = -1e30
ROWS = 36
PRIMED = 1
REUSE_SIGNALS = ("hav_done", "hg_done", "lv_free", "hro_ready", "att_done", "pte0", "pte1", "sm_done", "pt_done", "av_done",
                 "ra_ready", "ret_done", "dpte", "dsm_done", "dif_done", "dpt_done", "dav_done", "rav_done", "scan_done",
                 "gate_read", "par_used", "sq_used")

ATT_W, ATT_HD = 1024, 64
HG_HEADS = 8
PAIRS = 8
LAYERS = 2
RET_HEADS, DIF_HEADS, LRU_TILES = 6, 4, 6
LRU_BW = 96

T_PP, T_HGG, T_HG, T_ATT, T_OUT, T_PG, T_L2 = 0, 2, 10, 42, 74, 90, 106
R_LX, R_RET, R_DIF, R_LG, R_OUT, PER_LAYER = 0, 6, 30, 46, 52, 68
NT = T_L2 + LAYERS * PER_LAYER

G_PRE, G_POST, G_PLE, G_HG, LBF, LBB = 0, 16, 32, 48, 49, 65
PAR1 = 81
G2_PRE, G2_POST, G2_SUB, CONV_W, CONV_B, BA, BX, LAM = 0, 16, 32, 33, 57, 63, 69, 75
PAR2 = 81
C_INV, C_EPS, C_LAM = 0, 3, 4
CST = 8

LRU_PAIRS = [(a, b) for b in range(LRU_TILES) for a in range(LRU_TILES)
             if any(max(LRU_BW * n, P * a) < min(LRU_BW * (n + 1), P * (a + 1)) and
                    max(LRU_BW * n, P * b) < min(LRU_BW * (n + 1), P * (b + 1)) for n in range(8))]
NG = len(LRU_PAIRS)


LEVEL_AT = {1: 0, 2: 1, 3: 2, 4: 3, 6: 4, 7: 5, 8: 6, 10: 7, 11: 8, 12: 9}

DIF_SCORES = {0: 0, 3: 1, 7: 2, 11: 3}
DIF_SOFTMAX = {1: 0, 4: 1, 8: 2, 12: 3}
DIF_TURN = {3: 0, 6: 1, 10: 2, 14: 3}
DIF_VALUES = {4: 0, 7: 1, 11: 2, 15: 3}


class Tile:

    def __init__(self, c, *terms):
        self.c, self.terms = c, terms

    def plus(self, n):
        return Tile(self.c + n, *self.terms)

    def times(self, k, add=0):
        v = self.c * k + add
        for m, i in self.terms:
            v = i * (m * k) + v
        return v

    def pair(self):
        v = self.c // 2
        for m, i in self.terms:
            v = i * (m // 2) + v
        return v

    @property
    def odd(self):
        return self.c % 2


def build(nc, wt, xT, pT, pos1, pos2, par1, par2, dlam, gw, cst, idn, masks, bias, dec, cmask, out):
    ctx = ExitStack()
    with ctx:
        sems = {}

        def sb(name, shape, dt=F32):
            return ctx.enter_context(nc.sbuf_tensor(name, shape, dt))

        def sem(name):
            if name not in sems:
                sems[name] = ctx.enter_context(nc.semaphore(name))
            return sems[name]

        tabs = nc.dram_tensor("rope_tables", [6, P, S], F32, kind="Internal").ap()
        e_dram = nc.dram_tensor("e_scratch", [KT, P, S], F32, kind="Internal").ap()

        RAW = sb("w_raw", [P, 2, KT * P])
        WH = sb("w_high", [P, KT, P], F32R)
        WL = sb("w_low", [P, KT, P], F32R)
        UH = sb("u_high", [P, KT, S], F32R)
        UL = sb("u_low", [P, KT, S], F32R)
        MIX = sb("mixed", [P, KT, S])
        W = sb("work", [P, ROWS, S])
        MSK = sb("level_masks", [P, 8, P], U8)
        ONES = sb("ones", [P, P])
        IDN = sb("identity", [P, P])
        PR1 = sb("params_1", [P, PAR1])
        PR2 = sb("params_2", [P, PAR2])
        LB = sb("lower_bounds", [P, 4, 8])
        DL = sb("lambda_vectors", [P, 4, 64])
        CS = sb("constants", [P, CST])
        SM = sb("small", [P, 64])
        PRIME = sb("prime", [1, len(REUSE_SIGNALS) + 1])

        Z = [ctx.enter_context(nc.psum_tensor(f"z{i}", [P, S], F32)) for i in range(2)]
        SC = [ctx.enter_context(nc.psum_tensor(f"scores{i}", [P, S], F32)) for i in range(2)]
        TP = [ctx.enter_context(nc.psum_tensor(f"turned{i}", [P, S], F32)) for i in range(2)]
        OB = ctx.enter_context(nc.psum_tensor("o_bank", [P, S], F32))

        def row(r, n=1):
            return W[:, r, :] if n == 1 else W[:, r:r + n, :]

        def view(r, off, dims):
            a = W[:]
            return bass.AP(a.tensor, r * S + off, [a.ap[0]] + dims)

        H = 0
        E = 16
        SQ0, SQ1, ACC, RSTD = 32, 33, 34, 35
        COS, SIN = 4, 5
        FB, FF, Q, VT, QB, KF, QF, KB, TT, HVN, AT = 0, 1, 2, 3, 4, 5, 6, 7, 8, 10, 11
        HSQ, HRO, HTMP, KM, KS, SG, SE = 15, 16, 17, 18, 19, 20, 21
        QT, KTR, VTA, QN, KN, RW, TM = 22, 23, 24, 25, 26, 27, 28
        CT1, ST1, BIAS = 29, 30, 31
        SMR, PRB, VN, PT = 0, 2, 4, 5
        CTR, STR, CTD, STD, CM, DEC = 29, 30, 31, 32, 33, 34
        NRO = 8
        RA = [0, S, 2 * S - P, 3 * S - 3 * P]
        LTB, LR, LI, LA = 3, 5, 6, 7
        GW, XC = 9, 16

        PH, PL = UL[:, 12:14, :], UL[:, 14:16, :]

        block = ctx.enter_context(nc.Block())

        @block.sync
        def _(sp):
            def load(t):
                sp.dma_start(RAW[:, t.odd, :], wt[t_index(t)]).then_inc(sem("w_raw1" if t.odd else "w_raw0"), 16)

            def t_index(t):
                return t.times(1)

            load(Tile(0))
            load(Tile(1))
            with sp.Fori(1, NT // 2) as g:
                for o in range(2):
                    t = Tile(o, (2, g))
                    sp.wait_ge(sem("l_ready"), t.times(4, -4))
                    load(t)
            sp.wait_ge(sem("l_ready"), 4 * NT - 4)
            load(Tile(NT))
            sp.wait_ge(sem("w_raw0"), 16 * (NT // 2 + 1))

        @block.gpsimd
        def _(pool):
            for n, name in enumerate(REUSE_SIGNALS):
                pool.memset(PRIME[:, n:n + 1], 0.0).then_inc(sem(name), PRIMED)
            pool.memset(PRIME[:, len(REUSE_SIGNALS):], 0.0).then_inc(sem("tables_out"), 16)

            def low_parts(t):
                for q in range(4):
                    pool.wait_ge(sem("h_ready"), t.times(4, q + 1))
                    pool.tensor_tensor(
                        WL[:, 4 * q:4 * q + 4, :], RAW[:, t.odd, 512 * q:512 * q + 512].rearrange("p (k c) -> p k c", k=4),
                        WH[:, 4 * q:4 * q + 4, :].bitcast(F32), ALU.subtract).then_inc(sem("l_ready"), 1)

            def add_residual(loaded, n):
                loaded = loaded if isinstance(loaded, int) else pool.to_reg(loaded)
                pool.wait_ge(sem("x0_loaded"), 16)
                pool.wait_ge(sem("h_loaded"), loaded)
                with pool.Fori(0, KT // 2) as i:
                    for s in range(2):
                        pool.wait_ge(sem("tile_scaled"), i * 2 + n + s + 1)
                        m = i * 2 + s
                        pool.tensor_tensor(W[:, m, :], W[:, m, :], MIX[:, m, :], ALU.add).then_inc(sem("h_new"), 1)

            with pool.Fori(0, T_PG // 2) as i:
                for o in range(2):
                    low_parts(Tile(o, (2, i)))
            low_parts(Tile(T_PG))
            add_residual(64, 0)
            with pool.Fori(0, (T_L2 - T_PG) // 2) as i:
                for o in range(2):
                    low_parts(Tile(T_PG + 1 + o, (2, i)))
            add_residual(64, 16)
            with pool.Fori(0, LAYERS) as l:
                with pool.Fori(0, PER_LAYER // 2) as i:
                    for o in range(2):
                        low_parts(Tile(T_L2 + 1 + o, (PER_LAYER, l), (2, i)))
                add_residual(l * 64 + 128, l * 16 + 32)

        @block.tensor
        def _(pe):
            def quarter(t, q, gen=None):
                bank = Z[t.odd]
                if q == 0:
                    if t.c in (T_HGG, T_HGG + 1) and not t.terms:
                        pe.wait_ge(sem("e_out"), 16)
                    else:
                        pe.wait_ge(sem("z_free"), t.times(1, -T_HGG - 1))
                pe.wait_ge(sem("l_ready"), t.times(4, q + 1))
                for k in range(4 * q, 4 * q + 4):
                    if gen is not None:
                        pe.wait_ge(sem("u_ready"), gen * 16 + k + 1)
                    for n, (w, u) in enumerate(((WH, UH), (WH, UL), (WL, UH))):
                        mm = pe.matmul(bank[:], w[:, k, :], u[:, k, :], start=(k == 0 and n == 0),
                                       stop=(k == KT - 1 and n == 2))
                mm.then_inc(sem("w_free"), 1)

            def sum_rows(src, bank, wait, done):
                pe.wait_ge(*wait)
                pe.matmul(bank[:], ONES[:], src, start=True, stop=True).then_inc(sem(done), 1)

            def turn_v(src, wait, done):
                pe.wait_ge(*wait)
                for c in range(4):
                    mm = pe.transpose(TP[0][:, c * P:(c + 1) * P], src[:, c * P:(c + 1) * P], IDN[:])
                mm.then_inc(sem(done), 1)

            def hg_work(j, p):
                def level(n):
                    pe.wait_ge(sem("qk_ready"), j * 9 + max(n, 1))
                    if 1 <= n <= 7:
                        pe.wait_ge(sem("km_ready"), j * 7 + n)
                    if n < 2:
                        pe.wait_ge(sem("lv_free"), PRIMED + j * 10)
                    elif n < 9:
                        pe.wait_ge(sem("lv_free"), PRIMED + j * 10 + n - 1)
                    if n <= 8:
                        bank = SC[n % 2]
                        for c in range(4):
                            if n == 0:
                                kk, qq = row(KS)[:, c * P:(c + 1) * P], row(Q)[:, c * P:(c + 1) * P]
                            elif n < 8:
                                h = 1 << (n - 1)
                                kk = row(KM)[:, c * P:(c + 1) * P]
                                qq = view(QB, c * P, [[2 * h, P // (2 * h)], [2 * S + h, 2], [1, h]])
                            else:
                                kk = row(KB if c % 2 else KF)[:, c * P:(c + 1) * P]
                                o = c ^ 1
                                qq = row(QF if o % 2 else QB)[:, o * P:(o + 1) * P]
                            mm = pe.matmul(bank[:, c * P:(c + 1) * P], kk, qq, start=True, stop=True)
                    else:
                        pe.wait_ge(sem("hvn_ready"), j + 1)
                        pe.wait_ge(sem("hro_ready"), PRIMED + j)
                        for c in range(4):
                            bank = TP[c // 2]
                            kk = row(KF if c < 2 else KB)[:, c * P:(c + 1) * P]
                            qq = row(QF)[:, 256:512] if c < 2 else row(QB)[:, 0:256]
                            mm = pe.matmul(bank[:, (c % 2) * 256:(c % 2) * 256 + 256], kk, qq, start=True, stop=True)
                    mm.then_inc(sem("lv_done"), 1)

                if p == 1:
                    turn_v(row(VT), (sem("qk_ready"), j * 9 + 1), "hv_turned")
                if p in LEVEL_AT:
                    level(LEVEL_AT[p])
                if p == 13:
                    pe.wait_ge(sem("lv_free"), PRIMED + j * 10 + 10)
                    pe.wait_ge(sem("hg_done"), PRIMED + j)
                    for c in range(4):
                        mm = pe.matmul(OB[:], row(HVN)[:, c * P:(c + 1) * P], row(AT + c), start=(c == 0), stop=(c == 3))
                    mm.then_inc(sem("hav_done"), 1)
                if p == 14:
                    sum_rows(row(HSQ), TP[1], (sem("hsq_ready"), j + 1), "hss_done")

            def att_work(j, p):
                a = p // 4
                if p == 0:
                    pe.wait_ge(sem("pte0"), PRIMED + j * 4)
                    turn_v(row(VTA), (sem("qt_ready"), j + 1), "v_turned")
                if p % 4 == 0:
                    for hd in range(2):
                        u = 2 * a + hd
                        pe.wait_ge(sem("sm_done"), PRIMED + j * 8 + max(u - 1, 0))
                        o = 64 * hd
                        pe.matmul(SC[hd][:], row(QT)[o:o + 64, a * P:(a + 1) * P], row(KTR)[o:o + 64, :],
                                  start=True, stop=True).then_inc(sem("s_done"), 1)
                if p % 4 == 2:
                    for hd in range(2):
                        pe.wait_ge(sem("p_ready"), j * 8 + 2 * a + hd + 1)
                        if hd == 0 and a == 0:
                            pe.wait_ge(sem("vn_ready"), j + 1)
                        pe.wait_ge(sem(f"pte{hd}"), PRIMED + j * 4 + a)
                        for c in range(4):
                            mm = pe.transpose(TP[hd][:, c * P:(c + 1) * P], row(PRB + hd)[:, c * P:(c + 1) * P], IDN[:])
                        mm.then_inc(sem("pt_done"), 1)
                if p % 4 == 3:
                    if a == 0:
                        pe.wait_ge(sem("att_done"), PRIMED + j)
                    for hd in range(2):
                        pe.wait_ge(sem(f"pte{hd}"), PRIMED + j * 4 + a + 1)
                        for c in range(4):
                            mm = pe.matmul(OB[64 * hd:64 * hd + 64, a * P:(a + 1) * P],
                                           row(VN)[:, c * P + 64 * hd:c * P + 64 * hd + 64],
                                           row(PT + hd)[:, c * P:(c + 1) * P], start=(c == 0), stop=(c == 3))
                    mm.then_inc(sem("av_done"), 1)

            def ret_work(j, p, b):
                if p == 1:
                    pe.wait_ge(sem("gate_read"), PRIMED + j * 2)
                if p == 0:
                    turn_v(row(VTA), (sem("rqt_ready"), j + 1), "rv_turned")
                if 1 <= p <= 4:
                    c = p - 1
                    pe.wait_ge(sem("ra_ready"), PRIMED + j * 4 + max(c - 1, 0))
                    pe.matmul(SC[c % 2][:, 0:S - c * P], row(KTR)[:, c * P:(c + 1) * P], row(QT)[:, c * P:S],
                              start=True, stop=True).then_inc(sem("rs_done"), 1)
                if p == 6:
                    pe.wait_ge(sem("ra_ready"), PRIMED + j * 4 + 4)
                    pe.wait_ge(sem("rvn_ready"), j + 1)
                    pe.wait_ge(sem("ret_done"), PRIMED + j)
                    for c in range(4):
                        mm = pe.matmul(OB[:, c * P:S], row(VN)[:, c * P:(c + 1) * P], view(0, RA[c], [[1, S - c * P]]),
                                       start=(c == 0), stop=(c == 3), skip_group_check=True)
                    mm.then_inc(sem("rav_done"), 1)
                if p == 8:
                    sum_rows(row(NRO), TP[1], (sem("rsq_ready"), j + 1), "rss_done")
                if p == 9:
                    pe.wait_ge(sem("ra_ready"), PRIMED + j * 4 + 4)
                    for g in range(2):
                        use = [n for n, (x, y) in enumerate(LRU_PAIRS) if y == b]
                        for n in use:
                            mm = pe.matmul(SC[g][:], view(GW, (g * NG + n) * P, [[1, P]]), row(XC + LRU_PAIRS[n][0]),
                                           start=(n == use[0]), stop=(n == use[-1]))
                        mm.then_inc(sem("gate_done"), 1)

            def dif_work(j, p):
                if p == 0:
                    pe.wait_ge(sem("dpte"), PRIMED + j * 4)
                    turn_v(row(VTA), (sem("dqt_ready"), j + 1), "dv_turned")
                if p in DIF_VALUES:
                    a = DIF_VALUES[p]
                    if a == 0:
                        pe.wait_ge(sem("dif_done"), PRIMED + j)
                    pe.wait_ge(sem("dpte"), PRIMED + j * 4 + a + 1)
                    for c in range(a + 1):
                        mm = pe.matmul(OB[:, a * P:(a + 1) * P], row(VN)[:, c * P:(c + 1) * P],
                                       row(PT)[:, c * P:(c + 1) * P], start=(c == 0), stop=(c == a))
                    mm.then_inc(sem("dav_done"), 1)
                if p in DIF_TURN:
                    a = DIF_TURN[p]
                    pe.wait_ge(sem("dp_ready"), j * 4 + a + 1)
                    if a == 0:
                        pe.wait_ge(sem("dvn_ready"), j + 1)
                    pe.wait_ge(sem("dpte"), PRIMED + j * 4 + a)
                    for c in range(a + 1):
                        mm = pe.transpose(TP[0][:, c * P:(c + 1) * P], row(PRB)[:, c * P:(c + 1) * P], IDN[:])
                    mm.then_inc(sem("dpt_done"), 1)
                if p in DIF_SCORES:
                    a = DIF_SCORES[p]
                    for hd in range(2):
                        u = 2 * a + hd
                        pe.wait_ge(sem("dsm_done"), PRIMED + j * 8 + max(u - 1, 0))
                        o, w = 64 * hd, (a + 1) * P
                        pe.matmul(SC[hd][:, 0:w], row(QT)[o:o + 64, a * P:(a + 1) * P], row(KTR)[o:o + 64, 0:w],
                                  start=True, stop=True).then_inc(sem("ds_done"), 1)
                if p == 15:
                    sum_rows(row(NRO), TP[1], (sem("dsq_ready"), j + 1), "dss_done")

            WORK = {"hg": hg_work, "att": att_work, "ret": ret_work, "dif": dif_work}

            def step(t, work=None, j=None, **kw):
                for p in range(16):
                    s, q = divmod(p, 4)
                    if t is not None:
                        quarter(t.plus(s), q)
                    if work is not None:
                        WORK[work](j, p, **kw)

            def slots(t, n, gen=None):
                for s in range(2):
                    for q in range(4):
                        quarter(t.plus(s), q, gen if s == 0 else None)
                with pe.Fori(1, n // 2) as i:
                    for s in range(2):
                        for q in range(4):
                            quarter(Tile(t.c + s, *t.terms, (2, i)), q)

            pe.wait_ge(sem("p_split"), 2)
            for m in range(KT):
                t, n = divmod(m, 8)
                if n % 2 == 0:
                    pe.wait_ge(sem("l_ready"), 4 * t + n // 2 + 1)
                if m >= 2:
                    pe.wait_ge(sem("e_out"), m - 1)
                for k in range(2):
                    for i, (w, u) in enumerate(((WH, PH), (WH, PL), (WL, PH))):
                        mm = pe.matmul(Z[m % 2][:], w[:, 2 * n + k, :], u[:, k, :], start=(k == 0 and i == 0),
                                       stop=(k == 1 and i == 2))
                mm.then_inc(sem("w_free") if n % 2 else sem("e_even"), 1)

            for s in range(2):
                for q in range(4):
                    quarter(Tile(T_HGG + s), q, 0 if s == 0 else None)
            pe.wait_ge(sem("consts"), 16)
            pe.wait_ge(sem("ones_set"), 1)
            sum_rows(row(ACC), OB, (sem("sq_used"), PRIMED + 16), "ss_done")
            with pe.Fori(1, 4) as i:
                for s in range(2):
                    for q in range(4):
                        quarter(Tile(T_HGG + s, (2, i)), q)
            step(Tile(T_HG))
            with pe.Fori(1, HG_HEADS) as i:
                step(Tile(T_HG, (4, i)), work="hg", j=i - 1)
            step(Tile(T_ATT), work="hg", j=HG_HEADS - 1)
            pe.wait_ge(sem("hg_done"), PRIMED + HG_HEADS)
            with pe.Fori(1, PAIRS) as i:
                step(Tile(T_ATT, (4, i)), work="att", j=i - 1)
            step(None, work="att", j=PAIRS - 1)
            slots(Tile(T_OUT), 16, gen=1)
            sum_rows(row(ACC), OB, (sem("sq_used"), PRIMED + 32), "ss_done")
            slots(Tile(T_PG), 16, gen=2)
            sum_rows(row(ACC), OB, (sem("sq_used"), PRIMED + 48), "ss_done")

            with pe.Fori(0, LAYERS) as l:
                base = l * PER_LAYER
                for m in range(LRU_TILES):
                    for q in range(4):
                        quarter(Tile(T_L2 + R_LX + m, (PER_LAYER, l)), q, l * 2 + 3 if m == 0 else None)
                    if m == 1:
                        sum_rows(row(ACC), OB, (sem("sq_used"), PRIMED + l * 32 + 64), "ss_done")
                step(Tile(T_L2 + R_RET, (PER_LAYER, l)))
                for h in range(1, RET_HEADS + 1):
                    if h == 1:
                        gws = pe.to_reg(l * 16 + 16)
                        xcs = pe.to_reg(l * 6 + 6)
                        pe.wait_ge(sem("gw_loaded"), gws)
                        pe.wait_ge(sem("xc_ready"), xcs)
                    step(Tile(T_L2 + R_RET + 4 * h, (PER_LAYER, l)), work="ret",
                         j=l * RET_HEADS + h - 1, b=h - 1)
                pe.wait_ge(sem("gate_read"), PRIMED + l * 12 + 12)
                rets = pe.to_reg(l * RET_HEADS + (RET_HEADS + PRIMED))
                pe.wait_ge(sem("ones_set"), 1)
                pe.wait_ge(sem("ret_done"), rets)
                with pe.Fori(1, DIF_HEADS) as i:
                    step(Tile(T_L2 + R_DIF, (PER_LAYER, l), (4, i)),
                         work="dif", j=l * DIF_HEADS + i - 1)
                step(Tile(T_L2 + R_LG, (PER_LAYER, l)), work="dif", j=l * DIF_HEADS + DIF_HEADS - 1)
                for m in range(4, LRU_TILES):
                    for q in range(4):
                        quarter(Tile(T_L2 + R_LG + m, (PER_LAYER, l)), q)
                slots(Tile(T_L2 + R_OUT, (PER_LAYER, l)), 16, gen=l * 2 + 4)
                sum_rows(row(ACC), OB, (sem("sq_used"), PRIMED + l * 32 + 80), "ss_done")

        @block.scalar
        def _(act):
            def high(t, q):
                n = t.plus(1)
                act.wait_ge(sem("w_raw1" if n.odd else "w_raw0"), n.pair() * 16 + 16)
                act.wait_ge(sem("w_free"), t.times(4, q + 1))
                act.activation(WH[:, 4 * q:4 * q + 4, :],
                               RAW[:, n.odd, 512 * q:512 * q + 512].rearrange("p (k c) -> p k c", k=4),
                               ACT.Copy).then_inc(sem("h_ready"), 1)

            def copy(dst, src, done=None, **kw):
                i = act.activation(dst, src, ACT.Copy, **kw)
                if done:
                    i.then_inc(sem(done), 1)

            def inv_root(bank, dst, width, wait, done):
                act.wait_ge(*wait)
                act.activation(dst, bank[:], ACT.Ln, bias=CS[:, C_EPS:C_EPS + 1], scale=1.0 / width)
                act.drain()
                act.activation(dst, dst, ACT.Exp, scale=-0.5).then_inc(sem(done), 1)

            def gate_exp(t, src=RW, dst=TM, done="gexp"):
                act.wait_ge(sem("z_free"), t.times(1, -T_HGG + 1))
                act.activation(row(dst), row(src), ACT.Exp, scale=-1.0).then_inc(sem(done), 1)

            def hg_work(j, p):
                if p == 1:
                    act.wait_ge(sem("hav_done"), PRIMED + j)
                    act.wait_ge(sem("hv_turned"), j + 1)
                    copy(row(HVN), TP[0][:], "hvn_ready")
                    act.wait_ge(sem("lv_done"), j * 10 + 1)
                    copy(view(AT, 0, [[S + P, 4], [1, P]]), SC[0][:].rearrange("p (c t) -> p c t", c=4), "lv_free")
                n = LEVEL_AT.get(p, -1) + 1
                if 1 <= n <= 7:
                    h = 1 << (n - 1)
                    act.wait_ge(sem("qk_ready"), j * 9 + n)
                    copy(view(KM, 0, [[2 * h, S // (2 * h)], [h, 2], [1, h]]),
                         view(KF, 0, [[2 * h, S // (2 * h)], [2 * S + h, 2], [1, h]]), "km_ready")
                if n == 9:
                    act.wait_ge(sem("lv_done"), j * 10 + 9)
                    act.wait_ge(sem("lv_free"), PRIMED + j * 10 + 8)
                    copy(view(AT, P, [[2 * S + 2 * P, 2], [S - P, 2], [1, P]]),
                         SC[0][:].rearrange("p (a b t) -> p a b t", a=2, b=2), "lv_free")
                if n == 10:
                    act.wait_ge(sem("lv_done"), j * 10 + 10)
                    copy(view(AT, 256, [[S, 2], [1, 256]]), TP[0][:].rearrange("p (a t) -> p a t", a=2))
                    copy(view(AT + 2, 0, [[S, 2], [1, 256]]), TP[1][:].rearrange("p (a t) -> p a t", a=2), "lv_free")
                if p == 13:
                    act.wait_ge(sem("hav_done"), PRIMED + j + 1)
                    act.activation(row(HSQ), OB[:], ACT.Square).then_inc(sem("hsq_ready"), 1)
                if p == 14:
                    act.wait_ge(sem("hg_done"), PRIMED + j)
                    inv_root(TP[1], row(HRO), P, (sem("hss_done"), j + 1), "hro_ready")

            def att_work(j, p):
                a = p // 4
                if p == 0:
                    act.wait_ge(sem("av_done"), PRIMED + j * 4)
                    act.wait_ge(sem("v_turned"), j + 1)
                    copy(row(VN), TP[0][:], "vn_ready")
                if p % 4 == 1:
                    for hd in range(2):
                        u = 2 * a + hd
                        act.wait_ge(sem("sm_done"), PRIMED + j * 8 + u + 1)
                        act.wait_ge(sem("pt_done"), PRIMED + j * 8 + max(u - 1, 0))
                        act.activation(row(PRB + hd), row(SMR + hd), ACT.Exp, bias=SM[:, hd:hd + 1], scale=-1.0,
                                       accum_out=SM[:, 2 + hd:3 + hd]).then_inc(sem("exp_done"), 1)
                if p % 4 == 2:
                    act.wait_ge(sem("pt_done"), PRIMED + j * 8 + 2 * a + 1)
                    act.wait_ge(sem("av_done"), PRIMED + j * 4 + a)
                    copy(row(PT), TP[0][:], "pte0")

            def ret_work(j, p, load=None, b=None, cl=None):
                if p == 9:
                    if cl is not None:
                        act.wait_ge(sem("cl_ready"), cl)
                    for g in range(2):
                        act.wait_ge(sem("gate_done"), j * 2 + g + 1)
                        act.wait_ge(sem("scan_done"), PRIMED + j)
                        act.activation(row(LR + g), SC[g][:], ACT.Exp, bias=SM[:, 32 + 6 * g + b:33 + 6 * g + b],
                                       scale=-1.0).then_inc(sem("gate_read"), 1)
                if p == 10:
                    act.wait_ge(sem("r_ready"), j + 1)
                    act.activation(row(LA), row(LR), ACT.Exp, scale=SM[:, 44 + b:45 + b]).then_inc(sem("a_ready"), 1)
                    act.activation(MIX[:, 10 + b, :], row(LR), ACT.Exp, scale=SM[:, 50 + b:51 + b]).then_inc(sem("a_ready"), 1)
                if p == 13:
                    act.wait_ge(sem("m2_ready"), j + 1)
                    act.activation(MIX[:, 10 + b, :], MIX[:, 10 + b, :], ACT.Ln)
                    act.drain()
                    act.activation(MIX[:, 10 + b, :], MIX[:, 10 + b, :], ACT.Exp, scale=0.5).then_inc(sem("mult_ready"), 1)
                if p == 0:
                    act.wait_ge(sem("rav_done"), PRIMED + j)
                    act.wait_ge(sem("rv_turned"), j + 1)
                    copy(row(VN), TP[0][:], "rvn_ready")
                if p == 5 and load is not None:
                    act.wait_ge(sem("ra_ready"), PRIMED + j * 4 + 4)
                    act.dma_start(row(DEC), dec[load]).then_inc(sem("dec_loaded"), 16)
                if p == 6:
                    act.wait_ge(sem("ret_done"), PRIMED + j)
                    act.wait_ge(sem("rav_done"), PRIMED + j + 1)
                    act.activation(row(NRO), OB[:], ACT.Square).then_inc(sem("rsq_ready"), 1)
                if p == 8:
                    inv_root(TP[1], row(NRO), P, (sem("rss_done"), j + 1), "rro_ready")

            def dif_work(j, p):
                if p == 0:
                    act.wait_ge(sem("dav_done"), PRIMED + j * 4)
                    act.wait_ge(sem("dv_turned"), j + 1)
                    copy(row(VN), TP[0][:], "dvn_ready")
                if p in DIF_SOFTMAX:
                    a = DIF_SOFTMAX[p]
                    w = (a + 1) * P
                    for hd in range(2):
                        u = 2 * a + hd
                        act.wait_ge(sem("dsm_done"), PRIMED + j * 8 + u + 1)
                        act.wait_ge(sem("dpt_done"), PRIMED + j * 4 + a)
                        act.activation(row(PRB + hd)[:, 0:w], row(SMR + hd)[:, 0:w], ACT.Exp, bias=SM[:, hd:hd + 1],
                                       scale=-1.0, accum_out=SM[:, 2 + hd:3 + hd]).then_inc(sem("dexp_done"), 1)
                if p in DIF_TURN:
                    a = DIF_TURN[p]
                    w = (a + 1) * P
                    act.wait_ge(sem("dpt_done"), PRIMED + j * 4 + a + 1)
                    act.wait_ge(sem("dav_done"), PRIMED + j * 4 + a)
                    copy(row(PT)[:, 0:w], TP[0][:, 0:w], "dpte")
                if p == 15:
                    act.wait_ge(sem("dif_done"), PRIMED + j)
                    act.wait_ge(sem("dav_done"), PRIMED + j * 4 + 4)
                    act.activation(row(NRO), OB[:], ACT.Square).then_inc(sem("dsq_ready"), 1)
                    inv_root(TP[1], row(NRO), P, (sem("dss_done"), j + 1), "dro_ready")

            WORK = {"hg": hg_work, "att": att_work, "ret": ret_work, "dif": dif_work}

            def step(t, gate=False, gates=False, hg=False, work=None, j=None, **kw):
                for p in range(16):
                    s, q = divmod(p, 4)
                    if t is not None:
                        high(t.plus(s), q)
                    if hg and p in (3, 7, 11):
                        gate_exp(t.plus(s), SG, SE, "sg_exp")
                    if work is not None:
                        WORK[work](j, p, **kw)
                    if (gate and p == 15) or (gates and q == 3):
                        gate_exp(t.plus(s))

            def operand(t, src, scale=None, new=None):
                act.wait_ge(sem("w_free"), t.times(4))
                for q, (a, b) in enumerate(((0, 8), (8, 12), (12, 14), (14, 16))):
                    with act.Fori(a, b) as m:
                        if new is not None:
                            act.wait_ge(sem("h_new"), m + 1 + new)
                        if scale is None:
                            act.activation(UH[:, m, :], src[:, m, :], ACT.Copy).then_inc(sem("uh_ready"), 1)
                        else:
                            act.activation(UH[:, m, :], src[:, m, :], ACT.Copy,
                                           scale=scale[:, bass.ds(m, 1)]).then_inc(sem("uh_ready"), 1)
                    high(t, q)

            def squares(t, n):
                for m in range(KT):
                    act.wait_ge(sem("sq_used"), PRIMED + n + max(m - 1, 0))
                    act.activation(row(SQ0 + m % 2), row(H + m), ACT.Square).then_inc(sem("sq_ready"), 1)
                    if m % 4 == 3:
                        high(t, m // 4)

            def out_slots(t, n, gain, ss, root):
                def one(tt, m, s, used, first=False):
                    for q in range(4):
                        if not first:
                            high(tt, q)
                    act.wait_ge(sem("w_free"), tt.times(4, 4))
                    act.wait_ge(sem("sq_used"), PRIMED + used)
                    act.activation(row(SQ0 + s), Z[s][:], ACT.Square).then_inc(sem("sq_ready"), 1)
                    copy(MIX[:, m, :], Z[s][:], "z_free", scale=gain[:, bass.ds(m, 1)])

                for s in range(2):
                    one(t.plus(s), s, s, n, s == 0)
                with act.Fori(1, KT // 2) as i:
                    for s in range(2):
                        one(Tile(t.c + s, *t.terms, (2, i)), i * 2 + s, s, i * 2 + n + s - 1)
                inv_root(OB, row(ACC), D, (sem("ss_done"), ss), root)

            def load_h(src, done):
                for g in range(4):
                    act.dma_start(W[:, H + 4 * g:H + 4 * g + 4, :], src[4 * g:4 * g + 4].rearrange("m p t -> p m t")
                                  ).then_inc(sem(done), 16)

            def store_h(wait):
                for g in range(4):
                    act.wait_ge(sem("h_new"), wait + 4 * g + 4)
                    act.dma_start(out[4 * g:4 * g + 4].rearrange("m p t -> p m t"), W[:, H + 4 * g:H + 4 * g + 4, :]
                                  ).then_inc(sem("h_stored"), 16)

            act.dma_start(MIX[:, 14:16, :], pT.rearrange("k p t -> p k t")).then_inc(sem("p_loaded"), 16)
            act.dma_start(PR1[:], par1).then_inc(sem("cs_loaded"), 16)
            act.dma_start(CS[:], cst).then_inc(sem("cs_loaded"), 16)
            for g in range(4):
                act.dma_start(W[:, H + 4 * g:H + 4 * g + 4, :], xT[4 * g:4 * g + 4].rearrange("m p t -> p m t")
                              ).then_inc(sem(f"x{g}_loaded"), 16)
            act.preload_act_table_set("natural_log_exp_and_others")
            act.wait_ge(sem("p_loaded"), 16)
            for k in range(2):
                copy(PH[:, k, :], MIX[:, 14 + k, :], "ph_ready")
            for q in range(4):
                act.wait_ge(sem("w_raw0"), 16)
                act.activation(WH[:, 4 * q:4 * q + 4, :], RAW[:, 0, 512 * q:512 * q + 512].rearrange("p (k c) -> p k c", k=4),
                               ACT.Copy).then_inc(sem("h_ready"), 1)
            act.dma_start(MIX[:, 0, :].bitcast(I32), pos1.to_broadcast([P, S])).then_inc(sem("pos_loaded"), 16)
            act.dma_start(MIX[:, 1, :].bitcast(I32), pos2.to_broadcast([P, S])).then_inc(sem("pos_loaded"), 16)
            act.dma_start(IDN[:], idn).then_inc(sem("consts"), 16)
            act.dma_start(MIX[:, 6:8, :].rearrange("p a b -> p (a b)"), masks.rearrange("p n t -> p (n t)")
                          ).then_inc(sem("masks_loaded"), 16)
            act.wait_ge(sem("cs_loaded"), 32)
            for m in range(KT):
                if m % 2 == 0:
                    act.wait_ge(sem("e_even"), m // 2 + 1)
                else:
                    act.wait_ge(sem("w_free"), m // 2 + 1)
                copy(row(E + m), Z[m % 2][:], "e_out")
                if m % 2:
                    high(Tile(m // 8), (m // 2) % 4)
                act.wait_ge(sem(f"x{m // 4}_loaded"), 16)
                copy(UH[:, m, :], row(H + m), "uh_ready", scale=PR1[:, G_PRE + m:G_PRE + m + 1])
            act.wait_ge(sem("e_out"), 16)
            act.dma_start(e_dram.rearrange("m p t -> p m t"), W[:, E:E + 16, :]).then_inc(sem("e_stored"), 16)
            act.wait_ge(sem("lb_diff"), 1)
            act.activation(SM[:, 16:32], SM[:, 0:16], ACT.Exp).then_inc(sem("lb_exp"), 1)
            for q in range(4):
                high(Tile(T_HGG), q)
            squares(Tile(T_HGG + 1), 0)
            inv_root(OB, row(RSTD), D, (sem("ss_done"), 1), "rstd_ready")
            for s in range(2):
                gate_exp(Tile(T_HGG + s))
            with act.Fori(1, 4) as i:
                for s in range(2):
                    for q in range(4):
                        high(Tile(T_HGG + s, (2, i)), q)
                    gate_exp(Tile(T_HGG + s, (2, i)))
                    if s == 1:
                        continue
                    act.wait_ge(sem("angle_ready"), i * 2)
                    for r in (COS, SIN):
                        act.activation(row(r), row(r), ACT.Sin).then_inc(sem("table_ready"), 1)
                    act.preload_act_table_set("natural_log_exp_and_others")
                    act.wait_ge(sem("table_ready"), i * 2)
                    act.dma_start(tabs[bass.ds(i * 2 - 2, 2)].rearrange("n p t -> p n t"), row(COS, 2)).then_inc(sem("tables_out"), 16)
            act.wait_ge(sem("tables_out"), 64)
            act.dma_start(row(CT1), tabs[0]).then_inc(sem("tab1_loaded"), 16)
            act.dma_start(row(ST1), tabs[1]).then_inc(sem("tab1_loaded"), 16)
            act.dma_start(W[:, BIAS:BIAS + 4, :], bias).then_inc(sem("tab1_loaded"), 16)
            step(Tile(T_HG), hg=True)
            with act.Fori(1, HG_HEADS) as i:
                step(Tile(T_HG, (4, i)), hg=True, work="hg", j=i - 1)
            step(Tile(T_ATT), gate=True, work="hg", j=HG_HEADS - 1)
            act.wait_ge(sem("hg_done"), PRIMED + HG_HEADS)
            with act.Fori(1, PAIRS) as i:
                step(Tile(T_ATT, (4, i)), gate=True, work="att", j=i - 1)
            step(None, work="att", j=PAIRS - 1)
            act.wait_ge(sem("att_done"), PRIMED + PAIRS)
            load_h(xT, "h_loaded")
            act.dma_start(W[:, E:E + 16, :], e_dram.rearrange("m p t -> p m t")).then_inc(sem("e_loaded"), 16)
            operand(Tile(T_OUT), MIX[:])
            out_slots(Tile(T_OUT), 16, PR1[:, G_POST:G_POST + 16], 2, "root_ready")
            operand(Tile(T_PG), W[:, H:H + 16, :], new=0)

            def pg_slot(t, m, s, cnt):
                for q in range(4):
                    if t.terms or t.c != T_PG:
                        high(t, q)
                act.wait_ge(sem("sq_used"), PRIMED + cnt)
                act.wait_ge(sem("w_free"), t.times(4, 4))
                act.activation(row(SQ0 + s), Z[s][:], ACT.Exp, scale=-1.0).then_inc(sem("z_free"), 1)

            def pg_square(m, s, cnt):
                act.wait_ge(sem("pg_prod"), cnt)
                act.activation(row(SQ0 + s), MIX[:, m, :], ACT.Square).then_inc(sem("sq_ready"), 1)
                act.drain()
                copy(MIX[:, m, :], MIX[:, m, :], scale=PR1[:, G_PLE:G_PLE + 16][:, bass.ds(m, 1)])

            for s in range(2):
                pg_slot(Tile(T_PG + s), s, s, 32)
                pg_square(s, s, s + 1)
            with act.Fori(1, KT // 2) as i:
                for s in range(2):
                    pg_slot(Tile(T_PG + s, (2, i)), i * 2 + s, s, i * 2 + 32 + s - 1)
                    pg_square(i * 2 + s, s, i * 2 + s + 1)
            inv_root(OB, row(ACC), D, (sem("ss_done"), 3), "root_ready")

            with act.Fori(0, LAYERS) as l:
                act.wait_ge(sem("par_used"), PRIMED + l)
                act.dma_start(PR2[:], par2[l]).then_inc(sem("par_loaded"), 16)
                act.dma_start(DL[:].rearrange("p a b -> p (a b)"), dlam[l].to_broadcast([P, 256])).then_inc(sem("par_loaded"), 16)
                act.wait_ge(sem("par_loaded"), l * 32 + 32)
                operand(Tile(T_L2, (PER_LAYER, l)), W[:, H:H + 16, :], PR2[:, G2_PRE:G2_PRE + 16], l * 16 + 16)
                act.wait_ge(sem("h_new"), l * 16 + 32)
                for g in range(4):
                    act.dma_start(out[4 * g:4 * g + 4].rearrange("m p t -> p m t"), W[:, H + 4 * g:H + 4 * g + 4, :]
                                  ).then_inc(sem("h_stored"), 16)
                squares(Tile(T_L2 + 1, (PER_LAYER, l)), l * 32 + 48)
                act.dma_start(row(CTR), tabs[2]).then_inc(sem("tab2_loaded"), 16)
                act.dma_start(row(STR), tabs[3]).then_inc(sem("tab2_loaded"), 16)
                act.dma_start(row(CTD), tabs[4]).then_inc(sem("tab2_loaded"), 16)
                for n in range(2):
                    act.wait_ge(sem("lam_dot"), l + 1)
                    act.activation(SM[:, 10 + n:11 + n], SM[:, 8 + n:9 + n], ACT.Exp).then_inc(sem("lam_exp"), 1)
                act.wait_ge(sem("lam_abs"), l + 1)
                act.activation(SM[:, 18:24], SM[:, 12:18], ACT.Exp, scale=-1.0).then_inc(sem("lam_e"), 1)

                inv_root(OB, row(RSTD), D, (sem("ss_done"), l * 2 + 4), "rstd_ready")
                for m in range(2, LRU_TILES):
                    for q in range(4):
                        high(Tile(T_L2 + R_LX + m, (PER_LAYER, l)), q)
                act.wait_ge(sem("h_stored"), l * 64 + 64)
                act.dma_start(row(STD), tabs[5]).then_inc(sem("tab3_loaded"), 16)
                act.dma_start(row(CM), cmask).then_inc(sem("tab3_loaded"), 16)
                act.dma_start(row(DEC), dec[0]).then_inc(sem("dec_loaded"), 16)
                act.dma_start(W[:, GW:GW + 7, :], gw[l].rearrange("p (r t) -> p r t", r=7)).then_inc(sem("gw_loaded"), 16)
                step(Tile(T_L2 + R_RET, (PER_LAYER, l)), gate=True)
                for h in range(1, RET_HEADS + 1):
                    step(Tile(T_L2 + R_RET + 4 * h, (PER_LAYER, l)), gate=True, work="ret", j=l * RET_HEADS + h - 1,
                         load=h if h < RET_HEADS else None, b=h - 1, cl=l + 1 if h == 1 else None)
                act.wait_ge(sem("ret_done"), PRIMED + l * RET_HEADS + RET_HEADS)
                act.wait_ge(sem("scan_done"), PRIMED + l * LRU_TILES + LRU_TILES)
                with act.Fori(1, DIF_HEADS) as i:
                    step(Tile(T_L2 + R_DIF, (PER_LAYER, l), (4, i)), gate=True, work="dif",
                         j=l * DIF_HEADS + i - 1)
                step(Tile(T_L2 + R_LG, (PER_LAYER, l)), gates=True, work="dif", j=l * DIF_HEADS + DIF_HEADS - 1)
                act.wait_ge(sem("dif_done"), PRIMED + l * DIF_HEADS + DIF_HEADS)
                act.wait_ge(sem("h_stored"), l * 64 + 64)
                load_h(out, "h_loaded")
                for m in range(4, LRU_TILES):
                    t = Tile(T_L2 + R_LG + m, (PER_LAYER, l))
                    for q in range(4):
                        high(t, q)
                    gate_exp(t)
                act.wait_ge(sem("lru_done"), l * 6 + 6)
                operand(Tile(T_L2 + R_OUT, (PER_LAYER, l)), MIX[:])
                out_slots(Tile(T_L2 + R_OUT, (PER_LAYER, l)), l * 32 + 64, PR2[:, G2_POST:G2_POST + 16], l * 2 + 5, "root_ready")
            store_h(LAYERS * 16 + 16)
            act.wait_ge(sem("h_stored"), LAYERS * 64 + 64)

        @block.vector
        def _(v):
            def wait_apart(name, value):
                value = value if isinstance(value, int) else v.to_reg(value)
                v.wait_ge(sem("ones_set"), 1)
                v.wait_ge(sem(name), value)

            def rstd_mul(t, dst, done="z_free"):
                v.drain()
                v.wait_ge(sem("w_free"), t.times(4, 4))
                v.tensor_tensor(dst, Z[t.odd][:], row(RSTD), ALU.mult).then_inc(sem("z_free"), 1)

            def sigmoid_of(r):
                v.tensor_scalar(row(r), row(r), 1.0, None, ALU.add)
                v.drain()
                v.reciprocal(row(r), row(r))
                v.drain()

            def gate_tile(t, n, dst):
                rstd_mul(t, row(RW))
                v.wait_ge(sem("gexp"), n + 1)
                sigmoid_of(TM)
                v.tensor_tensor(dst, row(RW), row(TM), ALU.mult)
                v.drain()

            def rotated(t, dst, cos, sin, half, scale):
                z = Z[t.odd]
                v.drain()
                v.wait_ge(sem("w_free"), t.times(4, 4))
                v.scalar_tensor_tensor(out=row(dst), in0=z[:], scalar=scale, in1=row(cos), op0=ALU.mult, op1=ALU.mult)
                for o in range(0, P, half):
                    first = (o // half) % 2 == 0
                    x = o + half if first else o - half
                    i = v.scalar_tensor_tensor(out=row(TM)[o:o + half], in0=z[x:x + half, :], scalar=-scale if first else scale,
                                               in1=row(sin)[o:o + half], op0=ALU.mult, op1=ALU.mult)
                i.then_inc(sem("z_free"), 1)
                v.drain()
                v.tensor_tensor(row(dst), row(dst), row(TM), ALU.add)

            def take_heads(done):
                v.drain()
                v.tensor_copy(row(QT), row(QN))
                v.tensor_copy(row(KTR), row(KN)).then_inc(sem(done), 1)

            def hg_work(j, p):
                if p == 0:
                    v.tensor_scalar(row(KF), row(FF), -1.0, 1.0, ALU.mult, ALU.add)
                    v.tensor_scalar(row(KB), row(FB), -1.0, 1.0, ALU.mult, ALU.add)
                    v.tensor_tensor(view(QB, 0, [[2 * S, 2], [1, S]]), view(FB, 0, [[S, 2], [1, S]]),
                                    view(Q, 0, [[0, 2], [1, S]]), ALU.mult)
                    v.tensor_tensor(view(TT, 0, [[S, 2], [1, 256]]), view(FB, 0, [[S, 2], [2, 256]]),
                                    view(FB, 1, [[S, 2], [2, 256]]), ALU.mult)
                    v.drain()
                    v.tensor_tensor(row(KS), row(KF), row(KB), ALU.add).then_inc(sem("qk_ready"), 1)
                n = LEVEL_AT.get(p, 0)
                if 1 <= n <= 8:
                    h = 1 << (n - 1)
                    nb = S // (2 * h)
                    v.wait_ge(sem("lv_done"), j * 10 + n + 1)
                    tr, to = (FB, 0) if n == 1 else (TT, [0, 256, 384, 448, 480, 496, 504, 508][n - 2])
                    x = view(QF, h, [[-(S + h), 2], [2 * h, nb], [1, h]])
                    y = view(tr + 1, to, [[1, 2], [2, nb], [0, h]])
                    v.tensor_tensor(x, x, y, ALU.mult)
                    x = view(QB, 0, [[3 * S + h, 2], [2 * h, nb], [1, h]])
                    y = view(tr, to + 1, [[-1, 2], [2, nb], [0, h]])
                    v.tensor_tensor(x, x, y, ALU.mult).then_inc(sem("qk_ready"), 1)
                    if 2 <= n <= 7:
                        to2 = [0, 256, 384, 448, 480, 496, 504, 508][n - 1]
                        v.tensor_tensor(view(TT, to2, [[S, 2], [1, nb]]), view(TT, to, [[S, 2], [2, nb]]),
                                        view(TT, to + 1, [[S, 2], [2, nb]]), ALU.mult)
                    if n <= 7:
                        if n == 1:
                            wait_apart("lv_free", PRIMED + j * 10 + 1)
                        m = MSK[:, n, :]
                        mk = bass.AP(m.tensor, m.offset, [m.ap[0], [0, 4], [1, P]])
                        v.copy_predicated(view(AT, 0, [[S + P, 4], [1, P]]), mk,
                                          SC[n % 2][:].rearrange("p (c t) -> p c t", c=4)).then_inc(sem("lv_free"), 1)
                        v.drain()
                    else:
                        v.drain()
                if p == 15:
                    v.wait_ge(sem("hro_ready"), PRIMED + j + 1)
                    v.tensor_tensor(row(HTMP), OB[:], row(HRO), ALU.mult)
                    v.drain()
                    dst = MIX[:, j + 8, :]
                    v.scalar_tensor_tensor(out=dst, in0=row(HTMP), scalar=PR1[:, G_HG:G_HG + 1], in1=dst,
                                           op0=ALU.mult, op1=ALU.mult).then_inc(sem("hg_done"), 1)

            def att_work(j, p):
                a = p // 4
                if p % 4 == 0:
                    for hd in range(2):
                        u = 2 * a + hd
                        wait_apart("s_done", j * 8 + u + 1)
                        v.tensor_tensor_reduce(row(SMR + hd), SC[hd][:], row(BIAS + a), -1.0, 3.0e38, ALU.add, ALU.min,
                                               SM[:, hd:hd + 1]).then_inc(sem("sm_done"), 1)
                if p % 4 == 1:
                    v.wait_ge(sem("exp_done"), j * 8 + 2 * a + 2)
                    v.reciprocal(SM[:, 4:6], SM[:, 2:4])
                    v.drain()
                    for hd in range(2):
                        v.tensor_scalar(row(PRB + hd), row(PRB + hd), SM[:, 4 + hd:5 + hd], None,
                                        ALU.mult).then_inc(sem("p_ready"), 1)
                if p % 4 == 2:
                    v.wait_ge(sem("pt_done"), PRIMED + j * 8 + 2 * a + 2)
                    v.wait_ge(sem("av_done"), PRIMED + j * 4 + a)
                    v.tensor_copy(row(PT + 1), TP[1][:]).then_inc(sem("pte1"), 1)
                if p == 15:
                    v.wait_ge(sem("av_done"), PRIMED + j * 4 + 4)
                    v.tensor_tensor(MIX[:, j, :], OB[:], MIX[:, j, :], ALU.mult).then_inc(sem("att_done"), 1)

            def lru_work(j, p, b):
                I_, R_, TB, M2 = row(LI), row(LR), row(LTB), MIX[:, 10 + b, :]
                if p == 9:
                    v.wait_ge(sem("gate_read"), PRIMED + j * 2 + 2)
                    v.tensor_scalar(view(LR, 0, [[1, 2 * S]]), view(LR, 0, [[1, 2 * S]]), 1.0, None, ALU.add)
                    v.drain()
                    v.reciprocal(R_, R_).then_inc(sem("r_ready"), 1)
                    v.reciprocal(I_, I_)
                if p == 10:
                    v.tensor_tensor(I_, I_, row(XC + b), ALU.mult)
                    v.tensor_scalar(TB, R_, SM[:, 50 + b:51 + b], None, ALU.mult)
                if p == 11:
                    v.wait_ge(sem("a_ready"), j * 2 + 2)
                    v.tensor_scalar(R_, TB, -1.0 / 5040, None, ALU.mult)
                    for f in (720, 120, 24, 6, 2, 1):
                        v.drain()
                        v.scalar_tensor_tensor(out=R_, in0=R_, scalar=-1.0 / f, in1=TB, op0=ALU.add, op1=ALU.mult)
                if p == 12:
                    v.tensor_scalar(M2, M2, -1.0, 1.0, ALU.mult, ALU.add)
                    v.tensor_scalar(TB.bitcast(I32), TB, -0.25, None, ALU.is_gt)
                    v.drain()
                    v.copy_predicated(M2, TB.bitcast(I32), R_)
                    v.drain()
                    v.tensor_scalar(M2, M2, 1e-19, None, ALU.max).then_inc(sem("m2_ready"), 1)
                if p == 14:
                    v.wait_ge(sem("mult_ready"), j + 1)
                    v.tensor_tensor(I_, I_, M2, ALU.mult)
                    v.drain()
                    v.tensor_tensor_scan(M2, row(LA), I_, 0.0, ALU.mult, ALU.add).then_inc(sem("scan_done"), 1)

            def ret_work(j, p, m=None):
                lru_work(j, p, m)
                if 1 <= p <= 4:
                    c = p - 1
                    if c == 0:
                        v.wait_ge(sem("dec_loaded"), j * 16 + 16)
                    v.wait_ge(sem("rs_done"), j * 4 + c + 1)
                    v.tensor_tensor(view(0, RA[c], [[1, S - c * P]]), SC[c % 2][:, 0:S - c * P], row(DEC)[:, 0:S - c * P],
                                    ALU.mult).then_inc(sem("ra_ready"), 1)
                if p == 8:
                    v.wait_ge(sem("rro_ready"), j + 1)
                    v.tensor_tensor(row(NRO), OB[:], row(NRO), ALU.mult)
                    v.drain()
                    v.tensor_tensor(MIX[:, m, :], row(NRO), MIX[:, m, :], ALU.mult).then_inc(sem("ret_done"), 1)

            def dif_work(j, p, m=None):
                if p in DIF_SCORES:
                    a = DIF_SCORES[p]
                    w = (a + 1) * P
                    for hd in range(2):
                        wait_apart("ds_done", j * 8 + 2 * a + hd + 1)
                        v.tensor_tensor_reduce(row(SMR + hd)[:, 0:w], SC[hd][:, 0:w], row(CM)[:, S - w:S], -1.0, 3.0e38,
                                               ALU.add, ALU.min, SM[:, hd:hd + 1]).then_inc(sem("dsm_done"), 1)
                if p in DIF_SOFTMAX:
                    a = DIF_SOFTMAX[p]
                    w = (a + 1) * P
                    v.wait_ge(sem("dexp_done"), j * 8 + 2 * a + 2)
                    v.reciprocal(SM[:, 4:6], SM[:, 2:4])
                    v.drain()
                    v.tensor_tensor(SM[:, 6:7], SM[:, 5:6], SM[:, 60:61], ALU.mult)
                    v.tensor_scalar(row(PRB)[:, 0:w], row(PRB)[:, 0:w], SM[:, 4:5], None, ALU.mult)
                    v.drain()
                    v.scalar_tensor_tensor(out=row(PRB)[:, 0:w], in0=row(PRB + 1)[:, 0:w], scalar=SM[:, 6:7],
                                           in1=row(PRB)[:, 0:w], op0=ALU.mult, op1=ALU.add).then_inc(sem("dp_ready"), 1)
                if p == 15:
                    v.wait_ge(sem("dro_ready"), j + 1)
                    v.tensor_tensor(row(NRO), OB[:], row(NRO), ALU.mult)
                    v.drain()
                    v.scalar_tensor_tensor(out=MIX[:, m, :], in0=row(NRO), scalar=SM[:, 61:62], in1=MIX[:, m, :],
                                           op0=ALU.mult, op1=ALU.mult).then_inc(sem("dif_done"), 1)

            WORK = {"hg": hg_work, "att": att_work, "ret": ret_work, "dif": dif_work}

            def step(t, rot=None, scales=None, gate=None, hg=None, work=None, j=None, lru=None, take=None, **kw):
                for p in range(16):
                    s, q = divmod(p, 4)
                    if rot is not None:
                        if p in (3, 7):
                            rotated(t.plus(s), QN if p == 3 else KN, *rot, scales[s])
                        if p == 11:
                            rstd_mul(t.plus(2), row(VTA))
                    if hg is not None:
                        if p in (3, 7, 11):
                            rstd_mul(t.plus(s), row(SG))
                        if p == 15:
                            rstd_mul(t.plus(3), row(VT))
                    if lru is not None and q == 3:
                        lru_gate(t.plus(s), lru + s, s)
                    if work is not None:
                        v.drain()
                        WORK[work](j, p, **kw)
                    if hg is not None and p in (4, 8, 12):
                        v.wait_ge(sem("sg_exp"), hg * 3 + p // 4)
                        sigmoid_of(SE)
                        if p == 12:
                            v.tensor_tensor(row(Q), row(SG), row(SE), ALU.mult)
                        else:
                            d = 0 if p == 4 else 2
                            v.tensor_scalar(row(FF if p == 4 else FB), row(SE), LB[:, d + 1, :][:, hg_col(hg)],
                                            LB[:, d, :][:, hg_col(hg)], ALU.mult, ALU.add)
                    if take is not None and p == 13:
                        take_heads(take)
                    if gate is not None and p == 15:
                        gate_tile(t.plus(3), gate[0], MIX[:, gate[1], :])

            def hg_col(i):
                return bass.ds(i, 1)

            def lru_gate(t, n, b):
                gate_tile(t, n, row(RW))
                v.tensor_tensor(MIX[:, 10 + b, :], MIX[:, 10 + b, :], row(RW), ALU.mult).then_inc(sem("lru_done"), 1)

            def lru_conv(t, m):
                rstd_mul(t, row(QN))
                v.drain()
                cw = lambda n: PR2[:, CONV_W + 4 * m + n:CONV_W + 4 * m + n + 1]
                v.tensor_scalar(row(XC + m), row(QN), cw(3), PR2[:, CONV_B + m:CONV_B + m + 1], ALU.mult, ALU.add)
                for n in range(1, 4):
                    v.drain()
                    i = v.scalar_tensor_tensor(out=row(XC + m)[:, n:S], in0=row(QN)[:, 0:S - n], scalar=cw(3 - n),
                                               in1=row(XC + m)[:, n:S], op0=ALU.mult, op1=ALU.add)
                i.then_inc(sem("xc_ready"), 1)

            def low_tile(m, n, src, scale):
                v.wait_ge(sem("uh_ready"), m + 1 + n)
                hi = UH[:, m, :].bitcast(F32)
                if scale is None:
                    v.tensor_tensor(UL[:, m, :], src[:, m, :], hi, ALU.subtract).then_inc(sem("u_ready"), 1)
                else:
                    v.scalar_tensor_tensor(out=UL[:, m, :], in0=src[:, m, :], scalar=scale[:, bass.ds(m, 1)], in1=hi,
                                           op0=ALU.mult, op1=ALU.subtract).then_inc(sem("u_ready"), 1)

            def low(n, src, scale=None, a=0, b=KT):
                with v.Fori(a, b) as m:
                    low_tile(m, n, src, scale)

            def sum_squares(n):
                def one(s, cnt, first=False):
                    v.wait_ge(sem("sq_ready"), cnt)
                    if first:
                        i = v.tensor_copy(row(ACC), row(SQ0))
                    else:
                        i = v.tensor_tensor(row(ACC), row(ACC), row(SQ0 + s), ALU.add)
                    i.then_inc(sem("sq_used"), 1)
                    v.drain()
                one(0, n + 1, True)
                one(1, n + 2)
                with v.Fori(1, KT // 2) as i:
                    for s in range(2):
                        one(s, i * 2 + n + s + 1)

            def scale_tile(m):
                v.tensor_tensor(MIX[:, m, :], MIX[:, m, :], row(ACC), ALU.mult).then_inc(sem("tile_scaled"), 1)

            def new_operand(root, n, scale=None):
                wait_apart("root_ready", root)
                for m in range(4):
                    scale_tile(m)
                with v.Fori(0, 6) as i:
                    for s in range(2):
                        scale_tile(i * 2 + (s + 4))
                    for s in range(2):
                        low_tile(i * 2 + s, n, W[:, H:H + 16, :], scale)
                for m in range(12, 16):
                    low_tile(m, n, W[:, H:H + 16, :], scale)

            def angles(i, posf, dst_c, dst_s):
                TWO_PI = 6.283185307179586
                c1 = 6.28125
                c2 = 0.0019350051879882812
                c3 = TWO_PI - c1 - c2
                MAGIC = 12582912.0
                ang, nn, rr, mm = (row(r) for r in range(4))
                PI = 3.1415925
                v.tensor_scalar(ang, posf, CS[:, bass.ds(i + (C_INV - 1), 1)], None, ALU.mult)
                v.drain()
                v.tensor_scalar(nn, ang, 1.0 / TWO_PI, MAGIC, ALU.mult, ALU.add)
                v.drain()
                v.tensor_scalar(nn, nn, -MAGIC, None, ALU.add)
                v.drain()
                v.scalar_tensor_tensor(out=rr, in0=nn, scalar=-c1, in1=ang, op0=ALU.mult, op1=ALU.add)
                v.drain()
                v.scalar_tensor_tensor(out=rr, in0=nn, scalar=-c2, in1=rr, op0=ALU.mult, op1=ALU.add)
                v.drain()
                v.scalar_tensor_tensor(out=rr, in0=nn, scalar=-c3, in1=rr, op0=ALU.mult, op1=ALU.add)
                v.drain()
                v.tensor_scalar(mm, rr, TWO_PI / 4, -TWO_PI, ALU.is_gt, ALU.mult)
                v.drain()
                v.scalar_tensor_tensor(out=mm, in0=rr, scalar=TWO_PI / 4, in1=mm, op0=ALU.add, op1=ALU.add)
                v.drain()
                tabs_out = v.to_reg(i * 16)
                v.wait_ge(sem("tables_out"), tabs_out)
                v.tensor_scalar(dst_c, mm, PI, -PI, ALU.min, ALU.max).then_inc(sem("angle_ready"), 1)
                v.tensor_scalar(dst_s, rr, PI, -PI, ALU.min, ALU.max).then_inc(sem("angle_ready"), 1)
                v.drain()

            v.memset(ONES[:], 1.0).then_inc(sem("ones_set"), 1)
            for k in range(2):
                v.wait_ge(sem("ph_ready"), k + 1)
                v.tensor_tensor(PL[:, k, :], MIX[:, 14 + k, :], PH[:, k, :].bitcast(F32),
                                ALU.subtract).then_inc(sem("p_split"), 1)
            v.wait_ge(sem("cs_loaded"), 32)
            v.tensor_tensor(SM[:, 0:8], PR1[:, LBF + 8:LBF + 16], PR1[:, LBF:LBF + 8], ALU.subtract)
            v.tensor_tensor(SM[:, 8:16], PR1[:, LBB + 8:LBB + 16], PR1[:, LBB:LBB + 8], ALU.subtract).then_inc(sem("lb_diff"), 1)
            v.drain()
            low(0, W[:, H:H + 16, :], PR1[:, G_PRE:G_PRE + 16], 0, 12)
            v.wait_ge(sem("e_out"), 16)
            low(0, W[:, H:H + 16, :], PR1[:, G_PRE:G_PRE + 16], 12, 16)
            v.wait_ge(sem("masks_loaded"), 16)
            v.tensor_copy(MSK[:].rearrange("p n t -> p (n t)"), MIX[:, 6:8, :].rearrange("p a b -> p (a b)"))
            sum_squares(0)
            v.wait_ge(sem("lb_exp"), 1)
            v.tensor_scalar(SM[:, 16:32], SM[:, 16:32], 1.0, None, ALU.add)
            v.drain()
            v.reciprocal(LB[:, 0, :], SM[:, 16:24])
            v.reciprocal(LB[:, 2, :], SM[:, 24:32])
            v.drain()
            v.tensor_scalar(LB[:, 1, :], LB[:, 0, :], -1.0, 1.0, ALU.mult, ALU.add)
            v.tensor_scalar(LB[:, 3, :], LB[:, 2, :], -1.0, 1.0, ALU.mult, ALU.add)
            v.wait_ge(sem("pos_loaded"), 32)
            for n in range(3):
                v.tensor_copy(MIX[:, 2 + n, :], MIX[:, int(n > 0), :].bitcast(I32))
            v.wait_ge(sem("e_stored"), 16)
            v.wait_ge(sem("rstd_ready"), 1)
            for s in range(2):
                gate_tile(Tile(T_HGG + s), s, MIX[:, 8 + s, :])
            with v.Fori(1, 4) as i:
                angles(i, MIX[:, i + 1, :], row(COS), row(SIN))
                for s in range(2):
                    gate_tile(Tile(T_HGG + s, (2, i)), i * 2 + s, MIX[:, i * 2 + (8 + s), :])
            v.wait_ge(sem("tables_out"), 64)
            step(Tile(T_HG), hg=0)
            v.drain()
            with v.Fori(1, HG_HEADS) as i:
                step(Tile(T_HG, (4, i)), hg=i, work="hg", j=i - 1)
                v.drain()
            v.wait_ge(sem("tab1_loaded"), 48)
            for r in (CT1, ST1):
                v.tensor_tensor(row(r), row(r), row(RSTD), ALU.mult)
            v.drain()
            tb = (CT1, ST1, 32)
            sc1 = (ATT_HD ** -0.5, 1.0)
            step(Tile(T_ATT), rot=tb, scales=sc1, take="qt_ready", gate=(8, 0), work="hg", j=HG_HEADS - 1)
            with v.Fori(1, PAIRS) as i:
                step(Tile(T_ATT, (4, i)), rot=tb, scales=sc1, take="qt_ready", gate=(i + 8, i), work="att", j=i - 1)
            step(None, work="att", j=PAIRS - 1)
            low(16, MIX[:])
            sum_squares(16)
            new_operand(1, 32)
            v.wait_ge(sem("e_loaded"), 16)

            def pg_tile(m, s, cnt):
                v.wait_ge(sem("z_free"), cnt)
                sigmoid_of(SQ0 + s)
                v.drain()
                v.tensor_tensor(MIX[:, m, :], row(SQ0 + s), W[:, m + E, :] if not isinstance(m, int) else row(E + m),
                                ALU.mult).then_inc(sem("pg_prod"), 1)

            def pg_sum(s, cnt, first=False):
                v.wait_ge(sem("sq_ready"), cnt)
                if first:
                    i = v.tensor_copy(row(ACC), row(SQ0))
                else:
                    i = v.tensor_tensor(row(ACC), row(ACC), row(SQ0 + s), ALU.add)
                i.then_inc(sem("sq_used"), 1)
                v.drain()

            for s in range(2):
                pg_tile(s, s, T_PG + s - 1)
                pg_sum(s, 32 + s + 1, s == 0)
            with v.Fori(1, KT // 2) as i:
                for s in range(2):
                    pg_tile(i * 2 + s, s, i * 2 + (T_PG + s - 1))
                    pg_sum(s, i * 2 + 32 + s + 1)

            with v.Fori(0, LAYERS) as l:
                new_operand(l + 2, l * 32 + 48, PR2[:, G2_PRE:G2_PRE + 16])
                for n in range(2):
                    v.tensor_tensor(DL[:, 2 * n, :], DL[:, 2 * n, :], DL[:, 2 * n + 1, :], ALU.mult)
                v.drain()
                for n in range(2):
                    i = v.tensor_reduce(SM[:, 8 + n:9 + n], DL[:, 2 * n, :], AX.X, ALU.add)
                i.then_inc(sem("lam_dot"), 1)
                lam = PR2[:, LAM:LAM + 6]
                v.tensor_scalar(SM[:, 12:18], lam, -1.0, None, ALU.mult)
                v.tensor_scalar(SM[:, 24:30], lam, 0.0, None, ALU.min)
                v.tensor_scalar(SM[:, 32:44], PR2[:, BA:BA + 12], -1.0, None, ALU.mult)
                v.drain()
                v.tensor_tensor(SM[:, 12:18], SM[:, 12:18], lam, ALU.max).then_inc(sem("lam_abs"), 1)
                sum_squares(l * 32 + 48)
                v.wait_ge(sem("lam_exp"), l * 2 + 2)
                v.tensor_tensor(SM[:, 60:61], SM[:, 11:12], SM[:, 10:11], ALU.subtract)
                v.drain()
                v.tensor_tensor(SM[:, 60:61], SM[:, 60:61], CS[:, bass.ds(l * 2 + C_LAM, 1)], ALU.subtract)
                v.tensor_tensor(SM[:, 61:62], PR2[:, G2_SUB:G2_SUB + 1], CS[:, bass.ds(l * 2 + (C_LAM + 1), 1)], ALU.mult)
                v.wait_ge(sem("lam_e"), l + 1)
                e, w, w2, pl = SM[:, 18:24], SM[:, 44:50], SM[:, 50:56], SM[:, 12:18]
                v.tensor_scalar(w, e, 2.0, None, ALU.add)
                v.drain()
                v.reciprocal(w, w)
                v.drain()
                v.tensor_tensor(w, w, e, ALU.mult)
                v.drain()
                v.tensor_tensor(w2, w, w, ALU.mult)
                v.drain()
                v.tensor_scalar(pl, w2, 1.0 / 15, None, ALU.mult)
                for n in (13, 11, 9, 7, 5, 3):
                    v.drain()
                    v.scalar_tensor_tensor(out=pl, in0=pl, scalar=1.0 / n, in1=w2, op0=ALU.add, op1=ALU.mult)
                v.drain()
                v.scalar_tensor_tensor(out=pl, in0=pl, scalar=1.0, in1=w, op0=ALU.add, op1=ALU.mult)
                v.drain()
                v.scalar_tensor_tensor(out=pl, in0=pl, scalar=-2.0, in1=SM[:, 24:30], op0=ALU.mult, op1=ALU.add)
                v.drain()
                v.tensor_scalar(SM[:, 44:50], pl, 8.0, None, ALU.mult)
                v.tensor_scalar(SM[:, 50:56], pl, 16.0, None, ALU.mult).then_inc(sem("cl_ready"), 1)

                wait_apart("rstd_ready", l + 2)
                for m in range(LRU_TILES):
                    lru_conv(Tile(T_L2 + R_LX + m, (PER_LAYER, l)), m)
                v.wait_ge(sem("tab2_loaded"), l * 48 + 48)
                for r in (CTR, STR, CTD):
                    v.tensor_tensor(row(r), row(r), row(RSTD), ALU.mult)
                v.wait_ge(sem("tab3_loaded"), l * 32 + 32)
                v.tensor_tensor(row(STD), row(STD), row(RSTD), ALU.mult)
                v.drain()
                scr = (1.0, 128 ** -0.5)
                scd = (64 ** -0.5, 1.0)
                gl = l * 16 + 16
                step(Tile(T_L2 + R_RET, (PER_LAYER, l)), rot=(CTR, STR, 64), scales=scr, take="rqt_ready", gate=(gl, 0))
                for h in range(1, RET_HEADS):
                    step(Tile(T_L2 + R_RET + 4 * h, (PER_LAYER, l)), rot=(CTR, STR, 64), scales=scr,
                         take="rqt_ready", gate=(gl + h, h), work="ret", j=l * RET_HEADS + h - 1, m=h - 1)
                step(Tile(T_L2 + R_DIF, (PER_LAYER, l)), rot=(CTD, STD, 32), scales=scd, take="dqt_ready",
                     gate=(gl + 6, 6), work="ret", j=l * RET_HEADS + RET_HEADS - 1, m=5)
                with v.Fori(1, DIF_HEADS) as i:
                    step(Tile(T_L2 + R_DIF, (PER_LAYER, l), (4, i)), rot=(CTD, STD, 32), scales=scd,
                         take="dqt_ready", gate=(gl + i + 6, i + 6), work="dif", j=l * DIF_HEADS + i - 1, m=i + 5)
                step(Tile(T_L2 + R_LG, (PER_LAYER, l)), work="dif", j=l * DIF_HEADS + DIF_HEADS - 1, m=9, lru=gl + 10)
                for m in range(4, LRU_TILES):
                    lru_gate(Tile(T_L2 + R_LG + m, (PER_LAYER, l)), gl + 10 + m, m)
                v.tensor_scalar(SM[:, 62:63], SM[:, 61:62], 1.0, None, ALU.mult).then_inc(sem("par_used"), 1)
                low(l * 32 + 64, MIX[:])
                sum_squares(l * 32 + 64)
                v.drain()
            wait_apart("root_ready", LAYERS + 2)
            with v.Fori(0, KT) as m:
                scale_tile(m)



def tiles(w):
    r, c = w.shape
    return w.reshape(r // P, P, c // P, P).transpose(2, 1, 0, 3)


def cols(v):
    return v.reshape(-1, P).T


def constants():
    inv1 = np.power(np.float32(500000.0), -np.arange(0, 16, 2, dtype=np.float32) / np.float32(16))
    invr = (1.0 / (np.float32(10000.0) ** np.linspace(0, 1, 64, dtype=np.float32))).astype(np.float32)
    invd = (1.0 / (np.float32(10000.0) ** (np.arange(0, 64, 2, dtype=np.float32) / np.float32(64)))).astype(np.float32)
    cst = np.zeros((P, CST), np.float32)
    for p in range(P):
        if p % 32 < 8:
            cst[p, 0] = inv1[p % 32]
        cst[p, 1] = invr[p % 64]
        cst[p, 2] = invd[p % 32]
    cst[:, C_EPS] = EPS
    for l in range(LAYERS):
        li = 0.8 - 0.6 * np.exp(-0.3 * l)
        cst[:, C_LAM + 2 * l], cst[:, C_LAM + 2 * l + 1] = li, 1.0 - li
    a = np.arange(P)
    x = a[:, None] ^ a[None, :]
    masks = np.zeros((P, 8, P), np.float32)
    for n in range(1, 8):
        masks[:, n, :] = (x >= 1 << (n - 1)) & (x < 1 << n)
    t = np.arange(S)
    d = t[:, None] - t[None, :]
    count = np.zeros((S, S))
    for w, dil in ((128, 1), (512, 4), (2048, 16)):
        half = (w // 2) // dil
        count += (d % dil == 0) & (np.abs(d) // dil <= half)
    bias = np.where(count > 0, np.log(np.maximum(count, 1)), NEG).astype(np.float32)
    bias = np.ascontiguousarray(bias.reshape(4, P, S).transpose(1, 0, 2))
    dec = np.zeros((RET_HEADS, P, S), np.float32)
    dd = np.arange(S)[None, :] - np.arange(P)[:, None]
    for h in range(RET_HEADS):
        dec[h] = np.where(dd >= 0, np.exp(np.maximum(dd, 0) * np.log1p(-2.0 ** (-5.0 - h))), 0.0)
    cm = np.zeros((P, S), np.float32)
    cm[:, S - P:] = np.where(a[None, :] <= a[:, None], 0.0, NEG)
    return dict(cst=cst, idn=np.eye(P, dtype=np.float32), masks=masks, bias=bias, dec=dec, cmask=cm)


def layout(i):
    w1 = tiles(i["w_in"][0])
    head = np.r_[0:8, 16:40, 8:16, 40:64]
    w1 = np.concatenate([w1[:2 * PAIRS][..., np.r_[head, head + 64]], w1[2 * PAIRS:]])
    A = ATT_W // P
    aq, ak, av, ag, hq, ff, fb, hv, hg = (range(8 * n, 8 * n + 8) for n in range(9))
    order1 = list(hg) + [x for j in range(8) for x in (ff[j], fb[j], hq[j], hv[j])] + \
        [x for j in range(8) for x in (aq[j], ak[j], av[j], ag[j])]
    pp = i["w_pp"][0].reshape(2, P, 2, 8, P).transpose(2, 1, 3, 0, 4).reshape(2, P, KT * P)
    parts = [pp, w1[order1], tiles(i["w_out"][0]), tiles(i["w_pg"][0])]
    for l in range(LAYERS):
        w2 = tiles(i["w_in_2"][l])
        o2 = list(range(40, 46)) + [6 * n + j for j in range(6) for n in range(4)] + \
            [24 + 4 * n + j for j in range(4) for n in range(4)] + list(range(46, 52))
        parts += [w2[o2], tiles(i["w_out_2"][l])]
    parts.append(parts[0][0:1])
    wt = np.concatenate([x.reshape(-1, P, KT * P) for x in parts])
    par1 = np.concatenate([cols(i["g_pre"][0]), cols(i["g_post"][0]), cols(i["g_ple"][0]), cols(i["g_hg"][0])] +
                          [cols(i[n][r]) for n in ("lb_fwd", "lb_bwd") for r in range(2)], 1)
    par2, gws = [], []
    for l in range(LAYERS):
        cw = i["lru_conv_w_2"][l].reshape(4, LRU_TILES, P).transpose(2, 1, 0).reshape(P, 24)
        par2.append(np.concatenate([cols(i["pre_norm_g_2"][l]), cols(i["post_norm_g_2"][l]), cols(i["diff_subln_g_2"][l]), cw] +
                                   [cols(i[n][l]) for n in ("lru_conv_b_2", "lru_ba_2", "lru_bx_2", "lru_lambda_2")], 1))
        both = []
        for n in ("lru_wa_2", "lru_wx_2"):
            full = np.zeros((8 * LRU_BW, 8 * LRU_BW), np.float32)
            for b in range(8):
                full[b * LRU_BW:(b + 1) * LRU_BW, b * LRU_BW:(b + 1) * LRU_BW] = i[n][l, b]
            both += [full[P * x:P * x + P, P * y:P * y + P] for x, y in LRU_PAIRS]
        gws.append(np.stack(both, 1).reshape(P, 2 * NG * P))
    dl = np.stack([np.concatenate([i[f"diff_lambda_{n}_2"][l] for n in ("q1", "k1", "q2", "k2")]) for l in range(LAYERS)])
    return dict(wt=wt, xT=i["x"][0].T.reshape(KT, P, S), pT=i["p"][0, 0].T.reshape(2, P, S),
                pos1=i["positions"], pos2=i["positions_2"], par1=par1, par2=np.stack(par2), dlam=dl[:, None, :],
                gw=np.stack(gws))


ORDER = ["wt", "xT", "pT", "pos1", "pos2", "par1", "par2", "dlam", "gw", "cst", "idn", "masks", "bias", "dec", "cmask"]


def kernel(**inputs):
    import concourse.bacc as _bacc
    from concourse.bass_utils import run_bass_kernel_spmd as _run

    arrays = layout({n: np.asarray(a) for n, a in inputs.items()})
    arrays.update(constants())
    nc = _bacc.Bacc("TRN2", target_bir_lowering=False, num_devices=1)
    feed, args = {}, []
    for name in ORDER:
        a = np.ascontiguousarray(arrays[name])
        feed[f"in_{name}"] = a
        args.append(nc.dram_tensor(f"in_{name}", a.shape, mybir.dt.from_np(a.dtype), kind="ExternalInput").ap())
    args.append(nc.dram_tensor("out_hT", (KT, P, S), F32, kind="ExternalOutput").ap())
    build(nc, *args)
    r = _run(nc, [feed], core_ids=[0])
    return np.ascontiguousarray(r.results[0]["out_hT"].reshape(D, S).T)[None]
```

```python
from contextlib import ExitStack

import numpy as np
import concourse.bass as bass
from concourse import mybir

F32 = mybir.dt.float32
F32R = mybir.dt.float32r
U8 = mybir.dt.uint8
I32 = mybir.dt.int32
ACT = mybir.ActivationFunctionType
ALU = mybir.AluOpType
AX = mybir.AxisListType

P = 128
S = 512
D = 2048
KT = D // P
EPS = 1e-6
NEG = -1e30
ROWS = 36
PRIMED = 1
POOL_LAST = 10
REUSE_SIGNALS = ("hav_done", "hg_done", "lv_free", "hro_ready", "att_done", "pte0", "pte1", "sm_done", "pt_done", "av_done",
                 "ra_ready", "ret_done", "dpte", "dsm_done", "dif_done", "dpt_done", "dav_done", "rav_done", "scan_done",
                 "gate_read", "par_used", "sq_used")

ATT_W, ATT_HD = 1024, 64
HG_HEADS = 8
PAIRS = 8
LAYERS = 2
RET_HEADS, DIF_HEADS, LRU_TILES = 6, 4, 6
LRU_BW = 96

T_PP, T_HGG, T_HG, T_ATT, T_OUT, T_PG, T_L2 = 0, 2, 10, 42, 74, 90, 106
R_LX, R_RET, R_DIF, R_LG, R_OUT, PER_LAYER = 0, 6, 30, 46, 52, 68
NT = T_L2 + LAYERS * PER_LAYER

G_PRE, G_POST, G_PLE, G_HG, LBF, LBB = 0, 16, 32, 48, 49, 65
PAR1 = 81
G2_PRE, G2_POST, G2_SUB, CONV_W, CONV_B, BA, BX, LAM = 0, 16, 32, 33, 57, 63, 69, 75
PAR2 = 81
C_INV, C_EPS, C_LAM = 0, 3, 4
CST = 8

LRU_PAIRS = [(a, b) for b in range(LRU_TILES) for a in range(LRU_TILES)
             if any(max(LRU_BW * n, P * a) < min(LRU_BW * (n + 1), P * (a + 1)) and
                    max(LRU_BW * n, P * b) < min(LRU_BW * (n + 1), P * (b + 1)) for n in range(8))]
NG = len(LRU_PAIRS)


LEVEL_AT = {1: 0, 2: 1, 3: 2, 4: 3, 6: 4, 7: 5, 8: 6, 10: 7, 11: 8, 12: 9}

ATT_SCORES = {0: 0, 2: 1, 6: 2, 10: 3}
ATT_SOFTMAX = {1: 0, 4: 1, 8: 2, 12: 3}
ATT_TURN = {3: 0, 6: 1, 10: 2, 14: 3}
ATT_VALUES = {4: 0, 7: 1, 11: 2, 15: 3}
DIF_SCORES = {0: 0, 3: 1, 7: 2, 11: 3}
DIF_SOFTMAX = {1: 0, 4: 1, 8: 2, 12: 3}
DIF_TURN = {3: 0, 6: 1, 10: 2, 14: 3}
DIF_VALUES = {4: 0, 7: 1, 11: 2, 15: 3}


class Tile:

    def __init__(self, c, *terms):
        self.c, self.terms = c, terms

    def plus(self, n):
        return Tile(self.c + n, *self.terms)

    def times(self, k, add=0):
        v = self.c * k + add
        for m, i in self.terms:
            v = i * (m * k) + v
        return v

    def pair(self):
        v = self.c // 2
        for m, i in self.terms:
            v = i * (m // 2) + v
        return v

    @property
    def odd(self):
        return self.c % 2


def build(nc, wt, xT, pT, pos1, pos2, par1, par2, dlam, gw, cst, idn, masks, bias, dec, cmask, out):
    ctx = ExitStack()
    with ctx:
        sems = {}

        def sb(name, shape, dt=F32):
            return ctx.enter_context(nc.sbuf_tensor(name, shape, dt))

        def sem(name):
            if name not in sems:
                sems[name] = ctx.enter_context(nc.semaphore(name))
            return sems[name]

        tabs = nc.dram_tensor("rope_tables", [6, P, S], F32, kind="Internal").ap()
        e_dram = nc.dram_tensor("e_scratch", [KT, P, S], F32, kind="Internal").ap()

        RAW = sb("w_raw", [P, 2, KT * P])
        WH = sb("w_high", [P, KT, P], F32R)
        WL = sb("w_low", [P, KT, P], F32R)
        UH = sb("u_high", [P, KT, S], F32R)
        UL = sb("u_low", [P, KT, S], F32R)
        MIX = sb("mixed", [P, KT, S])
        W = sb("work", [P, ROWS, S])
        MSK = sb("level_masks", [P, 8, P], U8)
        ONES = sb("ones", [P, P])
        IDN = sb("identity", [P, P])
        PR1 = sb("params_1", [P, PAR1])
        PR2 = sb("params_2", [P, PAR2])
        LB = sb("lower_bounds", [P, 4, 8])
        DL = sb("lambda_vectors", [P, 4, 64])
        CS = sb("constants", [P, CST])
        SM = sb("small", [P, 64])
        PRIME = sb("prime", [1, len(REUSE_SIGNALS) + 1])

        Z = [ctx.enter_context(nc.psum_tensor(f"z{i}", [P, S], F32)) for i in range(2)]
        SC = [ctx.enter_context(nc.psum_tensor(f"scores{i}", [P, S], F32)) for i in range(2)]
        TP = [ctx.enter_context(nc.psum_tensor(f"turned{i}", [P, S], F32)) for i in range(2)]
        OB = ctx.enter_context(nc.psum_tensor("o_bank", [P, S], F32))

        def row(r, n=1):
            return W[:, r, :] if n == 1 else W[:, r:r + n, :]

        def view(r, off, dims):
            a = W[:]
            return bass.AP(a.tensor, r * S + off, [a.ap[0]] + dims)

        H = 0
        E = 16
        SQ0, ACC, RSTD = 32, 34, 35
        ANG, COS, SIN = 8, 12, 13
        FB, FF, Q, VT, QB, KF, QF, KB, TT, HVN, AT = 0, 1, 2, 3, 4, 5, 6, 7, 8, 10, 11
        HSQ, HRO, HTMP, KM, KS, SG, SE = 15, 16, 17, 18, 19, 20, 21
        QT, KTR, VTA, QN, KN, RW, TM = 22, 23, 24, 25, 26, 27, 28
        CT1, ST1, BIAS = 29, 30, 31
        SMR, PRB, VN, PT = 0, 2, 4, 5
        CTR, STR, CTD, STD, CM, DEC = 29, 30, 31, 32, 33, 34
        NRO = 8
        RA = [0, S, 2 * S - P, 3 * S - 3 * P]
        LTB, LR, LI, LA = 3, 5, 6, 7
        GW, XC = 9, 16

        SPARE = {2: SC[0], 3: SC[1]}
        PH, PL = UL[:, 12:14, :], UL[:, 14:16, :]

        block = ctx.enter_context(nc.Block())

        @block.sync
        def _(sp):
            def load(t):
                sp.dma_start(RAW[:, t.odd, :], wt[t.times(1)]).then_inc(sem("w_raw1" if t.odd else "w_raw0"), 16)

            load(Tile(0))
            load(Tile(1))
            with sp.Fori(1, NT // 2) as g:
                for o in range(2):
                    t = Tile(o, (2, g))
                    sp.wait_ge(sem("l_ready"), t.times(4, -4))
                    load(t)
            sp.wait_ge(sem("l_ready"), 4 * NT - 4)
            load(Tile(NT))
            sp.wait_ge(sem("w_raw0"), 16 * (NT // 2 + 1))

        @block.gpsimd
        def _(pool):
            for n, name in enumerate(REUSE_SIGNALS):
                pool.memset(PRIME[:, n:n + 1], 0.0).then_inc(sem(name), PRIMED)
            pool.memset(PRIME[:, len(REUSE_SIGNALS):], 0.0).then_inc(sem("tables_out"), 16)

            def low_parts(t):
                for q in range(4):
                    pool.wait_ge(sem("h_ready"), t.times(4, q + 1))
                    pool.tensor_tensor(
                        WL[:, 4 * q:4 * q + 4, :], RAW[:, t.odd, 512 * q:512 * q + 512].rearrange("p (k c) -> p k c", k=4),
                        WH[:, 4 * q:4 * q + 4, :].bitcast(F32), ALU.subtract).then_inc(sem("l_ready"), 1)

            def add_residual(loaded, n, tiles=KT):
                loaded = loaded if isinstance(loaded, int) else pool.to_reg(loaded)
                pool.wait_ge(sem("x0_loaded"), 16)
                pool.wait_ge(sem("h_loaded"), loaded)
                with pool.Fori(0, tiles // 2) as i:
                    for s in range(2):
                        pool.wait_ge(sem("tile_scaled"), i * 2 + n + s + 1)
                        m = i * 2 + s
                        pool.tensor_tensor(W[:, m, :], W[:, m, :], MIX[:, m, :], ALU.add).then_inc(sem("h_new"), 1)

            with pool.Fori(0, T_PG // 2) as i:
                for o in range(2):
                    low_parts(Tile(o, (2, i)))
            low_parts(Tile(T_PG))
            add_residual(64, 0)
            with pool.Fori(0, (T_L2 - T_PG) // 2) as i:
                for o in range(2):
                    low_parts(Tile(T_PG + 1 + o, (2, i)))
            with pool.Fori(0, LAYERS) as l:
                add_residual(l * 64 + 64, l * 16 + 16)
                with pool.Fori(0, PER_LAYER // 2) as i:
                    for o in range(2):
                        low_parts(Tile(T_L2 + 1 + o, (PER_LAYER, l), (2, i)))
            add_residual(LAYERS * 64 + 64, LAYERS * 16 + 16, POOL_LAST)

        @block.tensor
        def _(pe):
            def quarter(t, q, gen=None, spare=None, behind=2):
                bank = Z[t.odd] if spare is None else spare
                if q == 0 and spare is None:
                    if t.c in (T_HGG, T_HGG + 1) and not t.terms:
                        pe.wait_ge(sem("e_out"), 16)
                    else:
                        pe.wait_ge(sem("z_free"), t.times(1, 1 - T_HGG - behind))
                pe.wait_ge(sem("l_ready"), t.times(4, q + 1))
                for k in range(4 * q, 4 * q + 4):
                    if gen is not None:
                        pe.wait_ge(sem("u_ready"), gen * 16 + k + 1)
                    for n, (w, u) in enumerate(((WH, UH), (WH, UL), (WL, UH))):
                        mm = pe.matmul(bank[:], w[:, k, :], u[:, k, :], start=(k == 0 and n == 0),
                                       stop=(k == KT - 1 and n == 2))
                mm.then_inc(sem("w_free"), 1)

            def sum_rows(src, bank, wait, done):
                pe.wait_ge(*wait)
                pe.matmul(bank[:], ONES[:], src, start=True, stop=True).then_inc(sem(done), 1)

            def turn_v(src, wait, done):
                pe.wait_ge(*wait)
                for c in range(4):
                    mm = pe.transpose(TP[0][:, c * P:(c + 1) * P], src[:, c * P:(c + 1) * P], IDN[:])
                mm.then_inc(sem(done), 1)

            def hg_work(j, p):
                def level(n):
                    pe.wait_ge(sem("qk_ready"), j * 9 + max(n, 1))
                    if 1 <= n <= 7:
                        pe.wait_ge(sem("km_ready"), j * 7 + n)
                    if n < 2:
                        pe.wait_ge(sem("lv_free"), PRIMED + j * 10)
                    elif n < 9:
                        pe.wait_ge(sem("lv_free"), PRIMED + j * 10 + n - 1)
                    if n <= 8:
                        bank = SC[n % 2]
                        for c in range(4):
                            if n == 0:
                                kk, qq = row(KS)[:, c * P:(c + 1) * P], row(Q)[:, c * P:(c + 1) * P]
                            elif n < 8:
                                h = 1 << (n - 1)
                                kk = row(KM)[:, c * P:(c + 1) * P]
                                qq = view(QB, c * P, [[2 * h, P // (2 * h)], [2 * S + h, 2], [1, h]])
                            else:
                                kk = row(KB if c % 2 else KF)[:, c * P:(c + 1) * P]
                                o = c ^ 1
                                qq = row(QF if o % 2 else QB)[:, o * P:(o + 1) * P]
                            mm = pe.matmul(bank[:, c * P:(c + 1) * P], kk, qq, start=True, stop=True)
                    else:
                        pe.wait_ge(sem("hvn_ready"), j + 1)
                        pe.wait_ge(sem("hro_ready"), PRIMED + j)
                        for c in range(4):
                            bank = TP[c // 2]
                            kk = row(KF if c < 2 else KB)[:, c * P:(c + 1) * P]
                            qq = row(QF)[:, 256:512] if c < 2 else row(QB)[:, 0:256]
                            mm = pe.matmul(bank[:, (c % 2) * 256:(c % 2) * 256 + 256], kk, qq, start=True, stop=True)
                    mm.then_inc(sem("lv_done"), 1)

                if p == 1:
                    turn_v(row(VT), (sem("z_free"), j * 4 + (T_HG + 4 - T_HGG)), "hv_turned")
                if p in LEVEL_AT:
                    level(LEVEL_AT[p])
                if p == 13:
                    pe.wait_ge(sem("lv_free"), PRIMED + j * 10 + 10)
                    pe.wait_ge(sem("hg_done"), PRIMED + j)
                    for c in range(4):
                        mm = pe.matmul(OB[:], row(HVN)[:, c * P:(c + 1) * P], row(AT + c), start=(c == 0), stop=(c == 3))
                    mm.then_inc(sem("hav_done"), 1)
                if p == 14:
                    sum_rows(row(HSQ), TP[1], (sem("hsq_ready"), j + 1), "hss_done")

            def att_work(j, p):
                if p == 0:
                    pe.wait_ge(sem("pte0"), PRIMED + j * 4)
                    turn_v(row(VTA), (sem("qt_ready"), j + 1), "v_turned")
                if p in ATT_SCORES:
                    a = ATT_SCORES[p]
                    for hd in range(2):
                        u = 2 * a + hd
                        pe.wait_ge(sem("sm_done"), PRIMED + j * 8 + max(u - 1, 0))
                        o = 64 * hd
                        pe.matmul(SC[hd][:], row(QT)[o:o + 64, a * P:(a + 1) * P], row(KTR)[o:o + 64, :],
                                  start=True, stop=True).then_inc(sem("s_done"), 1)
                if p in ATT_TURN:
                    a = ATT_TURN[p]
                    for hd in range(2):
                        pe.wait_ge(sem("p_ready"), j * 8 + 2 * a + hd + 1)
                        if hd == 0 and a == 0:
                            pe.wait_ge(sem("vn_ready"), j + 1)
                        pe.wait_ge(sem(f"pte{hd}"), PRIMED + j * 4 + a)
                        for c in range(4):
                            mm = pe.transpose(TP[hd][:, c * P:(c + 1) * P], row(PRB + hd)[:, c * P:(c + 1) * P], IDN[:])
                        mm.then_inc(sem("pt_done"), 1)
                if p in ATT_VALUES:
                    a = ATT_VALUES[p]
                    if a == 0:
                        pe.wait_ge(sem("att_done"), PRIMED + j)
                    for hd in range(2):
                        pe.wait_ge(sem(f"pte{hd}"), PRIMED + j * 4 + a + 1)
                        for c in range(4):
                            mm = pe.matmul(OB[64 * hd:64 * hd + 64, a * P:(a + 1) * P],
                                           row(VN)[:, c * P + 64 * hd:c * P + 64 * hd + 64],
                                           row(PT + hd)[:, c * P:(c + 1) * P], start=(c == 0), stop=(c == 3))
                    mm.then_inc(sem("av_done"), 1)

            def ret_work(j, p, b):
                if p == 1:
                    pe.wait_ge(sem("gate_read"), PRIMED + j * 2)
                if p == 0:
                    turn_v(row(VTA), (sem("rqt_ready"), j + 1), "rv_turned")
                if 1 <= p <= 4:
                    c = p - 1
                    pe.wait_ge(sem("ra_ready"), PRIMED + j * 4 + max(c - 1, 0))
                    pe.matmul(SC[c % 2][:, 0:S - c * P], row(KTR)[:, c * P:(c + 1) * P], row(QT)[:, c * P:S],
                              start=True, stop=True).then_inc(sem("rs_done"), 1)
                if p == 6:
                    pe.wait_ge(sem("ra_ready"), PRIMED + j * 4 + 4)
                    pe.wait_ge(sem("rvn_ready"), j + 1)
                    pe.wait_ge(sem("ret_done"), PRIMED + j)
                    for c in range(4):
                        mm = pe.matmul(OB[:, c * P:S], row(VN)[:, c * P:(c + 1) * P], view(0, RA[c], [[1, S - c * P]]),
                                       start=(c == 0), stop=(c == 3), skip_group_check=True)
                    mm.then_inc(sem("rav_done"), 1)
                if p == 8:
                    sum_rows(row(NRO), TP[1], (sem("rsq_ready"), j + 1), "rss_done")
                if p == 9:
                    pe.wait_ge(sem("ra_ready"), PRIMED + j * 4 + 4)
                    for g in range(2):
                        use = [n for n, (x, y) in enumerate(LRU_PAIRS) if y == b]
                        for n in use:
                            mm = pe.matmul(SC[g][:], view(GW, (g * NG + n) * P, [[1, P]]), row(XC + LRU_PAIRS[n][0]),
                                           start=(n == use[0]), stop=(n == use[-1]))
                        mm.then_inc(sem("gate_done"), 1)

            def dif_work(j, p):
                if p == 0:
                    pe.wait_ge(sem("dpte"), PRIMED + j * 4)
                    turn_v(row(VTA), (sem("dqt_ready"), j + 1), "dv_turned")
                if p in DIF_VALUES:
                    a = DIF_VALUES[p]
                    if a == 0:
                        pe.wait_ge(sem("dif_done"), PRIMED + j)
                    pe.wait_ge(sem("dpte"), PRIMED + j * 4 + a + 1)
                    for c in range(a + 1):
                        mm = pe.matmul(OB[:, a * P:(a + 1) * P], row(VN)[:, c * P:(c + 1) * P],
                                       row(PT)[:, c * P:(c + 1) * P], start=(c == 0), stop=(c == a))
                    mm.then_inc(sem("dav_done"), 1)
                if p in DIF_TURN:
                    a = DIF_TURN[p]
                    pe.wait_ge(sem("dp_ready"), j * 4 + a + 1)
                    if a == 0:
                        pe.wait_ge(sem("dvn_ready"), j + 1)
                    pe.wait_ge(sem("dpte"), PRIMED + j * 4 + a)
                    for c in range(a + 1):
                        mm = pe.transpose(TP[0][:, c * P:(c + 1) * P], row(PRB)[:, c * P:(c + 1) * P], IDN[:])
                    mm.then_inc(sem("dpt_done"), 1)
                if p in DIF_SCORES:
                    a = DIF_SCORES[p]
                    for hd in range(2):
                        u = 2 * a + hd
                        pe.wait_ge(sem("dsm_done"), PRIMED + j * 8 + max(u - 1, 0))
                        o, w = 64 * hd, (a + 1) * P
                        pe.matmul(SC[hd][:, 0:w], row(QT)[o:o + 64, a * P:(a + 1) * P], row(KTR)[o:o + 64, 0:w],
                                  start=True, stop=True).then_inc(sem("ds_done"), 1)
                if p == 15:
                    sum_rows(row(NRO), TP[1], (sem("dsq_ready"), j + 1), "dss_done")

            WORK = {"hg": hg_work, "att": att_work, "ret": ret_work, "dif": dif_work}

            def step(t, work=None, j=None, between={}, **kw):
                for p in range(16):
                    s, q = divmod(p, 4)
                    if t is not None:
                        quarter(t.plus(s), q)
                    if work is not None:
                        WORK[work](j, p, **kw)
                    if p in between:
                        between[p]()

            def slots(t, n, gen=None, started=0):
                for s in range(2):
                    for q in range(0 if s else started, 4):
                        quarter(t.plus(s), q, gen if s == 0 else None)
                with pe.Fori(1, n // 2) as i:
                    for s in range(2):
                        for q in range(4):
                            quarter(Tile(t.c + s, *t.terms, (2, i)), q)

            pe.wait_ge(sem("p_split"), 2)
            for m in range(KT):
                t, n = divmod(m, 8)
                if n % 2 == 0:
                    pe.wait_ge(sem("l_ready"), 4 * t + n // 2 + 1)
                if m >= 2:
                    pe.wait_ge(sem("e_out"), m - 1)
                for k in range(2):
                    for i, (w, u) in enumerate(((WH, PH), (WH, PL), (WL, PH))):
                        mm = pe.matmul(Z[m % 2][:], w[:, 2 * n + k, :], u[:, k, :], start=(k == 0 and i == 0),
                                       stop=(k == 1 and i == 2))
                mm.then_inc(sem("w_free") if n % 2 else sem("e_even"), 1)

            for m in range(8):
                for q in range(4):
                    quarter(Tile(T_HGG + m), q, 0 if m == 0 else None, SPARE.get(m), 4 if m in (4, 5) else 2)
                if m == 2:
                    pe.wait_ge(sem("consts"), 16)
                    pe.wait_ge(sem("ones_set"), 1)
                    sum_rows(row(ACC), OB, (sem("sq_used"), PRIMED + 16), "ss_done")
            step(Tile(T_HG))
            with pe.Fori(1, HG_HEADS) as i:
                step(Tile(T_HG, (4, i)), work="hg", j=i - 1)
            step(Tile(T_ATT), work="hg", j=HG_HEADS - 1)
            pe.wait_ge(sem("hg_done"), PRIMED + HG_HEADS)
            with pe.Fori(1, PAIRS) as i:
                step(Tile(T_ATT, (4, i)), work="att", j=i - 1)
            step(None, work="att", j=PAIRS - 1,
                 between={p: lambda q=q: quarter(Tile(T_OUT), q, 1) for p, q in ((7, 0), (11, 1), (14, 2))})
            slots(Tile(T_OUT), 16, gen=1, started=3)
            sum_rows(row(ACC), OB, (sem("sq_used"), PRIMED + 32), "ss_done")
            slots(Tile(T_PG), 16, gen=2)
            sum_rows(row(ACC), OB, (sem("sq_used"), PRIMED + 48), "ss_done")

            with pe.Fori(0, LAYERS) as l:
                for m in range(LRU_TILES):
                    for q in range(4):
                        quarter(Tile(T_L2 + R_LX + m, (PER_LAYER, l)), q, l * 2 + 3 if m == 0 else None, SPARE.get(m))
                    if m == 2:
                        sum_rows(row(ACC), OB, (sem("sq_used"), PRIMED + l * 32 + 64), "ss_done")
                step(Tile(T_L2 + R_RET, (PER_LAYER, l)))
                pe.wait_ge(sem("gw_loaded"), l * 16 + 16)
                pe.wait_ge(sem("xc_ready"), l * 6 + 6)
                for h in range(1, RET_HEADS + 1):
                    step(Tile(T_L2 + R_RET + 4 * h, (PER_LAYER, l)), work="ret", j=l * RET_HEADS + h - 1, b=h - 1)
                pe.wait_ge(sem("gate_read"), PRIMED + l * 12 + 12)
                rets = pe.to_reg(l * RET_HEADS + (RET_HEADS + PRIMED))
                pe.wait_ge(sem("ones_set"), 1)
                pe.wait_ge(sem("ret_done"), rets)
                with pe.Fori(1, DIF_HEADS) as i:
                    step(Tile(T_L2 + R_DIF, (PER_LAYER, l), (4, i)),
                         work="dif", j=l * DIF_HEADS + i - 1)
                step(Tile(T_L2 + R_LG, (PER_LAYER, l)), work="dif", j=l * DIF_HEADS + DIF_HEADS - 1)
                for m in range(4, LRU_TILES):
                    for q in range(4):
                        quarter(Tile(T_L2 + R_LG + m, (PER_LAYER, l)), q)
                slots(Tile(T_L2 + R_OUT, (PER_LAYER, l)), 16, gen=l * 2 + 4)
                sum_rows(row(ACC), OB, (sem("sq_used"), PRIMED + l * 32 + 80), "ss_done")

        @block.scalar
        def _(act):
            def high(t, q):
                n = t.plus(1)
                act.wait_ge(sem("w_raw1" if n.odd else "w_raw0"), n.pair() * 16 + 16)
                act.wait_ge(sem("w_free"), t.times(4, q + 1))
                act.activation(WH[:, 4 * q:4 * q + 4, :],
                               RAW[:, n.odd, 512 * q:512 * q + 512].rearrange("p (k c) -> p k c", k=4),
                               ACT.Copy).then_inc(sem("h_ready"), 1)

            def copy(dst, src, done=None, **kw):
                i = act.activation(dst, src, ACT.Copy, **kw)
                if done:
                    i.then_inc(sem(done), 1)

            def inv_root(bank, dst, width, wait, done):
                act.wait_ge(*wait)
                act.activation(dst, bank[:], ACT.Ln, bias=CS[:, C_EPS:C_EPS + 1], scale=1.0 / width)
                act.drain()
                act.activation(dst, dst, ACT.Exp, scale=-0.5).then_inc(sem(done), 1)

            def gate_exp(t, src=RW, dst=TM, done="gexp"):
                act.wait_ge(sem("z_free"), t.times(1, -T_HGG + 1))
                act.activation(row(dst), row(src), ACT.Exp, scale=-1.0).then_inc(sem(done), 1)

            def hg_work(j, p):
                if p == 1:
                    act.wait_ge(sem("hav_done"), PRIMED + j)
                    act.wait_ge(sem("hv_turned"), j + 1)
                    copy(row(HVN), TP[0][:], "hvn_ready")
                    act.wait_ge(sem("lv_done"), j * 10 + 1)
                    copy(view(AT, 0, [[S + P, 4], [1, P]]), SC[0][:].rearrange("p (c t) -> p c t", c=4), "lv_free")
                n = LEVEL_AT.get(p, -1) + 1
                if 1 <= n <= 7:
                    h = 1 << (n - 1)
                    act.wait_ge(sem("qk_ready"), j * 9 + n)
                    copy(view(KM, 0, [[2 * h, S // (2 * h)], [h, 2], [1, h]]),
                         view(KF, 0, [[2 * h, S // (2 * h)], [2 * S + h, 2], [1, h]]), "km_ready")
                if n == 9:
                    act.wait_ge(sem("lv_done"), j * 10 + 9)
                    act.wait_ge(sem("lv_free"), PRIMED + j * 10 + 8)
                    copy(view(AT, P, [[2 * S + 2 * P, 2], [S - P, 2], [1, P]]),
                         SC[0][:].rearrange("p (a b t) -> p a b t", a=2, b=2), "lv_free")
                if n == 10:
                    act.wait_ge(sem("lv_done"), j * 10 + 10)
                    copy(view(AT, 256, [[S, 2], [1, 256]]), TP[0][:].rearrange("p (a t) -> p a t", a=2))
                    copy(view(AT + 2, 0, [[S, 2], [1, 256]]), TP[1][:].rearrange("p (a t) -> p a t", a=2), "lv_free")
                if p == 13:
                    act.wait_ge(sem("hav_done"), PRIMED + j + 1)
                    act.activation(row(HSQ), OB[:], ACT.Square).then_inc(sem("hsq_ready"), 1)
                if p == 14:
                    act.wait_ge(sem("hg_done"), PRIMED + j)
                    inv_root(TP[1], row(HRO), P, (sem("hss_done"), j + 1), "hro_ready")

            def att_work(j, p):
                if p == 0:
                    act.wait_ge(sem("av_done"), PRIMED + j * 4)
                    act.wait_ge(sem("v_turned"), j + 1)
                    copy(row(VN), TP[0][:], "vn_ready")
                if p in ATT_SOFTMAX:
                    a = ATT_SOFTMAX[p]
                    for hd in range(2):
                        u = 2 * a + hd
                        act.wait_ge(sem("sm_done"), PRIMED + j * 8 + u + 1)
                        act.wait_ge(sem("pt_done"), PRIMED + j * 8 + max(u - 1, 0))
                        act.activation(row(PRB + hd), row(SMR + hd), ACT.Exp, bias=SM[:, hd:hd + 1], scale=-1.0,
                                       accum_out=SM[:, 2 + hd:3 + hd]).then_inc(sem("exp_done"), 1)
                if p in ATT_TURN:
                    a = ATT_TURN[p]
                    act.wait_ge(sem("pt_done"), PRIMED + j * 8 + 2 * a + 1)
                    act.wait_ge(sem("av_done"), PRIMED + j * 4 + a)
                    copy(row(PT), TP[0][:], "pte0")

            def ret_work(j, p, load=None, b=None, cl=None):
                if p == 9:
                    if cl is not None:
                        act.wait_ge(sem("cl_ready"), cl)
                    for g in range(2):
                        act.wait_ge(sem("gate_done"), j * 2 + g + 1)
                        act.wait_ge(sem("scan_done"), PRIMED + j)
                        act.activation(row(LR + g), SC[g][:], ACT.Exp, bias=SM[:, 32 + 6 * g + b:33 + 6 * g + b],
                                       scale=-1.0).then_inc(sem("gate_read"), 1)
                if p == 10:
                    act.wait_ge(sem("r_ready"), j + 1)
                    act.activation(row(LA), row(LR), ACT.Exp, scale=SM[:, 44 + b:45 + b]).then_inc(sem("a_ready"), 1)
                    act.activation(MIX[:, 10 + b, :], row(LR), ACT.Exp, scale=SM[:, 50 + b:51 + b]).then_inc(sem("a_ready"), 1)
                if p == 13:
                    act.wait_ge(sem("m2_ready"), j + 1)
                    act.activation(MIX[:, 10 + b, :], MIX[:, 10 + b, :], ACT.Ln)
                    act.drain()
                    act.activation(MIX[:, 10 + b, :], MIX[:, 10 + b, :], ACT.Exp, scale=0.5).then_inc(sem("mult_ready"), 1)
                if p == 0:
                    act.wait_ge(sem("rav_done"), PRIMED + j)
                    act.wait_ge(sem("rv_turned"), j + 1)
                    copy(row(VN), TP[0][:], "rvn_ready")
                if p == 5 and load is not None:
                    act.wait_ge(sem("ra_ready"), PRIMED + j * 4 + 4)
                    act.dma_start(row(DEC), dec[load]).then_inc(sem("dec_loaded"), 16)
                if p == 6:
                    act.wait_ge(sem("ret_done"), PRIMED + j)
                    act.wait_ge(sem("rav_done"), PRIMED + j + 1)
                    act.activation(row(NRO), OB[:], ACT.Square).then_inc(sem("rsq_ready"), 1)
                if p == 8:
                    inv_root(TP[1], row(NRO), P, (sem("rss_done"), j + 1), "rro_ready")

            def dif_work(j, p):
                if p == 0:
                    act.wait_ge(sem("dav_done"), PRIMED + j * 4)
                    act.wait_ge(sem("dv_turned"), j + 1)
                    copy(row(VN), TP[0][:], "dvn_ready")
                if p in DIF_SOFTMAX:
                    a = DIF_SOFTMAX[p]
                    w = (a + 1) * P
                    for hd in range(2):
                        u = 2 * a + hd
                        act.wait_ge(sem("dsm_done"), PRIMED + j * 8 + u + 1)
                        act.wait_ge(sem("dpt_done"), PRIMED + j * 4 + a)
                        act.activation(row(PRB + hd)[:, 0:w], row(SMR + hd)[:, 0:w], ACT.Exp, bias=SM[:, hd:hd + 1],
                                       scale=-1.0, accum_out=SM[:, 2 + hd:3 + hd]).then_inc(sem("dexp_done"), 1)
                if p in DIF_TURN:
                    a = DIF_TURN[p]
                    w = (a + 1) * P
                    act.wait_ge(sem("dpt_done"), PRIMED + j * 4 + a + 1)
                    act.wait_ge(sem("dav_done"), PRIMED + j * 4 + a)
                    copy(row(PT)[:, 0:w], TP[0][:, 0:w], "dpte")
                if p == 15:
                    act.wait_ge(sem("dif_done"), PRIMED + j)
                    act.wait_ge(sem("dav_done"), PRIMED + j * 4 + 4)
                    act.activation(row(NRO), OB[:], ACT.Square).then_inc(sem("dsq_ready"), 1)
                    inv_root(TP[1], row(NRO), P, (sem("dss_done"), j + 1), "dro_ready")

            WORK = {"hg": hg_work, "att": att_work, "ret": ret_work, "dif": dif_work}

            def step(t, gate=False, gates=False, hg=False, work=None, j=None, between={}, **kw):
                for p in range(16):
                    s, q = divmod(p, 4)
                    if t is not None:
                        high(t.plus(s), q)
                    if p in between:
                        between[p]()
                    if hg and p in (3, 7, 11):
                        gate_exp(t.plus(s), SG, SE, "sg_exp")
                    if work is not None:
                        WORK[work](j, p, **kw)
                    if (gate and p == 15) or (gates and q == 3):
                        gate_exp(t.plus(s))

            def operand(t, src, scale=None, new=None, late=None):
                act.wait_ge(sem("w_free"), t.times(4))
                for q, (a, b) in enumerate(((0, 8), (8, 12), (12, 14), (14, 16))):
                    if late is not None and a == 14:
                        act.wait_ge(*late)
                    with act.Fori(a, b) as m:
                        if new is not None:
                            act.wait_ge(sem("h_new"), m + 1 + new)
                        if scale is None:
                            act.activation(UH[:, m, :], src[:, m, :], ACT.Copy).then_inc(sem("uh_ready"), 1)
                        else:
                            act.activation(UH[:, m, :], src[:, m, :], ACT.Copy,
                                           scale=scale[:, bass.ds(m, 1)]).then_inc(sem("uh_ready"), 1)
                    high(t, q)

            def squares(t, n):
                for m in range(KT):
                    act.wait_ge(sem("sq_used"), PRIMED + n + max(m - 1, 0))
                    act.activation(row(SQ0 + m % 2), row(H + m), ACT.Square).then_inc(sem("sq_ready"), 1)
                    if m % 4 == 3:
                        high(t, m // 4)

            def out_slots(t, n, gain, ss, root, loads=()):
                def one(tt, m, s, used, first=False):
                    for q in range(4):
                        if not first:
                            high(tt, q)
                    act.wait_ge(sem("w_free"), tt.times(4, 4))
                    act.wait_ge(sem("sq_used"), PRIMED + used)
                    act.activation(row(SQ0 + s), Z[s][:], ACT.Square).then_inc(sem("sq_ready"), 1)
                    copy(MIX[:, m, :], Z[s][:], "z_free", scale=gain[:, bass.ds(m, 1)])

                for s in range(2):
                    one(t.plus(s), s, s, n, s == 0)
                    if loads:
                        loads[s]()
                with act.Fori(1, KT // 2) as i:
                    for s in range(2):
                        one(Tile(t.c + s, *t.terms, (2, i)), i * 2 + s, s, i * 2 + n + s - 1)
                inv_root(OB, row(ACC), D, (sem("ss_done"), ss), root)

            def load_h(src, done):
                for g in range(4):
                    act.dma_start(W[:, H + 4 * g:H + 4 * g + 4, :], src[4 * g:4 * g + 4].rearrange("m p t -> p m t")
                                  ).then_inc(sem(done), 16)

            act.dma_start(MIX[:, 14:16, :], pT.rearrange("k p t -> p k t")).then_inc(sem("p_loaded"), 16)
            act.dma_start(PR1[:], par1).then_inc(sem("cs_loaded"), 16)
            act.dma_start(CS[:], cst).then_inc(sem("cs_loaded"), 16)
            for g in range(4):
                act.dma_start(W[:, H + 4 * g:H + 4 * g + 4, :], xT[4 * g:4 * g + 4].rearrange("m p t -> p m t")
                              ).then_inc(sem(f"x{g}_loaded"), 16)
            act.preload_act_table_set("natural_log_exp_and_others")
            act.wait_ge(sem("p_loaded"), 16)
            for k in range(2):
                copy(PH[:, k, :], MIX[:, 14 + k, :], "ph_ready")
            for q in range(4):
                act.wait_ge(sem("w_raw0"), 16)
                act.activation(WH[:, 4 * q:4 * q + 4, :], RAW[:, 0, 512 * q:512 * q + 512].rearrange("p (k c) -> p k c", k=4),
                               ACT.Copy).then_inc(sem("h_ready"), 1)
            act.dma_start(MIX[:, 8, :].bitcast(I32), pos1.to_broadcast([P, S])).then_inc(sem("pos_loaded"), 16)
            act.dma_start(MIX[:, 9, :].bitcast(I32), pos2.to_broadcast([P, S])).then_inc(sem("pos_loaded"), 16)
            act.dma_start(IDN[:], idn).then_inc(sem("consts"), 16)
            act.dma_start(MIX[:, 6:8, :].rearrange("p a b -> p (a b)"), masks.rearrange("p n t -> p (n t)")
                          ).then_inc(sem("masks_loaded"), 16)
            act.wait_ge(sem("cs_loaded"), 32)
            for m in range(KT):
                if m % 2 == 0:
                    act.wait_ge(sem("e_even"), m // 2 + 1)
                else:
                    act.wait_ge(sem("w_free"), m // 2 + 1)
                copy(row(E + m), Z[m % 2][:], "e_out")
                if m % 2:
                    high(Tile(m // 8), (m // 2) % 4)
                act.wait_ge(sem(f"x{m // 4}_loaded"), 16)
                copy(UH[:, m, :], row(H + m), "uh_ready", scale=PR1[:, G_PRE + m:G_PRE + m + 1])
            act.wait_ge(sem("e_out"), 16)
            act.dma_start(e_dram.rearrange("m p t -> p m t"), W[:, E:E + 16, :]).then_inc(sem("e_stored"), 16)
            act.wait_ge(sem("lb_diff"), 1)
            act.activation(SM[:, 16:32], SM[:, 0:16], ACT.Exp).then_inc(sem("lb_exp"), 1)
            for q in range(4):
                high(Tile(T_HGG), q)
            squares(Tile(T_HGG + 1), 0)
            for q in range(4):
                high(Tile(T_HGG + 2), q)
            inv_root(OB, row(RSTD), D, (sem("ss_done"), 1), "rstd_ready")

            def gate_exps(*tiles):
                for m in tiles:
                    gate_exp(Tile(T_HGG + m))

            def next_weights(m):
                for q in range(4):
                    high(Tile(T_HGG + m), q)

            def sines(n):
                act.wait_ge(sem("angle_ready"), n * 2)
                for r in (COS, SIN):
                    act.activation(row(r), row(r), ACT.Sin).then_inc(sem("table_ready"), 1)
                act.preload_act_table_set("natural_log_exp_and_others")
                act.wait_ge(sem("table_ready"), n * 2)
                act.dma_start(tabs[n * 2 - 2:n * 2].rearrange("n p t -> p n t"), row(COS, 2)).then_inc(sem("tables_out"), 16)

            gate_exps(0)
            next_weights(3)
            gate_exps(1, 2)
            next_weights(4)
            gate_exps(3, 4)
            next_weights(5)
            gate_exps(5)
            next_weights(6)
            sines(1)
            gate_exps(6)
            next_weights(7)
            gate_exps(7)
            step(Tile(T_HG), hg=True, between={7: lambda: sines(2), 11: lambda: sines(3)})
            act.wait_ge(sem("tables_out"), 64)
            act.dma_start(row(CT1), tabs[0]).then_inc(sem("tab1_loaded"), 16)
            act.dma_start(row(ST1), tabs[1]).then_inc(sem("tab1_loaded"), 16)
            act.dma_start(W[:, BIAS:BIAS + 4, :], bias).then_inc(sem("tab1_loaded"), 16)
            with act.Fori(1, HG_HEADS) as i:
                step(Tile(T_HG, (4, i)), hg=True, work="hg", j=i - 1)
            step(Tile(T_ATT), gate=True, work="hg", j=HG_HEADS - 1)
            act.wait_ge(sem("hg_done"), PRIMED + HG_HEADS)
            with act.Fori(1, PAIRS) as i:
                step(Tile(T_ATT, (4, i)), gate=True, work="att", j=i - 1)

            def finished_tile(p):
                if p == 0:
                    act.wait_ge(sem("w_free"), 4 * T_OUT)
                    act.wait_ge(sem("att_done"), PRIMED + PAIRS - 1)
                copy(UH[:, p, :], MIX[:, p, :], "uh_ready")
                if p in (11, 14):
                    high(Tile(T_OUT), (p - 11) // 3)

            step(None, work="att", j=PAIRS - 1, between={p: lambda p=p: finished_tile(p) for p in range(15)})
            act.wait_ge(sem("att_done"), PRIMED + PAIRS)
            copy(UH[:, 15, :], MIX[:, 15, :], "uh_ready")
            for q in (2, 3):
                high(Tile(T_OUT), q)
            out_slots(Tile(T_OUT), 16, PR1[:, G_POST:G_POST + 16], 2, "root_ready", (
                lambda: load_h(xT, "h_loaded"),
                lambda: act.dma_start(W[:, E:E + 16, :], e_dram.rearrange("m p t -> p m t")).then_inc(sem("e_loaded"), 16)))
            operand(Tile(T_PG), W[:, H:H + 16, :], new=0)

            def pg_slot(t, m, s, cnt):
                for q in range(4):
                    if t.terms or t.c != T_PG:
                        high(t, q)
                act.wait_ge(sem("sq_used"), PRIMED + cnt)
                act.wait_ge(sem("w_free"), t.times(4, 4))
                act.activation(row(SQ0 + s), Z[s][:], ACT.Exp, scale=-1.0).then_inc(sem("z_free"), 1)

            def pg_square(m, s, cnt):
                act.wait_ge(sem("pg_prod"), cnt)
                act.activation(row(SQ0 + s), MIX[:, m, :], ACT.Square).then_inc(sem("sq_ready"), 1)
                act.drain()
                copy(MIX[:, m, :], MIX[:, m, :], scale=PR1[:, G_PLE:G_PLE + 16][:, bass.ds(m, 1)])

            for s in range(2):
                pg_slot(Tile(T_PG + s), s, s, 32)
                pg_square(s, s, s + 1)
            with act.Fori(1, KT // 2) as i:
                for s in range(2):
                    pg_slot(Tile(T_PG + s, (2, i)), i * 2 + s, s, i * 2 + 32 + s - 1)
                    pg_square(i * 2 + s, s, i * 2 + s + 1)
            inv_root(OB, row(ACC), D, (sem("ss_done"), 3), "root_ready")

            with act.Fori(0, LAYERS) as l:
                act.wait_ge(sem("par_used"), PRIMED + l)
                act.dma_start(PR2[:], par2[l]).then_inc(sem("par_loaded"), 16)
                act.dma_start(DL[:].rearrange("p a b -> p (a b)"), dlam[l].to_broadcast([P, 256])).then_inc(sem("par_loaded"), 16)
                act.wait_ge(sem("par_loaded"), l * 32 + 32)
                operand(Tile(T_L2, (PER_LAYER, l)), W[:, H:H + 16, :], PR2[:, G2_PRE:G2_PRE + 16], l * 16 + 16)
                act.wait_ge(sem("h_new"), l * 16 + 32)
                for g in range(4):
                    act.dma_start(out[4 * g:4 * g + 4].rearrange("m p t -> p m t"), W[:, H + 4 * g:H + 4 * g + 4, :]
                                  ).then_inc(sem("h_stored"), 16)
                squares(Tile(T_L2 + 1, (PER_LAYER, l)), l * 32 + 48)
                act.dma_start(row(CTR), tabs[2]).then_inc(sem("tab2_loaded"), 16)
                act.dma_start(row(STR), tabs[3]).then_inc(sem("tab2_loaded"), 16)
                act.dma_start(row(CTD), tabs[4]).then_inc(sem("tab2_loaded"), 16)
                for n in range(2):
                    act.wait_ge(sem("lam_dot"), l + 1)
                    act.activation(SM[:, 10 + n:11 + n], SM[:, 8 + n:9 + n], ACT.Exp).then_inc(sem("lam_exp"), 1)
                act.wait_ge(sem("lam_abs"), l + 1)
                act.activation(SM[:, 18:24], SM[:, 12:18], ACT.Exp, scale=-1.0).then_inc(sem("lam_e"), 1)

                for m in range(2, LRU_TILES):
                    for q in range(4):
                        high(Tile(T_L2 + R_LX + m, (PER_LAYER, l)), q)
                    if m == 2:
                        inv_root(OB, row(RSTD), D, (sem("ss_done"), l * 2 + 4), "rstd_ready")
                act.wait_ge(sem("h_stored"), l * 64 + 64)
                act.dma_start(row(STD), tabs[5]).then_inc(sem("tab3_loaded"), 16)
                act.dma_start(row(CM), cmask).then_inc(sem("tab3_loaded"), 16)
                act.dma_start(row(DEC), dec[0]).then_inc(sem("dec_loaded"), 16)
                act.dma_start(W[:, GW:GW + 7, :], gw[l].rearrange("p (r t) -> p r t", r=7)).then_inc(sem("gw_loaded"), 16)
                step(Tile(T_L2 + R_RET, (PER_LAYER, l)), gate=True)
                for h in range(1, RET_HEADS + 1):
                    step(Tile(T_L2 + R_RET + 4 * h, (PER_LAYER, l)), gate=True, work="ret", j=l * RET_HEADS + h - 1,
                         load=h if h < RET_HEADS else None, b=h - 1, cl=l + 1 if h == 1 else None)
                act.wait_ge(sem("ret_done"), PRIMED + l * RET_HEADS + RET_HEADS)
                act.wait_ge(sem("scan_done"), PRIMED + l * LRU_TILES + LRU_TILES)
                with act.Fori(1, DIF_HEADS) as i:
                    step(Tile(T_L2 + R_DIF, (PER_LAYER, l), (4, i)), gate=True, work="dif",
                         j=l * DIF_HEADS + i - 1)
                step(Tile(T_L2 + R_LG, (PER_LAYER, l)), gates=True, work="dif", j=l * DIF_HEADS + DIF_HEADS - 1)
                for m in range(4, LRU_TILES):
                    t = Tile(T_L2 + R_LG + m, (PER_LAYER, l))
                    for q in range(4):
                        high(t, q)
                    gate_exp(t)
                    if m == 4:
                        act.wait_ge(sem("dif_done"), PRIMED + l * DIF_HEADS + DIF_HEADS)
                        act.wait_ge(sem("h_stored"), l * 64 + 64)
                        load_h(out, "h_loaded")
                act.wait_ge(sem("lru_done"), l * 6 + 5)
                operand(Tile(T_L2 + R_OUT, (PER_LAYER, l)), MIX[:], late=(sem("lru_done"), act.to_reg(l * 6 + 6)))
                out_slots(Tile(T_L2 + R_OUT, (PER_LAYER, l)), l * 32 + 64, PR2[:, G2_POST:G2_POST + 16], l * 2 + 5, "root_ready")
            n = LAYERS * 16 + 16
            for name, count, a, b in (("h_new", n + 4, 0, 4), ("h_new", n + 8, 4, 8), ("h_new", n + POOL_LAST, 8, POOL_LAST),
                                      ("h_last", KT - POOL_LAST, POOL_LAST, KT)):
                act.wait_ge(sem(name), count)
                act.dma_start(out[a:b].rearrange("m p t -> p m t"), W[:, H + a:H + b, :]).then_inc(sem("h_stored"), 16)
            act.wait_ge(sem("h_stored"), LAYERS * 64 + 64)

        @block.vector
        def _(v):
            def wait_apart(name, value):
                value = value if isinstance(value, int) else v.to_reg(value)
                v.wait_ge(sem("ones_set"), 1)
                v.wait_ge(sem(name), value)

            def rstd_mul(t, dst, bank=None):
                v.drain()
                v.wait_ge(sem("w_free"), t.times(4, 4))
                v.tensor_tensor(dst, (Z[t.odd] if bank is None else bank)[:], row(RSTD), ALU.mult).then_inc(sem("z_free"), 1)

            def sigmoid_of(r):
                v.tensor_scalar(row(r), row(r), 1.0, None, ALU.add)
                v.drain()
                v.reciprocal(row(r), row(r))
                v.drain()

            def gate_tile(t, n, dst, bank=None):
                rstd_mul(t, row(RW), bank)
                v.wait_ge(sem("gexp"), n + 1)
                sigmoid_of(TM)
                v.tensor_tensor(dst, row(RW), row(TM), ALU.mult)
                v.drain()

            def rotated(t, dst, cos, sin, half, scale):
                z = Z[t.odd]
                v.drain()
                v.wait_ge(sem("w_free"), t.times(4, 4))
                v.scalar_tensor_tensor(out=row(dst), in0=z[:], scalar=scale, in1=row(cos), op0=ALU.mult, op1=ALU.mult)
                for o in range(0, P, half):
                    first = (o // half) % 2 == 0
                    x = o + half if first else o - half
                    i = v.scalar_tensor_tensor(out=row(TM)[o:o + half], in0=z[x:x + half, :], scalar=-scale if first else scale,
                                               in1=row(sin)[o:o + half], op0=ALU.mult, op1=ALU.mult)
                i.then_inc(sem("z_free"), 1)
                v.drain()
                v.tensor_tensor(row(dst), row(dst), row(TM), ALU.add)

            def take_heads(done):
                v.drain()
                v.tensor_copy(row(QT), row(QN))
                v.tensor_copy(row(KTR), row(KN)).then_inc(sem(done), 1)

            def hg_prepare(j):
                v.drain()
                if j is not None:
                    v.wait_ge(sem("lv_done"), j * 10 + 10)
                v.tensor_scalar(row(KF), row(FF), -1.0, 1.0, ALU.mult, ALU.add)
                v.tensor_scalar(row(KB), row(FB), -1.0, 1.0, ALU.mult, ALU.add)
                v.tensor_tensor(view(QB, 0, [[2 * S, 2], [1, S]]), view(FB, 0, [[S, 2], [1, S]]),
                                view(Q, 0, [[0, 2], [1, S]]), ALU.mult)
                v.tensor_tensor(view(TT, 0, [[S, 2], [1, 256]]), view(FB, 0, [[S, 2], [2, 256]]),
                                view(FB, 1, [[S, 2], [2, 256]]), ALU.mult)
                v.drain()
                v.tensor_tensor(row(KS), row(KF), row(KB), ALU.add).then_inc(sem("qk_ready"), 1)

            def hg_work(j, p):
                n = LEVEL_AT.get(p, 0)
                if 1 <= n <= 8:
                    h = 1 << (n - 1)
                    nb = S // (2 * h)
                    v.wait_ge(sem("lv_done"), j * 10 + n + 1)
                    tr, to = (FB, 0) if n == 1 else (TT, [0, 256, 384, 448, 480, 496, 504, 508][n - 2])
                    x = view(QF, h, [[-(S + h), 2], [2 * h, nb], [1, h]])
                    y = view(tr + 1, to, [[1, 2], [2, nb], [0, h]])
                    v.tensor_tensor(x, x, y, ALU.mult)
                    x = view(QB, 0, [[3 * S + h, 2], [2 * h, nb], [1, h]])
                    y = view(tr, to + 1, [[-1, 2], [2, nb], [0, h]])
                    v.tensor_tensor(x, x, y, ALU.mult).then_inc(sem("qk_ready"), 1)
                    if 2 <= n <= 7:
                        to2 = [0, 256, 384, 448, 480, 496, 504, 508][n - 1]
                        v.tensor_tensor(view(TT, to2, [[S, 2], [1, nb]]), view(TT, to, [[S, 2], [2, nb]]),
                                        view(TT, to + 1, [[S, 2], [2, nb]]), ALU.mult)
                    if n <= 7:
                        if n == 1:
                            wait_apart("lv_free", PRIMED + j * 10 + 1)
                        m = MSK[:, n, :]
                        mk = bass.AP(m.tensor, m.offset, [m.ap[0], [0, 4], [1, P]])
                        v.copy_predicated(view(AT, 0, [[S + P, 4], [1, P]]), mk,
                                          SC[n % 2][:].rearrange("p (c t) -> p c t", c=4)).then_inc(sem("lv_free"), 1)
                        v.drain()
                    else:
                        v.drain()
                if p == 15:
                    v.wait_ge(sem("hro_ready"), PRIMED + j + 1)
                    v.tensor_tensor(row(HTMP), OB[:], row(HRO), ALU.mult)
                    v.drain()
                    dst = MIX[:, j, :]
                    v.scalar_tensor_tensor(out=dst, in0=row(HTMP), scalar=PR1[:, G_HG:G_HG + 1], in1=dst,
                                           op0=ALU.mult, op1=ALU.mult).then_inc(sem("hg_done"), 1)

            def att_work(j, p):
                if p in ATT_SCORES:
                    a = ATT_SCORES[p]
                    for hd in range(2):
                        u = 2 * a + hd
                        wait_apart("s_done", j * 8 + u + 1)
                        v.tensor_tensor_reduce(row(SMR + hd), SC[hd][:], row(BIAS + a), -1.0, 3.0e38, ALU.add, ALU.min,
                                               SM[:, hd:hd + 1]).then_inc(sem("sm_done"), 1)
                if p in ATT_SOFTMAX:
                    a = ATT_SOFTMAX[p]
                    v.wait_ge(sem("exp_done"), j * 8 + 2 * a + 2)
                    v.reciprocal(SM[:, 4:6], SM[:, 2:4])
                    v.drain()
                    for hd in range(2):
                        v.tensor_scalar(row(PRB + hd), row(PRB + hd), SM[:, 4 + hd:5 + hd], None,
                                        ALU.mult).then_inc(sem("p_ready"), 1)
                if p in ATT_TURN:
                    a = ATT_TURN[p]
                    v.wait_ge(sem("pt_done"), PRIMED + j * 8 + 2 * a + 2)
                    v.wait_ge(sem("av_done"), PRIMED + j * 4 + a)
                    v.tensor_copy(row(PT + 1), TP[1][:]).then_inc(sem("pte1"), 1)
                if p == 15:
                    v.wait_ge(sem("av_done"), PRIMED + j * 4 + 4)
                    v.tensor_tensor(MIX[:, j + 8, :], OB[:], MIX[:, j + 8, :], ALU.mult).then_inc(sem("att_done"), 1)

            def lru_work(j, p, b):
                I_, R_, TB, M2 = row(LI), row(LR), row(LTB), MIX[:, 10 + b, :]
                if p == 9:
                    v.wait_ge(sem("gate_read"), PRIMED + j * 2 + 2)
                    v.tensor_scalar(view(LR, 0, [[1, 2 * S]]), view(LR, 0, [[1, 2 * S]]), 1.0, None, ALU.add)
                    v.drain()
                    v.reciprocal(R_, R_).then_inc(sem("r_ready"), 1)
                    v.reciprocal(I_, I_)
                if p == 10:
                    v.tensor_tensor(I_, I_, row(XC + b), ALU.mult)
                    v.tensor_scalar(TB, R_, SM[:, 50 + b:51 + b], None, ALU.mult)
                if p == 11:
                    v.wait_ge(sem("a_ready"), j * 2 + 2)
                    v.tensor_scalar(R_, TB, -1.0 / 5040, None, ALU.mult)
                    for f in (720, 120, 24, 6, 2, 1):
                        v.drain()
                        v.scalar_tensor_tensor(out=R_, in0=R_, scalar=-1.0 / f, in1=TB, op0=ALU.add, op1=ALU.mult)
                if p == 12:
                    v.tensor_scalar(M2, M2, -1.0, 1.0, ALU.mult, ALU.add)
                    v.tensor_scalar(TB.bitcast(I32), TB, -0.25, None, ALU.is_gt)
                    v.drain()
                    v.copy_predicated(M2, TB.bitcast(I32), R_)
                    v.drain()
                    v.tensor_scalar(M2, M2, 1e-19, None, ALU.max).then_inc(sem("m2_ready"), 1)
                if p == 14:
                    v.wait_ge(sem("mult_ready"), j + 1)
                    v.tensor_tensor(I_, I_, M2, ALU.mult)
                    v.drain()
                    v.tensor_tensor_scan(M2, row(LA), I_, 0.0, ALU.mult, ALU.add).then_inc(sem("scan_done"), 1)

            def ret_work(j, p, m=None):
                lru_work(j, p, m)
                if 1 <= p <= 4:
                    c = p - 1
                    if c == 0:
                        v.wait_ge(sem("dec_loaded"), j * 16 + 16)
                    v.wait_ge(sem("rs_done"), j * 4 + c + 1)
                    v.tensor_tensor(view(0, RA[c], [[1, S - c * P]]), SC[c % 2][:, 0:S - c * P], row(DEC)[:, 0:S - c * P],
                                    ALU.mult).then_inc(sem("ra_ready"), 1)
                if p == 8:
                    v.wait_ge(sem("rro_ready"), j + 1)
                    v.tensor_tensor(row(NRO), OB[:], row(NRO), ALU.mult)
                    v.drain()
                    v.tensor_tensor(MIX[:, m, :], row(NRO), MIX[:, m, :], ALU.mult).then_inc(sem("ret_done"), 1)

            def dif_work(j, p, m=None):
                if p in DIF_SCORES:
                    a = DIF_SCORES[p]
                    w = (a + 1) * P
                    for hd in range(2):
                        wait_apart("ds_done", j * 8 + 2 * a + hd + 1)
                        v.tensor_tensor_reduce(row(SMR + hd)[:, 0:w], SC[hd][:, 0:w], row(CM)[:, S - w:S], -1.0, 3.0e38,
                                               ALU.add, ALU.min, SM[:, hd:hd + 1]).then_inc(sem("dsm_done"), 1)
                if p in DIF_SOFTMAX:
                    a = DIF_SOFTMAX[p]
                    w = (a + 1) * P
                    v.wait_ge(sem("dexp_done"), j * 8 + 2 * a + 2)
                    v.reciprocal(SM[:, 4:6], SM[:, 2:4])
                    v.drain()
                    v.tensor_tensor(SM[:, 6:7], SM[:, 5:6], SM[:, 60:61], ALU.mult)
                    v.tensor_scalar(row(PRB)[:, 0:w], row(PRB)[:, 0:w], SM[:, 4:5], None, ALU.mult)
                    v.drain()
                    v.scalar_tensor_tensor(out=row(PRB)[:, 0:w], in0=row(PRB + 1)[:, 0:w], scalar=SM[:, 6:7],
                                           in1=row(PRB)[:, 0:w], op0=ALU.mult, op1=ALU.add).then_inc(sem("dp_ready"), 1)
                if p == 15:
                    v.wait_ge(sem("dro_ready"), j + 1)
                    v.tensor_tensor(row(NRO), OB[:], row(NRO), ALU.mult)
                    v.drain()
                    v.scalar_tensor_tensor(out=MIX[:, m, :], in0=row(NRO), scalar=SM[:, 61:62], in1=MIX[:, m, :],
                                           op0=ALU.mult, op1=ALU.mult).then_inc(sem("dif_done"), 1)

            WORK = {"hg": hg_work, "att": att_work, "ret": ret_work, "dif": dif_work}

            def step(t, rot=None, scales=None, gate=None, hg=None, work=None, j=None, lru=None, take=None, between={}, **kw):
                for p in range(16):
                    s, q = divmod(p, 4)
                    if rot is not None:
                        if p in (3, 7):
                            rotated(t.plus(s), QN if p == 3 else KN, *rot, scales[s])
                        if p == 11:
                            rstd_mul(t.plus(2), row(VTA))
                    if hg is not None:
                        if p in (3, 7, 11):
                            rstd_mul(t.plus(s), row(SG))
                        if p == 15:
                            rstd_mul(t.plus(3), row(VT))
                    if lru is not None and q == 3:
                        lru_gate(t.plus(s), lru + s, s)
                    if work is not None:
                        v.drain()
                        WORK[work](j, p, **kw)
                    if p in between:
                        between[p]()
                    if hg is not None and p in (4, 8, 12):
                        v.wait_ge(sem("sg_exp"), hg * 3 + p // 4)
                        sigmoid_of(SE)
                        if p == 12:
                            v.tensor_tensor(row(Q), row(SG), row(SE), ALU.mult)
                        else:
                            d = 0 if p == 4 else 2
                            v.tensor_scalar(row(FF if p == 4 else FB), row(SE), LB[:, d + 1, :][:, hg_col(hg)],
                                            LB[:, d, :][:, hg_col(hg)], ALU.mult, ALU.add)
                    if hg is not None and p == 14:
                        hg_prepare(j if work == "hg" else None)
                    if take is not None and p == 13:
                        take_heads(take)
                    if gate is not None and p == 15:
                        gate_tile(t.plus(3), gate[0], MIX[:, gate[1], :])

            def hg_col(i):
                return bass.ds(i, 1)

            def lru_gate(t, n, b):
                gate_tile(t, n, row(RW))
                v.tensor_tensor(MIX[:, 10 + b, :], MIX[:, 10 + b, :], row(RW), ALU.mult).then_inc(sem("lru_done"), 1)

            def lru_conv(t, m):
                rstd_mul(t, row(QN), SPARE.get(m))
                v.drain()
                cw = lambda n: PR2[:, CONV_W + 4 * m + n:CONV_W + 4 * m + n + 1]
                v.tensor_scalar(row(XC + m), row(QN), cw(3), PR2[:, CONV_B + m:CONV_B + m + 1], ALU.mult, ALU.add)
                for n in range(1, 4):
                    v.drain()
                    i = v.scalar_tensor_tensor(out=row(XC + m)[:, n:S], in0=row(QN)[:, 0:S - n], scalar=cw(3 - n),
                                               in1=row(XC + m)[:, n:S], op0=ALU.mult, op1=ALU.add)
                i.then_inc(sem("xc_ready"), 1)

            def low_tile(m, n, src, scale):
                v.wait_ge(sem("uh_ready"), m + 1 + n)
                hi = UH[:, m, :].bitcast(F32)
                if scale is None:
                    v.tensor_tensor(UL[:, m, :], src[:, m, :], hi, ALU.subtract).then_inc(sem("u_ready"), 1)
                else:
                    v.scalar_tensor_tensor(out=UL[:, m, :], in0=src[:, m, :], scalar=scale[:, bass.ds(m, 1)], in1=hi,
                                           op0=ALU.mult, op1=ALU.subtract).then_inc(sem("u_ready"), 1)

            def low(n, src, scale=None, a=0, b=KT):
                with v.Fori(a, b) as m:
                    low_tile(m, n, src, scale)

            def sum_squares(n):
                def one(s, cnt, first=False):
                    v.wait_ge(sem("sq_ready"), cnt)
                    if first:
                        i = v.tensor_copy(row(ACC), row(SQ0))
                    else:
                        i = v.tensor_tensor(row(ACC), row(ACC), row(SQ0 + s), ALU.add)
                    i.then_inc(sem("sq_used"), 1)
                    v.drain()
                one(0, n + 1, True)
                one(1, n + 2)
                with v.Fori(1, KT // 2) as i:
                    for s in range(2):
                        one(s, i * 2 + n + s + 1)

            def scale_tile(m):
                v.tensor_tensor(MIX[:, m, :], MIX[:, m, :], row(ACC), ALU.mult).then_inc(sem("tile_scaled"), 1)

            def new_operand(root, n, scale=None):
                wait_apart("root_ready", root)
                for m in range(4):
                    scale_tile(m)
                with v.Fori(0, 6) as i:
                    for s in range(2):
                        scale_tile(i * 2 + (s + 4))
                    for s in range(2):
                        low_tile(i * 2 + s, n, W[:, H:H + 16, :], scale)
                for m in range(12, 16):
                    low_tile(m, n, W[:, H:H + 16, :], scale)

            def angles(n):
                posf, dst_c, dst_s = MIX[:, n + 9, :], row(COS), row(SIN)
                TWO_PI = 6.283185307179586
                c1 = 6.28125
                c2 = 0.0019350051879882812
                c3 = TWO_PI - c1 - c2
                MAGIC = 12582912.0
                ang, nn, rr, mm = (row(ANG + r) for r in range(4))
                PI = 3.1415925
                v.tensor_scalar(ang, posf, CS[:, C_INV + n - 1:C_INV + n], None, ALU.mult)
                v.drain()
                v.tensor_scalar(nn, ang, 1.0 / TWO_PI, MAGIC, ALU.mult, ALU.add)
                v.drain()
                v.tensor_scalar(nn, nn, -MAGIC, None, ALU.add)
                v.drain()
                v.scalar_tensor_tensor(out=rr, in0=nn, scalar=-c1, in1=ang, op0=ALU.mult, op1=ALU.add)
                v.drain()
                v.scalar_tensor_tensor(out=rr, in0=nn, scalar=-c2, in1=rr, op0=ALU.mult, op1=ALU.add)
                v.drain()
                v.scalar_tensor_tensor(out=rr, in0=nn, scalar=-c3, in1=rr, op0=ALU.mult, op1=ALU.add)
                v.drain()
                v.tensor_scalar(mm, rr, TWO_PI / 4, -TWO_PI, ALU.is_gt, ALU.mult)
                v.drain()
                v.scalar_tensor_tensor(out=mm, in0=rr, scalar=TWO_PI / 4, in1=mm, op0=ALU.add, op1=ALU.add)
                v.drain()
                v.wait_ge(sem("tables_out"), n * 16)
                v.tensor_scalar(dst_c, mm, PI, -PI, ALU.min, ALU.max).then_inc(sem("angle_ready"), 1)
                v.tensor_scalar(dst_s, rr, PI, -PI, ALU.min, ALU.max).then_inc(sem("angle_ready"), 1)
                v.drain()

            v.memset(ONES[:], 1.0).then_inc(sem("ones_set"), 1)
            for k in range(2):
                v.wait_ge(sem("ph_ready"), k + 1)
                v.tensor_tensor(PL[:, k, :], MIX[:, 14 + k, :], PH[:, k, :].bitcast(F32),
                                ALU.subtract).then_inc(sem("p_split"), 1)
            v.wait_ge(sem("cs_loaded"), 32)
            v.tensor_tensor(SM[:, 0:8], PR1[:, LBF + 8:LBF + 16], PR1[:, LBF:LBF + 8], ALU.subtract)
            v.tensor_tensor(SM[:, 8:16], PR1[:, LBB + 8:LBB + 16], PR1[:, LBB:LBB + 8], ALU.subtract).then_inc(sem("lb_diff"), 1)
            v.drain()
            low(0, W[:, H:H + 16, :], PR1[:, G_PRE:G_PRE + 16], 0, 12)
            v.wait_ge(sem("e_out"), 16)
            low(0, W[:, H:H + 16, :], PR1[:, G_PRE:G_PRE + 16], 12, 16)
            v.wait_ge(sem("masks_loaded"), 16)
            v.tensor_copy(MSK[:].rearrange("p n t -> p (n t)"), MIX[:, 6:8, :].rearrange("p a b -> p (a b)"))
            sum_squares(0)
            v.wait_ge(sem("lb_exp"), 1)
            v.tensor_scalar(SM[:, 16:32], SM[:, 16:32], 1.0, None, ALU.add)
            v.drain()
            v.reciprocal(LB[:, 0, :], SM[:, 16:24])
            v.reciprocal(LB[:, 2, :], SM[:, 24:32])
            v.drain()
            v.tensor_scalar(LB[:, 1, :], LB[:, 0, :], -1.0, 1.0, ALU.mult, ALU.add)
            v.tensor_scalar(LB[:, 3, :], LB[:, 2, :], -1.0, 1.0, ALU.mult, ALU.add)
            v.wait_ge(sem("pos_loaded"), 32)
            for n in range(3):
                v.tensor_copy(MIX[:, 10 + n, :], MIX[:, 8 + int(n > 0), :].bitcast(I32))
            v.wait_ge(sem("e_stored"), 16)
            v.wait_ge(sem("rstd_ready"), 1)
            for m in range(8):
                gate_tile(Tile(T_HGG + m), m, MIX[:, m, :], SPARE.get(m))
                if m == 5:
                    angles(1)
            step(Tile(T_HG), hg=0, between={5: lambda: angles(2), 9: lambda: angles(3)})
            v.wait_ge(sem("tables_out"), 64)
            v.drain()
            with v.Fori(1, HG_HEADS) as i:
                step(Tile(T_HG, (4, i)), hg=i, work="hg", j=i - 1)
                v.drain()
            v.wait_ge(sem("tab1_loaded"), 48)
            for r in (CT1, ST1):
                v.tensor_tensor(row(r), row(r), row(RSTD), ALU.mult)
            v.drain()
            tb = (CT1, ST1, 32)
            sc1 = (ATT_HD ** -0.5, 1.0)
            step(Tile(T_ATT), rot=tb, scales=sc1, take="qt_ready", gate=(8, 8), work="hg", j=HG_HEADS - 1)
            with v.Fori(1, PAIRS) as i:
                step(Tile(T_ATT, (4, i)), rot=tb, scales=sc1, take="qt_ready", gate=(i + 8, i + 8), work="att", j=i - 1)
            step(None, work="att", j=PAIRS - 1, between={p: lambda p=p: low_tile(p, 16, MIX[:], None) for p in range(15)})
            v.drain()
            low_tile(15, 16, MIX[:], None)
            sum_squares(16)
            new_operand(1, 32)
            v.wait_ge(sem("e_loaded"), 16)

            def pg_tile(m, s, cnt):
                v.wait_ge(sem("z_free"), cnt)
                sigmoid_of(SQ0 + s)
                v.drain()
                v.tensor_tensor(MIX[:, m, :], row(SQ0 + s), W[:, m + E, :] if not isinstance(m, int) else row(E + m),
                                ALU.mult).then_inc(sem("pg_prod"), 1)

            def pg_sum(s, cnt, first=False):
                v.wait_ge(sem("sq_ready"), cnt)
                if first:
                    i = v.tensor_copy(row(ACC), row(SQ0))
                else:
                    i = v.tensor_tensor(row(ACC), row(ACC), row(SQ0 + s), ALU.add)
                i.then_inc(sem("sq_used"), 1)
                v.drain()

            for s in range(2):
                pg_tile(s, s, T_PG + s - 1)
                pg_sum(s, 32 + s + 1, s == 0)
            with v.Fori(1, KT // 2) as i:
                for s in range(2):
                    pg_tile(i * 2 + s, s, i * 2 + (T_PG + s - 1))
                    pg_sum(s, i * 2 + 32 + s + 1)

            with v.Fori(0, LAYERS) as l:
                new_operand(l + 2, l * 32 + 48, PR2[:, G2_PRE:G2_PRE + 16])
                for n in range(2):
                    v.tensor_tensor(DL[:, 2 * n, :], DL[:, 2 * n, :], DL[:, 2 * n + 1, :], ALU.mult)
                v.drain()
                for n in range(2):
                    i = v.tensor_reduce(SM[:, 8 + n:9 + n], DL[:, 2 * n, :], AX.X, ALU.add)
                i.then_inc(sem("lam_dot"), 1)
                lam = PR2[:, LAM:LAM + 6]
                v.tensor_scalar(SM[:, 12:18], lam, -1.0, None, ALU.mult)
                v.tensor_scalar(SM[:, 24:30], lam, 0.0, None, ALU.min)
                v.tensor_scalar(SM[:, 32:44], PR2[:, BA:BA + 12], -1.0, None, ALU.mult)
                v.drain()
                v.tensor_tensor(SM[:, 12:18], SM[:, 12:18], lam, ALU.max).then_inc(sem("lam_abs"), 1)
                sum_squares(l * 32 + 48)
                v.wait_ge(sem("lam_exp"), l * 2 + 2)
                v.tensor_tensor(SM[:, 60:61], SM[:, 11:12], SM[:, 10:11], ALU.subtract)
                v.drain()
                v.tensor_tensor(SM[:, 60:61], SM[:, 60:61], CS[:, bass.ds(l * 2 + C_LAM, 1)], ALU.subtract)
                v.tensor_tensor(SM[:, 61:62], PR2[:, G2_SUB:G2_SUB + 1], CS[:, bass.ds(l * 2 + (C_LAM + 1), 1)], ALU.mult)
                v.wait_ge(sem("lam_e"), l + 1)
                e, w, w2, pl = SM[:, 18:24], SM[:, 44:50], SM[:, 50:56], SM[:, 12:18]
                v.tensor_scalar(w, e, 2.0, None, ALU.add)
                v.drain()
                v.reciprocal(w, w)
                v.drain()
                v.tensor_tensor(w, w, e, ALU.mult)
                v.drain()
                v.tensor_tensor(w2, w, w, ALU.mult)
                v.drain()
                v.tensor_scalar(pl, w2, 1.0 / 15, None, ALU.mult)
                for n in (13, 11, 9, 7, 5, 3):
                    v.drain()
                    v.scalar_tensor_tensor(out=pl, in0=pl, scalar=1.0 / n, in1=w2, op0=ALU.add, op1=ALU.mult)
                v.drain()
                v.scalar_tensor_tensor(out=pl, in0=pl, scalar=1.0, in1=w, op0=ALU.add, op1=ALU.mult)
                v.drain()
                v.scalar_tensor_tensor(out=pl, in0=pl, scalar=-2.0, in1=SM[:, 24:30], op0=ALU.mult, op1=ALU.add)
                v.drain()
                v.tensor_scalar(SM[:, 44:50], pl, 8.0, None, ALU.mult)
                v.tensor_scalar(SM[:, 50:56], pl, 16.0, None, ALU.mult).then_inc(sem("cl_ready"), 1)

                wait_apart("rstd_ready", l + 2)
                for m in range(LRU_TILES):
                    lru_conv(Tile(T_L2 + R_LX + m, (PER_LAYER, l)), m)
                v.wait_ge(sem("tab2_loaded"), l * 48 + 48)
                for r in (CTR, STR, CTD):
                    v.tensor_tensor(row(r), row(r), row(RSTD), ALU.mult)
                v.wait_ge(sem("tab3_loaded"), l * 32 + 32)
                v.tensor_tensor(row(STD), row(STD), row(RSTD), ALU.mult)
                v.drain()
                scr = (1.0, 128 ** -0.5)
                scd = (64 ** -0.5, 1.0)
                gl = l * 16 + 16
                step(Tile(T_L2 + R_RET, (PER_LAYER, l)), rot=(CTR, STR, 64), scales=scr, take="rqt_ready", gate=(gl, 0))
                for h in range(1, RET_HEADS):
                    step(Tile(T_L2 + R_RET + 4 * h, (PER_LAYER, l)), rot=(CTR, STR, 64), scales=scr,
                         take="rqt_ready", gate=(gl + h, h), work="ret", j=l * RET_HEADS + h - 1, m=h - 1)
                step(Tile(T_L2 + R_DIF, (PER_LAYER, l)), rot=(CTD, STD, 32), scales=scd, take="dqt_ready",
                     gate=(gl + 6, 6), work="ret", j=l * RET_HEADS + RET_HEADS - 1, m=5)
                with v.Fori(1, DIF_HEADS) as i:
                    step(Tile(T_L2 + R_DIF, (PER_LAYER, l), (4, i)), rot=(CTD, STD, 32), scales=scd,
                         take="dqt_ready", gate=(gl + i + 6, i + 6), work="dif", j=l * DIF_HEADS + i - 1, m=i + 5)
                step(Tile(T_L2 + R_LG, (PER_LAYER, l)), work="dif", j=l * DIF_HEADS + DIF_HEADS - 1, m=9, lru=gl + 10)
                lru_gate(Tile(T_L2 + R_LG + 4, (PER_LAYER, l)), gl + 14, 4)
                rstd_mul(Tile(T_L2 + R_LG + 5, (PER_LAYER, l)), row(RW))
                low(l * 32 + 64, MIX[:], b=8)
                v.drain()
                v.wait_ge(sem("gexp"), gl + 16)
                sigmoid_of(TM)
                v.tensor_tensor(row(RW), row(RW), row(TM), ALU.mult)
                v.drain()
                v.tensor_tensor(MIX[:, 15, :], MIX[:, 15, :], row(RW), ALU.mult).then_inc(sem("lru_done"), 1)
                v.tensor_scalar(SM[:, 62:63], SM[:, 61:62], 1.0, None, ALU.mult).then_inc(sem("par_used"), 1)
                low(l * 32 + 64, MIX[:], a=8)
                sum_squares(l * 32 + 64)
                v.drain()
            wait_apart("root_ready", LAYERS + 2)
            with v.Fori(0, POOL_LAST) as m:
                scale_tile(m)
            with v.Fori(POOL_LAST, KT) as m:
                v.tensor_tensor(MIX[:, m, :], MIX[:, m, :], row(ACC), ALU.mult)
            v.drain()
            v.wait_ge(sem("h_loaded"), LAYERS * 64 + 64)
            with v.Fori(POOL_LAST, KT) as m:
                v.tensor_tensor(W[:, m, :], W[:, m, :], MIX[:, m, :], ALU.add).then_inc(sem("h_last"), 1)



def tiles(w):
    r, c = w.shape
    return w.reshape(r // P, P, c // P, P).transpose(2, 1, 0, 3)


def cols(v):
    return v.reshape(-1, P).T


def constants():
    inv1 = np.power(np.float32(500000.0), -np.arange(0, 16, 2, dtype=np.float32) / np.float32(16))
    invr = (1.0 / (np.float32(10000.0) ** np.linspace(0, 1, 64, dtype=np.float32))).astype(np.float32)
    invd = (1.0 / (np.float32(10000.0) ** (np.arange(0, 64, 2, dtype=np.float32) / np.float32(64)))).astype(np.float32)
    cst = np.zeros((P, CST), np.float32)
    for p in range(P):
        if p % 32 < 8:
            cst[p, 0] = inv1[p % 32]
        cst[p, 1] = invr[p % 64]
        cst[p, 2] = invd[p % 32]
    cst[:, C_EPS] = EPS
    for l in range(LAYERS):
        li = 0.8 - 0.6 * np.exp(-0.3 * l)
        cst[:, C_LAM + 2 * l], cst[:, C_LAM + 2 * l + 1] = li, 1.0 - li
    a = np.arange(P)
    x = a[:, None] ^ a[None, :]
    masks = np.zeros((P, 8, P), np.float32)
    for n in range(1, 8):
        masks[:, n, :] = (x >= 1 << (n - 1)) & (x < 1 << n)
    t = np.arange(S)
    d = t[:, None] - t[None, :]
    count = np.zeros((S, S))
    for w, dil in ((128, 1), (512, 4), (2048, 16)):
        half = (w // 2) // dil
        count += (d % dil == 0) & (np.abs(d) // dil <= half)
    bias = np.where(count > 0, np.log(np.maximum(count, 1)), NEG).astype(np.float32)
    bias = np.ascontiguousarray(bias.reshape(4, P, S).transpose(1, 0, 2))
    dec = np.zeros((RET_HEADS, P, S), np.float32)
    dd = np.arange(S)[None, :] - np.arange(P)[:, None]
    for h in range(RET_HEADS):
        dec[h] = np.where(dd >= 0, np.exp(np.maximum(dd, 0) * np.log1p(-2.0 ** (-5.0 - h))), 0.0)
    cm = np.zeros((P, S), np.float32)
    cm[:, S - P:] = np.where(a[None, :] <= a[:, None], 0.0, NEG)
    return dict(cst=cst, idn=np.eye(P, dtype=np.float32), masks=masks, bias=bias, dec=dec, cmask=cm)


def layout(i):
    w1 = tiles(i["w_in"][0])
    head = np.r_[0:8, 16:40, 8:16, 40:64]
    w1 = np.concatenate([w1[:2 * PAIRS][..., np.r_[head, head + 64]], w1[2 * PAIRS:]])
    aq, ak, av, ag, hq, ff, fb, hv, hg = (range(8 * n, 8 * n + 8) for n in range(9))
    order1 = list(hg) + [x for j in range(8) for x in (ff[j], fb[j], hq[j], hv[j])] + \
        [x for j in range(8) for x in (aq[j], ak[j], av[j], ag[j])]
    pp = i["w_pp"][0].reshape(2, P, 2, 8, P).transpose(2, 1, 3, 0, 4).reshape(2, P, KT * P)
    parts = [pp, w1[order1], tiles(np.concatenate([i["w_out"][0][ATT_W:], i["w_out"][0][:ATT_W]])), tiles(i["w_pg"][0])]
    for l in range(LAYERS):
        w2 = tiles(i["w_in_2"][l])
        o2 = list(range(40, 46)) + [6 * n + j for j in range(6) for n in range(4)] + \
            [24 + 4 * n + j for j in range(4) for n in range(4)] + list(range(46, 52))
        parts += [w2[o2], tiles(i["w_out_2"][l])]
    parts.append(parts[0][0:1])
    wt = np.concatenate([x.reshape(-1, P, KT * P) for x in parts])
    par1 = np.concatenate([cols(i["g_pre"][0]), cols(i["g_post"][0]), cols(i["g_ple"][0]), cols(i["g_hg"][0])] +
                          [cols(i[n][r]) for n in ("lb_fwd", "lb_bwd") for r in range(2)], 1)
    par2, gws = [], []
    for l in range(LAYERS):
        cw = i["lru_conv_w_2"][l].reshape(4, LRU_TILES, P).transpose(2, 1, 0).reshape(P, 24)
        par2.append(np.concatenate([cols(i["pre_norm_g_2"][l]), cols(i["post_norm_g_2"][l]), cols(i["diff_subln_g_2"][l]), cw] +
                                   [cols(i[n][l]) for n in ("lru_conv_b_2", "lru_ba_2", "lru_bx_2", "lru_lambda_2")], 1))
        both = []
        for n in ("lru_wa_2", "lru_wx_2"):
            full = np.zeros((8 * LRU_BW, 8 * LRU_BW), np.float32)
            for b in range(8):
                full[b * LRU_BW:(b + 1) * LRU_BW, b * LRU_BW:(b + 1) * LRU_BW] = i[n][l, b]
            both += [full[P * x:P * x + P, P * y:P * y + P] for x, y in LRU_PAIRS]
        gws.append(np.stack(both, 1).reshape(P, 2 * NG * P))
    dl = np.stack([np.concatenate([i[f"diff_lambda_{n}_2"][l] for n in ("q1", "k1", "q2", "k2")]) for l in range(LAYERS)])
    return dict(wt=wt, xT=i["x"][0].T.reshape(KT, P, S), pT=i["p"][0, 0].T.reshape(2, P, S),
                pos1=i["positions"], pos2=i["positions_2"], par1=par1, par2=np.stack(par2), dlam=dl[:, None, :],
                gw=np.stack(gws))


ORDER = ["wt", "xT", "pT", "pos1", "pos2", "par1", "par2", "dlam", "gw", "cst", "idn", "masks", "bias", "dec", "cmask"]


def kernel(**inputs):
    import concourse.bacc as _bacc
    from concourse.bass_utils import run_bass_kernel_spmd as _run

    arrays = layout({n: np.asarray(a) for n, a in inputs.items()})
    arrays.update(constants())
    nc = _bacc.Bacc("TRN2", target_bir_lowering=False, num_devices=1)
    feed, args = {}, []
    for name in ORDER:
        a = np.ascontiguousarray(arrays[name])
        feed[f"in_{name}"] = a
        args.append(nc.dram_tensor(f"in_{name}", a.shape, mybir.dt.from_np(a.dtype), kind="ExternalInput").ap())
    args.append(nc.dram_tensor("out_hT", (KT, P, S), F32, kind="ExternalOutput").ap())
    build(nc, *args)
    r = _run(nc, [feed], core_ids=[0])
    return np.ascontiguousarray(r.results[0]["out_hT"].reshape(D, S).T)[None]
```
